# Optimizing a Trainium2 kernel written in Bass

```python
import jax
import jax.numpy as jnp
from jax import lax
import numpy as np

D_MODEL = 1024
BATCH = 1
SEQ = 128
DEPTH = 2
DEC_BATCH = 1
DEC_SEQ = 128
PAST_LEN = 128

GRID_W = 64
N_EVEN = (DEPTH + 1) // 2
N_ODD = DEPTH // 2
H_A = 8
DK_A = 64
DV_A = 64
CHUNK = 16
H_B = 8
Q_RANK = 256
KV_RANK = 128
D_NOPE = 64
D_ROPE = 32
DV_B = 64
ROPE_BASE = 10000.0
Q_BLOCK = 128
H_C = 16
N_C = 64
W_LORA = 64
A_LORA = 64
G_LORA = 128
D_FF = 2816
N_EXPERTS = 8
TOP_K = 2
D_FF_EXPERT = 2816
EPS = 1e-6
GN_EPS = 64e-5
HGRN_SIZES = (H_A * DK_A, H_A * DK_A, H_A * DK_A, H_A * DV_A, H_A * DV_A)
MLA_SIZES = (Q_RANK, KV_RANK, D_ROPE)
P_EVEN = sum(HGRN_SIZES) + sum(MLA_SIZES)
MIX_EVEN = H_A * DV_A + H_B * DV_B

kernel_name = 'hybrid_hgrn2_mla_rwkv7_prefix_dit'

def rms_norm(x, g):
    xf = x.astype(jnp.float32)
    y = xf * lax.rsqrt(jnp.mean(xf * xf, axis=-1, keepdims=True) + EPS)
    return (y * g.astype(jnp.float32)).astype(x.dtype)

def modulation(cond, w, b):
    mod = jax.nn.silu(cond) @ w + b
    return [m[:, None, :] for m in jnp.split(mod, 6, axis=-1)]

def axial_rope(rows):
    row, col = jnp.meshgrid(jnp.arange(rows), jnp.arange(GRID_W), indexing='ij')
    row = row.reshape(-1).astype(jnp.float32)
    col = col.reshape(-1).astype(jnp.float32)
    n_freq = D_ROPE // 4
    inv = 1.0 / (ROPE_BASE ** (jnp.arange(n_freq, dtype=jnp.float32) / n_freq))
    ar = row[:, None] * inv
    ac = col[:, None] * inv
    ang = jnp.concatenate([ar, ar, ac, ac], axis=-1)
    return jnp.cos(ang), jnp.sin(ang)

def rotate_axial(x):
    xb = x.reshape(x.shape[:-1] + (2, 2, D_ROPE // 4))
    rot = jnp.concatenate([-xb[..., 1:, :], xb[..., :1, :]], axis=-2)
    return rot.reshape(x.shape)

def apply_rope(x, cos, sin):
    return x * cos.astype(x.dtype) + rotate_axial(x) * sin.astype(x.dtype)

def blocked_attention(q, k, v, scale):
    bsz, t_len, n_h, d_q = q.shape
    nb = t_len // Q_BLOCK
    qb = jnp.moveaxis(q.reshape(bsz, nb, Q_BLOCK, n_h, d_q), 1, 0)

    def one_block(qi):
        s = jnp.einsum('bqhd,bkhd->bhqk', qi, k).astype(jnp.float32) * scale
        p = jax.nn.softmax(s, axis=-1).astype(v.dtype)
        return jnp.einsum('bhqk,bkhd->bqhd', p, v)

    o = lax.map(one_block, qb)
    return jnp.moveaxis(o, 0, 1).reshape(bsz, t_len, n_h, v.shape[-1])

def gla_chunkwise(q, k, v, logf, s0):
    bsz, t_len, n_h, _ = q.shape
    dv = v.shape[-1]
    nc = t_len // CHUNK

    def blk(t):
        return jnp.transpose(t.astype(jnp.float32).reshape(bsz, nc, CHUNK, n_h, t.shape[-1]), (0, 3, 1, 2, 4))

    q, k, v, logf = blk(q), blk(k), blk(v), blk(logf)
    bcum = jnp.cumsum(logf, axis=3)
    causal = jnp.tril(jnp.ones((CHUNK, CHUNK), dtype=bool))
    diff = bcum[:, :, :, :, None, :] - bcum[:, :, :, None, :, :]
    decay = jnp.exp(jnp.where(causal[:, :, None], diff, -jnp.inf))
    attn = jnp.einsum('bhnid,bhnjd,bhnijd->bhnij', q, k, decay)
    o_intra = jnp.einsum('bhnij,bhnjv->bhniv', attn, v)
    blast = bcum[:, :, :, -1, :]
    k_dec = k * jnp.exp(blast[:, :, :, None, :] - bcum)
    upd = jnp.einsum('bhnjd,bhnjv->bhndv', k_dec, v)

    def step(s, inp):
        d, u = inp
        return d[..., None] * s + u, s

    s_fin, s_prev = lax.scan(step, s0.astype(jnp.float32),
                             (jnp.moveaxis(jnp.exp(blast), 2, 0), jnp.moveaxis(upd, 2, 0)))
    s_prev = jnp.moveaxis(s_prev, 0, 2)
    o_inter = jnp.einsum('bhnid,bhndv->bhniv', q * jnp.exp(bcum), s_prev)
    o = jnp.transpose(o_intra + o_inter, (0, 2, 3, 1, 4)).reshape(bsz, t_len, n_h, dv)
    return o, s_fin

def hgrn_gates(logit, lb):
    logit = logit.astype(jnp.float32)
    logf = jnp.logaddexp(jnp.log(lb), jnp.log1p(-lb) + jax.nn.log_sigmoid(logit))
    key = (1.0 - lb) * jax.nn.sigmoid(-logit)
    return logf, key

def even_mixer(h, w_in, lb, hgrn_gain, q_gain, w_q_up, kv_gain, w_kv_up, w_out, s0_f, s0_b, ctx_ckv, ctx_krope, rope):
    bsz, t_len, _ = h.shape
    idx = np.cumsum(HGRN_SIZES + MLA_SIZES)[:-1].tolist()
    q_a, f_fw, f_bw, i_a, g_a, cq, ckv, krope = jnp.split(h @ w_in, idx, axis=-1)

    def heads(t):
        return t.reshape(bsz, t_len, H_A, -1)

    def flip(t):
        return jnp.flip(t, axis=1)

    logf_f, k_f = hgrn_gates(f_fw, lb[0])
    logf_b, k_b = hgrn_gates(f_bw, lb[1])
    qh, vh = heads(q_a), heads(i_a)
    o_f, sf_f = gla_chunkwise(qh, heads(k_f), vh, heads(logf_f), s0_f)
    o_b, sf_b = gla_chunkwise(flip(qh), flip(heads(k_b)), flip(vh), flip(heads(logf_b)), s0_b)
    o_a = rms_norm(o_f + flip(o_b), hgrn_gain).astype(h.dtype) * jax.nn.silu(heads(g_a))
    o_a = o_a.reshape(bsz, t_len, H_A * DV_A)

    q = (rms_norm(cq, q_gain) @ w_q_up).reshape(bsz, t_len, H_B, D_NOPE + D_ROPE)
    q_nope, q_rope = q[..., :D_NOPE], q[..., D_NOPE:]
    ckv = rms_norm(ckv, kv_gain)
    if rope is None:
        keys_ckv, keys_krope = ckv, krope
    else:
        cos, sin = rope
        q_rope = apply_rope(q_rope, cos[:, None, :], sin[:, None, :])
        keys_ckv = jnp.concatenate([ctx_ckv.astype(h.dtype), ckv], axis=1)
        keys_krope = jnp.concatenate([ctx_krope.astype(h.dtype), apply_rope(krope, cos, sin)], axis=1)
    n_keys = keys_ckv.shape[1]
    kv = (keys_ckv @ w_kv_up).reshape(bsz, n_keys, H_B, D_NOPE + DV_B)
    k_nope, v = kv[..., :D_NOPE], kv[..., D_NOPE:]
    k = jnp.concatenate([k_nope, jnp.broadcast_to(keys_krope[:, :, None, :], (bsz, n_keys, H_B, D_ROPE))], axis=-1)
    o_att = blocked_attention(jnp.concatenate([q_nope, q_rope], axis=-1), k, v, (D_NOPE + D_ROPE) ** -0.5)
    out = jnp.concatenate([o_a, o_att.reshape(bsz, t_len, H_B * DV_B)], axis=-1) @ w_out
    return out, (sf_f, sf_b, ckv, krope)

def centred_shift(x):
    prev = jnp.pad(x[:, :-1], ((0, 0), (1, 0), (0, 0)))
    nxt = jnp.pad(x[:, 1:], ((0, 0), (0, 1), (0, 0)))
    return 0.5 * (prev + nxt) - x

def rwkv7_scan(r, logw, k, v, kk, a, s0):
    def step(s, inp):
        r_t, lw_t, k_t, v_t, kk_t, a_t = inp
        sa = jnp.einsum('bhvk,bhk->bhv', s, -kk_t)
        s = (s * jnp.exp(lw_t)[:, :, None, :] + sa[..., None] * (kk_t * a_t)[:, :, None, :]
             + v_t[..., None] * k_t[:, :, None, :])
        return s, jnp.einsum('bhvk,bhk->bhv', s, r_t)

    xs = tuple(jnp.moveaxis(t, 1, 0) for t in (r, logw, k, v, kk, a))
    s_fin, y = lax.scan(step, s0.astype(jnp.float32), xs)
    return jnp.moveaxis(y, 0, 1), s_fin

def odd_mixer(h, mu, w_r, w_k, w_v, w_o, w0, w1, w2, a0, a1, a2, g1, g2, k_k, k_a, r_k, ln_w, ln_b, s0_f, s0_b):
    bsz, t_len, d = h.shape
    xx = centred_shift(h)
    xr, xw, xk, xv, xa, xg = [h + xx * mu[i] for i in range(6)]
    r = xr @ w_r
    k = xk @ w_k
    v = xv @ w_v
    a = jax.nn.sigmoid(a0 + (xa @ a1) @ a2)
    g = jax.nn.sigmoid(xg @ g1) @ g2

    def heads(t):
        return t.astype(jnp.float32).reshape(bsz, t_len, H_C, N_C)

    def log_decay(dr):
        wr = (w0[dr] + jnp.tanh(xw @ w1[dr]) @ w2[dr]).astype(jnp.float32)
        return heads(-jnp.exp(-jax.nn.softplus(-wr) - 0.5))

    def flip(t):
        return jnp.flip(t, axis=1)

    kk = heads(k * k_k)
    kk = kk * lax.rsqrt(jnp.sum(kk * kk, axis=-1, keepdims=True) + 1e-12)
    k = k * (1.0 + (a - 1.0) * k_a)
    rh, kh, vh, ah = heads(r), heads(k), heads(v), heads(a)
    y_f, sf_f = rwkv7_scan(rh, log_decay(0), kh, vh, kk, ah, s0_f)
    y_b, sf_b = rwkv7_scan(flip(rh), flip(log_decay(1)), flip(kh), flip(vh), flip(kk), flip(ah), s0_b)
    y = y_f + flip(y_b)
    mean = jnp.mean(y, axis=-1, keepdims=True)
    var = jnp.mean(jnp.square(y - mean), axis=-1, keepdims=True)
    y = ((y - mean) * lax.rsqrt(var + GN_EPS)).reshape(bsz, t_len, d) * ln_w + ln_b
    bonus = jnp.sum(rh * kh * r_k.reshape(H_C, N_C).astype(jnp.float32), axis=-1, keepdims=True) * vh
    y = (y + bonus.reshape(bsz, t_len, d)).astype(h.dtype)
    return (y * g) @ w_o, (sf_f, sf_b)

def swiglu(x, wg, wu, wd):
    return (jax.nn.silu(x @ wg) * (x @ wu)) @ wd

def moe_swiglu(x, w_router, wg, wu, wd):
    bsz, t_len, d = x.shape
    xt = x.reshape(-1, d)
    logits = (xt @ w_router).astype(jnp.float32)
    top_v, top_i = lax.top_k(logits, TOP_K)
    top_w = jax.nn.softmax(top_v, axis=-1)
    gate = jnp.sum(jax.nn.one_hot(top_i, N_EXPERTS, dtype=jnp.float32) * top_w[..., None], axis=1)
    out = jnp.zeros_like(xt)
    for e in range(N_EXPERTS):
        out = out + gate[:, e:e + 1].astype(x.dtype) * swiglu(xt, wg[e], wu[e], wd[e])
    return out.reshape(bsz, t_len, d)

def setup_inputs(seed: int = 0) -> dict:
    key = jax.random.key(seed)
    keys = jax.random.split(key, 64)
    counter = [0]

    def nxt():
        kk = keys[counter[0]]
        counter[0] += 1
        return kk

    def nrm(shape, scale):
        return scale * jax.random.normal(nxt(), shape, jnp.float32)

    def gain(shape):
        return 1.0 + nrm(shape, 0.05)

    D = D_MODEL
    return {
        'x_prompt': nrm((BATCH, SEQ, D), 1.0),
        'x_sample': nrm((DEC_BATCH, DEC_SEQ, D), 1.0),
        'cache_ckv': nrm((DEC_BATCH, N_EVEN, PAST_LEN, KV_RANK), 1.0),
        'cache_krope': nrm((DEC_BATCH, N_EVEN, PAST_LEN, D_ROPE), 1.0),
        'state_hgrn': nrm((DEC_BATCH, N_EVEN, 2, H_A, DK_A, DV_A), 0.5),
        'state_rwkv': nrm((DEC_BATCH, N_ODD, 2, H_C, N_C, N_C), 0.5),
        'c': nrm((DEC_BATCH, D), 1.0),
        'c_ctx': nrm((D,), 1.0),
        'ada_w': nrm((DEPTH, D, 6 * D), 0.5 * D ** -0.5),
        'ada_b': nrm((DEPTH, 6 * D), 0.02),
        'norm_gains': gain((DEPTH, 4, D)),
        'ev_w_in': nrm((N_EVEN, D, P_EVEN), D ** -0.5),
        'hgrn_lb_logits': nrm((N_EVEN, 2, H_A * DK_A), 0.5),
        'hgrn_norm': gain((N_EVEN, DV_A)),
        'mla_q_norm': gain((N_EVEN, Q_RANK)),
        'mla_w_q_up': nrm((N_EVEN, Q_RANK, H_B * (D_NOPE + D_ROPE)), Q_RANK ** -0.5),
        'mla_kv_norm': gain((N_EVEN, KV_RANK)),
        'mla_w_kv_up': nrm((N_EVEN, KV_RANK, H_B * (D_NOPE + DV_B)), KV_RANK ** -0.5),
        'ev_w_out': nrm((N_EVEN, MIX_EVEN, D), MIX_EVEN ** -0.5),
        'rw_mu': jax.random.uniform(nxt(), (N_ODD, 6, D), jnp.float32),
        'rw_w_r': nrm((N_ODD, D, D), D ** -0.5),
        'rw_w_k': nrm((N_ODD, D, D), D ** -0.5),
        'rw_w_v': nrm((N_ODD, D, D), D ** -0.5),
        'rw_w_o': nrm((N_ODD, D, D), D ** -0.5),
        'rw_w0': nrm((N_ODD, 2, D), 1.0) - 1.0,
        'rw_w1': nrm((N_ODD, 2, D, W_LORA), D ** -0.5),
        'rw_w2': nrm((N_ODD, 2, W_LORA, D), 0.5 * W_LORA ** -0.5),
        'rw_a0': nrm((N_ODD, D), 0.5),
        'rw_a1': nrm((N_ODD, D, A_LORA), D ** -0.5),
        'rw_a2': nrm((N_ODD, A_LORA, D), 0.5 * A_LORA ** -0.5),
        'rw_g1': nrm((N_ODD, D, G_LORA), D ** -0.5),
        'rw_g2': nrm((N_ODD, G_LORA, D), G_LORA ** -0.5),
        'rw_k_k': 0.85 + nrm((N_ODD, D), 0.05),
        'rw_k_a': gain((N_ODD, D)),
        'rw_r_k': nrm((N_ODD, D), 0.1),
        'rw_ln_w': gain((N_ODD, D)),
        'rw_ln_b': nrm((N_ODD, D), 0.02),
        'ffn_w_gate': nrm((N_EVEN, D, D_FF), D ** -0.5),
        'ffn_w_up': nrm((N_EVEN, D, D_FF), D ** -0.5),
        'ffn_w_down': nrm((N_EVEN, D_FF, D), D_FF ** -0.5),
        'moe_router': nrm((N_ODD, D, N_EXPERTS), D ** -0.5),
        'moe_w_gate': nrm((N_ODD, N_EXPERTS, D, D_FF_EXPERT), D ** -0.5),
        'moe_w_up': nrm((N_ODD, N_EXPERTS, D, D_FF_EXPERT), D ** -0.5),
        'moe_w_down': nrm((N_ODD, N_EXPERTS, D_FF_EXPERT, D), D_FF_EXPERT ** -0.5),
    }

def reference(x_prompt, x_sample, cache_ckv, cache_krope, state_hgrn, state_rwkv, c, c_ctx,
              ada_w, ada_b, norm_gains,
              ev_w_in, hgrn_lb_logits, hgrn_norm, mla_q_norm, mla_w_q_up, mla_kv_norm, mla_w_kv_up, ev_w_out,
              rw_mu, rw_w_r, rw_w_k, rw_w_v, rw_w_o, rw_w0, rw_w1, rw_w2, rw_a0, rw_a1, rw_a2, rw_g1, rw_g2,
              rw_k_k, rw_k_a, rw_r_k, rw_ln_w, rw_ln_b,
              ffn_w_gate, ffn_w_up, ffn_w_down, moe_router, moe_w_gate, moe_w_up, moe_w_down):
    lb_all = jnp.cumsum(jax.nn.softmax(hgrn_lb_logits.astype(jnp.float32), axis=0), axis=0)
    lb_all = lb_all - lb_all[:1]
    rows = x_sample.shape[1] // GRID_W
    rope = axial_rope(rows)
    cond_ctx = jnp.broadcast_to(c_ctx[None, :], (x_prompt.shape[0], D_MODEL))

    def layer(l, x, cond, latent):
        j = l // 2
        bsz = x.shape[0]
        sh_m, sc_m, gt_m, sh_f, sc_f, gt_f = modulation(cond, ada_w[l], ada_b[l])
        h = rms_norm(x, norm_gains[l, 0]) * (1.0 + sc_m) + sh_m
        if l % 2 == 0:
            if latent:
                s0_f, s0_b = state_hgrn[:, j, 0], state_hgrn[:, j, 1]
                ctx_ckv, ctx_krope, rp = cache_ckv[:, j], cache_krope[:, j], rope
            else:
                s0_f = jnp.zeros((bsz, H_A, DK_A, DV_A), jnp.float32)
                s0_b = s0_f
                ctx_ckv, ctx_krope, rp = None, None, None
            out, new = even_mixer(h, ev_w_in[j], lb_all[j], hgrn_norm[j], mla_q_norm[j], mla_w_q_up[j],
                                  mla_kv_norm[j], mla_w_kv_up[j], ev_w_out[j], s0_f, s0_b, ctx_ckv, ctx_krope, rp)
        else:
            if latent:
                s0_f, s0_b = state_rwkv[:, j, 0], state_rwkv[:, j, 1]
            else:
                s0_f = jnp.zeros((bsz, H_C, N_C, N_C), jnp.float32)
                s0_b = s0_f
            out, new = odd_mixer(h, rw_mu[j], rw_w_r[j], rw_w_k[j], rw_w_v[j], rw_w_o[j], rw_w0[j], rw_w1[j],
                                 rw_w2[j], rw_a0[j], rw_a1[j], rw_a2[j], rw_g1[j], rw_g2[j], rw_k_k[j], rw_k_a[j],
                                 rw_r_k[j], rw_ln_w[j], rw_ln_b[j], s0_f, s0_b)
        x = x + gt_m * rms_norm(out, norm_gains[l, 1])
        h = rms_norm(x, norm_gains[l, 2]) * (1.0 + sc_f) + sh_f
        if l % 2 == 0:
            ff = swiglu(h, ffn_w_gate[j], ffn_w_up[j], ffn_w_down[j])
        else:
            ff = moe_swiglu(h, moe_router[j], moe_w_gate[j], moe_w_up[j], moe_w_down[j])
        x = x + gt_f * rms_norm(ff, norm_gains[l, 3])
        return x, new

    y_prompt = x_prompt
    ckv_l, krope_l, hgrn_l, rwkv_l = [], [], [], []
    for l in range(DEPTH):
        y_prompt, new = layer(l, y_prompt, cond_ctx, False)
        if l % 2 == 0:
            hgrn_l.append(jnp.stack(new[:2], axis=1))
            ckv_l.append(new[2])
            krope_l.append(new[3])
        else:
            rwkv_l.append(jnp.stack(new, axis=1))
    dt = x_prompt.dtype
    new_ckv = jnp.stack(ckv_l, axis=1).astype(dt)
    new_krope = jnp.stack(krope_l, axis=1).astype(dt)
    new_hgrn = jnp.stack(hgrn_l, axis=1).astype(dt)
    new_rwkv = jnp.stack(rwkv_l, axis=1).astype(dt)

    y_sample = x_sample
    for l in range(DEPTH):
        y_sample, _ = layer(l, y_sample, c, True)

    return (y_prompt, y_sample, new_ckv, new_krope, new_hgrn, new_rwkv)


_drawn_inputs = setup_inputs


def setup_inputs(seed=0):
    import zlib

    import numpy as np

    out = dict(_drawn_inputs(seed))
    spreads = {}
    factors = {'state_hgrn': 3.411,
     'mla_q_norm': 22.475,
     'rw_ln_w': 21.465,
     'rw_ln_b': 60.934,
     'hgrn_norm': 3.633,
     'rw_r_k': 7.533}
    for name, (base, spread) in spreads.items():
        noise = np.random.default_rng([zlib.crc32(name.encode()), seed]).standard_normal(out[name].shape)
        drawn = base * np.exp(spread * noise) if base else spread * noise
        out[name] = jnp.asarray(drawn.astype(out[name].dtype))
    for name, factor in factors.items():
        out[name] = (out[name] * factor).astype(out[name].dtype)
    return out
```

```python
import math
from contextlib import ExitStack, contextmanager

import concourse.bass as bass
import numpy as np
from concourse import mybir

F32 = mybir.dt.float32
U8 = mybir.dt.uint8
ALU = mybir.AluOpType
ACT = mybir.ActivationFunctionType
AX = mybir.AxisListType

P = 128
D = 1024
KC = D // P
NST = 2
TW = 256
RING = 11
FT = 2816 // TW
NE = 8
HA, HC = 8, 16
DH = 64
EPS = 1e-6
GN_EPS = 64e-5
KAPPA = math.exp(-0.5)
SCALE = 96 ** -0.5
LEVELS = 7
GRID_W = 64

N_EVEN_OUT = 24 + 12 + 2
N_FFN = N_EVEN_OUT + 4
N_ADA1 = N_FFN + 3 * FT
N_ODD = N_ADA1 + 24
N_ODD_OUT = N_ODD + 12 + 5
N_MOE = N_ODD_OUT + 4 + 1


def up_used(j):
    return 2 if j == 0 else 3 * j + 1


def down_used(j):
    return 3 * j + 5 if j < FT - 1 else 3 * FT


ADAB, COND, GAIN, MU, W0, A0, KK, KA, RK, QN = 0, 96, 112, 176, 224, 240, 248, 256, 264, 272
NPV = 274
C_ID, C_TRI, C_BLK, C_COS, C_SIN, C_ONE = 0, 128, 640, 768, 800, 832
NCST = 833


def constants():
    c = np.zeros((P, NCST), np.float32)
    i = np.arange(P)
    row, col = i[:, None], i[None, :]
    c[:, C_ID:C_ID + P] = row == col
    c[:, C_ONE] = 1
    c[:, C_TRI:C_TRI + P] = row < col
    c[:, C_TRI + P:C_TRI + 2 * P] = row <= col
    c[:, C_TRI + 2 * P:C_TRI + 3 * P] = row > col
    c[:, C_TRI + 3 * P:C_TRI + 4 * P] = row >= col
    c[:, C_BLK:C_BLK + P] = row // DH == col // DH
    inv = (1.0 / (np.float32(10000.0) ** (np.arange(8, dtype=np.float32) / 8))).astype(np.float32)
    ar = (i // GRID_W).astype(np.float32)[:, None] * inv
    ac = (i % GRID_W).astype(np.float32)[:, None] * inv
    ang = np.concatenate([ar, ar, ac, ac], 1)
    sign = np.tile(np.repeat(np.array([-1.0, 1.0], np.float32), 8), 2)
    c[:, C_COS:C_COS + 32] = np.cos(ang)
    c[:, C_SIN:C_SIN + 32] = np.sin(ang) * sign
    m = np.zeros((P, 2 * LEVELS + 1, P), np.float32)
    for l in range(LEVELS):
        same = row >> (l + 1) == col >> (l + 1)
        m[:, 2 * l] = same & ((row >> l) % 2 == 0) & ((col >> l) % 2 == 1)
        m[:, 2 * l + 1] = same & ((row >> l) % 2 == 1) & ((col >> l) % 2 == 0)
    m[:, 2 * LEVELS] = row == col
    return c, m.reshape(P, -1)


def program(nc, t, out):
    ctx = ExitStack()
    with ctx:
        def sb(name, shape, dt=F32):
            return ctx.enter_context(nc.sbuf_tensor(name, shape, dt))

        sems = {}

        def sem(name):
            if name not in sems:
                sems[name] = ctx.enter_context(nc.semaphore(name))
            return sems[name]

        ring = sb("ring", [P, RING, KC * TW])
        X = sb("x", [P, NST, D])
        HT = sb("ht", [P, KC, NST * P])
        O = sb("o", [P, NST, D])
        GB = sb("gb", [P, NST, D])
        W = [sb(f"w{i}", [P, 2048]) for i in range(10)]
        CST = sb("cst", [P, NCST])
        MSK = sb("msk", [P, (2 * LEVELS + 1) * P], U8)
        PV = sb("pv", [P, NPV])
        MOD = sb("mod", [P, 6, KC, NST])
        AG = sb("ag", [P, 4, KC, NST])
        CT = sb("ct", [P, NST, KC])
        SM = sb("sm", [P, 200])
        bank = [ctx.enter_context(nc.psum_tensor(f"bank{i}", [P, 512], F32)) for i in range(8)]

        ident = CST[:, C_ID:C_ID + P]
        ones = CST[:, C_ONE:C_ONE + 1].to_broadcast([P, P])
        blk = CST[:, C_BLK:C_BLK + P]

        def mask(level, side):
            n = 2 * level + side
            return MSK[:, n * P:(n + 1) * P]

        Q = W[0][:, 0:1024].rearrange("p (c n) -> p c n", c=4)
        V0 = W[0][:, 1024:2048].rearrange("p (s n) -> p s n", s=NST)
        FL = W[1][:, :].rearrange("p (d c n) -> p d c n", d=2, c=4)
        LF = W[2]
        BC = W[3]
        KG = W[4]
        EX = W[5]
        WQ = W[6]
        AT = [W[7], W[8]]
        GA = W[9][:, 0:1024].rearrange("p (s n) -> p s n", s=NST)
        CQ = W[9][:, 1024:1536].rearrange("p (s n) -> p s n", s=NST)
        CKV = W[9][:, 1536:1856].rearrange("p (s n) -> p s n", s=NST)
        HG = W[9][:, 1856:1920]
        KVG = W[9][:, 1920:2048]
        KR = GB[:, 0, 0:288].rearrange("p (t n) -> p t n", t=3)
        CC = GB[:, 0, 288:416]
        CKN = GB[:, 0, 416:672].rearrange("p (s n) -> p s n", s=NST)
        S0A = GB[:, 1, :].rearrange("p (d c v) -> p d c v", d=2, c=4)
        CQT = W[3][:, 1024:1536].rearrange("p (c n) -> p c n", c=2)
        OA = W[1][:, 0:1024].rearrange("p (s n) -> p s n", s=NST)
        SG = W[1][:, 1024:2048].rearrange("p (s n) -> p s n", s=NST)
        OM = O
        KD = W[2][:, 0:1024].rearrange("p (d c n) -> p d c n", d=2, c=4)
        SH = W[2][:, 1024:2048].rearrange("p (d c n) -> p d c n", d=2, c=4)
        CKT = W[3][:, 0:384]
        TQ = W[3][:, 384:384 + 768]
        QT = W[4][:, 0:1536].rearrange("p (s n) -> p s n", s=NST)
        PR = W[5][:, :].rearrange("p (b h n) -> p b h n", b=4, h=2)
        PT = W[6][:, :].rearrange("p (b n) -> p b n", b=4)
        KT = [W[7], W[8]]
        VM = W[0][:, 0:1536].rearrange("p (t n) -> p t n", t=3)
        MT = W[2][:, :].rearrange("p (c n) -> p c n", c=KC)

        def kt(h):
            return KT[h // 4][:, (h % 4) * 384:(h % 4 + 1) * 384]

        def fm(b):
            return b[:, :].rearrange("p (c n) -> p c n", c=KC)

        R, K, NK, B = (fm(W[i]) for i in range(4))
        SGM = [fm(W[4]), fm(W[5])]
        V1 = W[6][:, :].rearrange("p (s n) -> p s n", s=NST)
        G1 = W[7][:, :].rearrange("p (s n) -> p s n", s=NST)
        XS = [fm(W[8]), fm(W[9])]
        XX = O[:, :, :].rearrange("p s (c n) -> p (s c) n", n=NST * P)
        Of = O[:, :, :].rearrange("p s n -> p (s n)")
        GBf = GB[:, :, :].rearrange("p s n -> p (s n)")
        HTf = HT[:, :, :].rearrange("p c n -> p (c n)")
        Y1 = W[0][:, :].rearrange("p (c s n) -> p c s n", c=KC, s=NST)
        M4 = [W[9][:, :], Of]
        M4 = [m.rearrange("p (j m n) -> p j m n", j=4, m=4) for m in M4]
        PX = [HTf, GBf]
        IP, IX, IZ = ([b[:, k * 512:(k + 1) * 512].rearrange("p (j n) -> p j n", j=4) for b in PX] for k in range(3))
        GS, US = ([b[:, 512 + k * 256:768 + k * 256].rearrange("p (j n) -> p j n", j=4) for b in PX] for k in range(2))
        NQ = W[8][:, 0:1024].rearrange("p (d s m n) -> p d s m n", d=2, s=2, m=2)
        BD = W[8][:, 1024:1536].rearrange("p (d s n) -> p d s n", d=2, s=2)
        KDC = W[8][:, 1536:2048].rearrange("p (d s n) -> p d s n", d=2, s=2)
        CS = W[7][:, 0:516].rearrange("p (a n) -> p a n", a=4)
        EE = W[7][:, 516:1032].rearrange("p (a n) -> p a n", a=4)
        E2 = W[7][:, 1032:1544].rearrange("p (a n) -> p a n", a=4)
        TRK = W[7][:, 1032:1544].rearrange("p (d m n) -> p d m n", d=2, m=2)
        VS = W[7][:, 1544:1800].rearrange("p (s n) -> p s n", s=NST)
        S0P = HTf[:, 1792:2048].rearrange("p (d v) -> p d v", d=2)
        S0S = HTf[0:DH, 1536:1792].rearrange("p (d n) -> p d n", d=2)
        SO = HTf[DH:P, 1536:1792].rearrange("p (d n) -> p d n", d=2)
        SF = GBf[:, 1536:1664].rearrange("p (d v) -> p d v", d=2)
        MG = GBf[:, 1664:1920]
        MW, MA = W[7][:, 0:256], W[7][:, 256:512]
        rows = [W[i][:, 1792:1920] for i in (7, 8, 6)]
        BON = SM[:, 160:192].rearrange("p (s h) -> p s h", s=NST)
        SIL = W[0][:, 0:1024].rearrange("p (b n) -> p b n", b=2)
        HID = W[0][:, 1024:2048].rearrange("p (b n) -> p b n", b=2)
        GT = sb("gt", [P, NST, NE])

        class Counts:

            def __init__(self):
                self.n, self.i, self.per, self.base = {}, None, {}, {}

            def made(self, name):
                self.n[name] = self.n.get(name, 0) + 1
                return sem(name)

            def so_far(self, name):
                if self.i is None:
                    return self.n.get(name, 0)
                return self.i * self.per[name] + (self.base.get(name, 0) + self.n.get(name, 0))

            @contextmanager
            def in_loop(self, i, n, per):
                self.base, self.n, self.per, self.i = self.n, {}, per, i
                yield
                got, self.n, self.i = self.n, dict(self.base), None
                assert got == per, got
                for name, k in got.items():
                    self.n[name] = self.base.get(name, 0) + n * k

        class Walk:
            def __init__(self):
                self.n, self.due = 0, [0] * RING

            def next(self, loads=1):
                s = self.n % RING
                self.n += 1
                self.due[s] += 16 * loads
                return s, self.due[s]

        kp = lambda ap: ap.rearrange("(k p) n -> p k n", p=P)

        block = ctx.enter_context(nc.Block())

        @block.sync
        def _(sp):
            walk = Walk()

            def tile(parts, i=None, per=0, dues=0):
                n = walk.n
                s, _ = walk.next(len(parts))
                if n >= RING or i is not None:
                    sp.wait_ge(sem("tile_used"), n - RING + 1 if i is None else i * per + (n - RING + 1))
                for dst, src in parts:
                    sp.dma_start(dst(ring[:, s, :]), src).then_inc(sem(f"slot{s}"), 16)

            def cols(w, a, n=TW):
                src = kp(w)[:, :, a if not isinstance(a, int) else slice(a, a + n)]
                return (lambda slot: slot[:, 0:KC * n].rearrange("p (k n) -> p k n", k=KC), src)

            def whole(a, n, src, parts=P):
                return (lambda slot: slot[0:parts, a:a + n], src)

            def ada(l):
                for n in range(24):
                    tile([cols(t["ada_w"][l], n * TW)])

            def down(w, j):
                src = w[j * TW:(j + 1) * TW, :].rearrange("(k p) n -> p k n", p=P)
                return (lambda slot: slot.rearrange("p (k n) -> p k n", k=2), src)

            def hidden(wg, wu, wd):
                for j in range(FT):
                    tile([cols(wg, j * TW)])
                    tile([cols(wu, j * TW)])
                    if j:
                        tile([down(wd, j - 1)])
                tile([down(wd, FT - 1)])

            ada(0)
            w = t["ev_w_in"][0]
            for n in range(11):
                tile([cols(w, n * TW)])
            tile([cols(w, 11 * TW, 160)])
            tile([(lambda s: s[:, 0:1536].rearrange("p (k n) -> p k n", k=2),
                   t["mla_w_q_up"][0].rearrange("(k p) n -> p k n", p=P))])
            tile([whole(0, 1024, t["mla_w_kv_up"][0])])
            for n in range(4):
                tile([cols(t["ev_w_out"][0], n * TW)])
            hidden(t["ffn_w_gate"][0], t["ffn_w_up"][0], t["ffn_w_down"][0])
            ada(1)
            for name in ("rw_w_r", "rw_w_k", "rw_w_v"):
                for n in range(4):
                    tile([cols(t[name][0], n * TW)])
            tile([(lambda s: s[:, 0:1024].rearrange("p (k n) -> p k n", k=KC)[:, :, 0:64], kp(t["rw_w1"][0, 0])),
                  (lambda s: s[:, 0:1024].rearrange("p (k n) -> p k n", k=KC)[:, :, 64:128], kp(t["rw_w1"][0, 1])),
                  (lambda s: s[:, 1024:1536].rearrange("p (k n) -> p k n", k=KC), kp(t["rw_a1"][0]))])
            tile([cols(t["rw_g1"][0], 0, 128)])
            tile([whole(0, 1024, t["rw_w2"][0].rearrange("d k n -> (d k) n"))])
            tile([whole(0, 1024, t["rw_a2"][0], 64)])
            tile([whole(0, 1024, t["rw_g2"][0])])
            for n in range(4):
                tile([cols(t["rw_w_o"][0], n * TW)])
            tile([(lambda s: s[:, 0:KC * NE].rearrange("p (k n) -> p k n", k=KC), kp(t["moe_router"][0]))])
            n0 = walk.n
            with sp.Fori(0, NE) as e:
                def expert(name):
                    return t[name][0][bass.ds(e, 1)].rearrange("a k n -> (a k) n")
                wg, wu, wd = expert("moe_w_gate"), expert("moe_w_up"), expert("moe_w_down")

                def etile(part):
                    tile([part], i=e, per=3 * FT)
                for j in range(FT):
                    etile(cols(wg, j * TW))
                    etile(cols(wu, j * TW))
                    if j:
                        etile(down(wd, j - 1))
                etile(down(wd, FT - 1))
            assert walk.n - n0 == 3 * FT

        @block.gpsimd
        def _(pool):
            counts = Counts()
            made, so_far, in_loop = counts.made, counts.so_far, counts.in_loop
            g = nc.gpsimd

            def load(dst, src, ev):
                pool.dma_start(dst, src).then_inc(sem(ev), 16)

            pool.wait_ge(sem("msk_in"), 16)
            g.tensor_copy(MSK[:, :], W[5][:, 0:(2 * LEVELS + 1) * P]).then_inc(sem("msk_bytes"), 1)
            load(HG, t["hgrn_norm"][0].partition_broadcast(P), "hg_in")
            load(KVG, t["mla_kv_norm"][0].partition_broadcast(P), "kvg_in")
            load(KR[:, 0, 64:96], t["cache_krope"][0, 0], "cache_in")
            load(CC, t["cache_ckv"][0, 0], "cache_in")
            g.memset(S0A[:, :, :, :], 0.0).then_inc(made("pool_chain"), 1)
            pool.wait_ge(sem("pool_chain"), so_far("pool_chain"))
            for d in range(2):
                states = t["state_hgrn"][0, 0, d].rearrange("(c h) k v -> h k c v", h=2)
                for h in range(2):
                    load(S0A[64 * h:64 * h + 64, d, :, 64 * h:64 * h + 64], states[h], "s0_in")
            g.memset(KR[:, 0, 0:64], 0.0).then_inc(sem("kr_zero"), 1)
            g.memset(KR[:, 1, 0:64], 0.0).then_inc(sem("kr_zero"), 1)
            g.memset(KR[:, 2, 0:64], 0.0).then_inc(sem("kr_zero"), 1)
            pool.wait_ge(sem("ckn"), 2)
            pool.dma_start(out["new_ckv"][0, 0], CKN[:, 0, :]).then_inc(sem("stored_ckv"), 16)
            pool.dma_start(out["new_krope"][0, 0], CKV[:, 0, P:P + 32]).then_inc(sem("stored_krope"), 16)
            for d in range(2):
                pool.wait_ge(sem("sh_ready"), d + 1)
                for h in range(2):
                    dst = out["new_hgrn"][0, 0, d].rearrange("(c h) k v -> h k c v", h=2)[h]
                    pool.dma_start(dst, SH[64 * h:64 * h + 64, d, :, 64 * h:64 * h + 64]).then_inc(sem("stored_hgrn"), 16)
            pool.wait_ge(sem("rw_inputs"), 1)
            with pool.Fori(0, KC) as c:
                pool.wait_ge(sem("rw_free"), c + 1)
                pool.sem_inc(sem("pool_settled"), 1)
                pool.dma_start(S0S[:, 0, :].rearrange("v (h k) -> v h k", h=2),
                               t["state_rwkv"][0, 0, 0].rearrange("(c h) v k -> c v h k", h=2)[bass.ds(c, 1)]
                               .rearrange("a v h k -> (a v) h k")).then_inc(sem("s0s"), 16)
                pool.dma_start(S0S[:, 1, :].rearrange("v (h k) -> v h k", h=2),
                               t["state_rwkv"][0, 0, 1].rearrange("(c h) v k -> c v h k", h=2)[bass.ds(c, 1)]
                               .rearrange("a v h k -> (a v) h k")).then_inc(sem("s0s"), 16)
                g.tensor_copy(VS[:, :, :], V1[:, :, bass.ds(c * P, P)]).then_inc(sem("vs"), 1)
                pool.wait_ge(sem("so"), c * 2 + 2)
                pool.sem_inc(sem("pool_settled"), 1)
                for d in range(2):
                    dst = out["new_rwkv"][0, 0, d].rearrange("(c h) v k -> c v h k", h=2)[bass.ds(c, 1)]
                    pool.dma_start(dst.rearrange("a v h k -> (a v) h k"),
                                   SO[:, d, :].rearrange("v (h k) -> v h k", h=2)).then_inc(sem("stored_rwkv"), 16)
                pool.wait_ge(sem("stored_rwkv"), c * 32 + 32)
            pool.wait_ge(sem("y_copy"), KC)
            load(W[1][:, 0:1024], t["rw_ln_w"][0].partition_broadcast(P), "ln_in")
            load(W[1][:, 1024:2048], t["rw_ln_b"][0].partition_broadcast(P), "ln_in")
            pool.wait_ge(sem("x_final"), 2)
            pool.dma_start(out["y_prompt"][0], X[:, 0, :]).then_inc(sem("stored_y"), 16)
            pool.dma_start(out["y_sample"][0], X[:, 1, :]).then_inc(sem("stored_y"), 16)
            pool.wait_ge(sem("stored_ckv"), 16)
            pool.wait_ge(sem("stored_krope"), 16)
            pool.wait_ge(sem("stored_hgrn"), 64)
            pool.wait_ge(sem("stored_rwkv"), 16 * 2 * KC)
            pool.wait_ge(sem("stored_y"), 32)

        @block.tensor
        def _(pe):
            mm, tr = nc.tensor.matmul, nc.tensor.transpose
            walk = Walk()

            def arrived(loads=1, i=None, per=0):
                s, due = walk.next(loads)
                pe.wait_ge(sem(f"slot{s}"), due if i is None else i * per + due)
                return ring[:, s, :]

            proj = [0]

            def target():
                p = proj[0]
                proj[0] += 1
                if p >= 4:
                    pe.wait_ge(sem("proj_copied"), p - 3)
                return bank[p % 4]

            def products(nc_, src, w, feature_major, n=TW):
                b = target()
                for a in range(2):
                    for k in range(KC):
                        if feature_major:
                            ins = mm(b[:, a * TW:(a + 1) * TW], w[:, k, a * P:(a + 1) * P], src[:, k, :],
                                     start=k == 0, stop=k == KC - 1)
                        else:
                            ins = mm(b[:, a * TW:a * TW + n], src[:, k, a * P:(a + 1) * P], w[:, k, 0:n],
                                     start=k == 0, stop=k == KC - 1)
                ins.then_inc(sem("tile_used"), 1)

            def tile_product(src, feature_major, n=TW):
                w = arrived()[:, 0:KC * n].rearrange("p (k n) -> p k n", k=KC)
                products(None, src, w, feature_major, n)

            def free_slot():
                pe.drain().then_inc(sem("tile_used"), 1)

            def ada(l):
                for n in range(24):
                    w = arrived()[:, :].rearrange("p (k n) -> p k n", k=KC)
                    for a in range(2):
                        col = (2 * n + a) * 2
                        for k in range(KC):
                            ins = mm(bank[7][:, col:col + 2], w[:, k, a * P:(a + 1) * P], CT[:, :, k],
                                     start=k == 0, stop=k == KC - 1)
                    ins.then_inc(sem("tile_used"), 1)

            def gates(n):
                pe.wait_ge(sem("ag"), n // 2 + 1)
                for st in range(NST):
                    for c in range(KC):
                        b = bank[4 + 2 * st + c // 4]
                        ins = mm(b[:, (c % 4) * P:(c % 4 + 1) * P],
                                 AG[:, n_gate(n), c, st:st + 1].to_broadcast([P, P]), ident, start=True, stop=True)
                        if c % 4 == 3:
                            ins.then_inc(sem("gb_done"), 1)

            def n_gate(n):
                return 1 + 2 * (n % 2)

            def turn(src, k):
                for st in range(NST):
                    for h in range(2):
                        for c in range(4):
                            ins = tr(bank[2 * st + h][:, c * P:(c + 1) * P], src(4 * h + c, st), ident)
                        ins.then_inc(sem("turned"), 1)

            def token_major(buf):
                return lambda c, st: buf[:, st, c * P:(c + 1) * P]

            pe.wait_ge(sem("rows_in"), 16 * 13)
            pe.wait_ge(sem("cst_in"), 16)
            tr(bank[4][:, 0:112], rows[0][0:112, :], ident[0:112, 0:112])
            tr(bank[4][:, 112:224], rows[1][0:112, :], ident[0:112, 0:112])
            tr(bank[4][:, 224:274], rows[2][0:50, :], ident[0:50, 0:50]).then_inc(sem("pv_done"), 1)
            pe.wait_ge(sem("ct"), 1)
            ada(0)

            pe.wait_ge(sem("xn"), 2)
            turn(token_major(O), 0)
            pe.wait_ge(sem("ht"), 1)
            for n in range(12):
                tile_product(HT, n < 6, TW if n < 11 else 160)

            pe.wait_ge(sem("kg"), 1)
            pe.wait_ge(sem("proj_copied"), 12)
            for lv in range(LEVELS + 1):
                if lv:
                    pe.wait_ge(sem("wq"), lv)
                for g in range(8):
                    n = 8 * lv + g
                    if n >= 4:
                        pe.wait_ge(sem("at"), n - 3)
                    d, h, pair = g // 4, g // 2 % 2, g % 2
                    hp = slice(64 * h, 64 * h + 64)
                    for j in range(4):
                        seg = ((4 * d + 2 * pair) * 2 + j) * P
                        seg, qs = slice(seg, seg + P), slice(seg - d * 1024, seg - d * 1024 + P)
                        lhs, rhs = (WQ[hp, seg], WQ[hp, seg]) if lv else (KG[hp, seg], W[0][hp, qs])
                        ins = mm(bank[n % 4][:, j * P:(j + 1) * P], lhs, rhs, start=True, stop=True)
                    ins.then_inc(sem("at_done"), 1)
            pe.wait_ge(sem("at"), 8 * (LEVELS + 1))
            pe.wait_ge(sem("qe"), 2)
            pe.wait_ge(sem("s0_in"), 64)
            for st in range(NST):
                for hd in range(HA):
                    c, h = hd // 2, hd % 2
                    o = bank[4 + st][:, hd * DH:(hd + 1) * DH]
                    v = V0[:, st, hd * DH:(hd + 1) * DH]
                    for d in range(2):
                        n = (h * 4 + c) * 2 + st
                        ins = mm(o, AT[d][:, n * P:(n + 1) * P], v, start=hd == 0 and d == 0, stop=True,
                                 skip_group_check=True)
                if st == 1:
                    for c in range(4):
                        for d in range(2):
                            seg = ((d * 4 + c) * 2 + 1) * P
                            ins = mm(bank[5][:, c * P:(c + 1) * P], WQ[:, seg:seg + P], S0A[:, d, c, :],
                                     start=False, stop=True, skip_group_check=True)
                ins.then_inc(sem("oa_done"), 1)
            pe.wait_ge(sem("kdf"), 1)
            for d in range(2):
                for c in range(4):
                    seg = ((d * 4 + c) * 2) * P
                    ins = tr(bank[d][:, c * P:(c + 1) * P], EX[:, seg:seg + P], ident)
                ins.then_inc(sem("kd_done"), 1)
            for d in range(2):
                pe.wait_ge(sem("kd"), d + 1)
                for c in range(4):
                    ins = mm(bank[2 + d][:, c * P:(c + 1) * P], KD[:, d, c, :], V0[:, 0, c * P:(c + 1) * P],
                             start=True, stop=True)
                ins.then_inc(sem("sh_done"), 1)

            pe.wait_ge(sem("cqn"), 2)
            for st in range(NST):
                for c in range(2):
                    ins = tr(bank[6][:, (2 * c + st) * P:(2 * c + st + 1) * P], CQ[:, st, c * P:(c + 1) * P], ident)
            ins.then_inc(sem("cqt_done"), 1)
            pe.wait_ge(sem("ckn"), 2)
            pe.wait_ge(sem("cache_in"), 32)
            for n, src in enumerate((CC, CKN[:, 1, :], CKN[:, 0, :])):
                ins = tr(bank[7][:, n * P:(n + 1) * P], src, ident)
            ins.then_inc(sem("ckt_done"), 1)
            pe.wait_ge(sem("kr_zero"), 3)
            pe.wait_ge(sem("kr"), 2)
            pe.wait_ge(sem("kd"), 2)
            for n in range(3):
                ins = tr(bank[0][0:96, n * P:(n + 1) * P], KR[:, n, :], ident)
            ins.then_inc(sem("krt_done"), 1)
            w = arrived()[:, 0:1536].rearrange("p (k n) -> p k n", k=2)
            pe.wait_ge(sem("cqt"), 1)
            pe.wait_ge(sem("sh_copied"), 2)
            for st in range(NST):
                for half in range(2):
                    b = bank[(1, 2, 3, 6)[2 * st + half]]
                    for k in range(2):
                        ins = mm(b[:, 0:384], CQT[:, k, st * P:(st + 1) * P], w[:, k, half * 384:(half + 1) * 384],
                                 start=k == 0, stop=k == 1)
                    ins.then_inc(sem("qt_done"), 1)
            free_slot()
            w = arrived()[:, 0:1024].rearrange("p (h m n) -> p h m n", h=HA, m=2)
            pe.wait_ge(sem("ckt"), 1)
            for hd in range(HA):
                b = bank[(7, 0)[hd % 2]]
                if hd == 1:
                    pe.wait_ge(sem("krt"), 1)
                if hd >= 2:
                    pe.wait_ge(sem("kt"), hd - 1)
                mm(b[0:64, 0:384], w[:, hd, 0, :], CKT, start=True, stop=True).then_inc(sem("kt_done"), 1)
            pe.wait_ge(sem("qt"), 4)
            for n in range(3):
                mm(bank[1 + n][:, :], CKT[:, n * P:(n + 1) * P], w[:, :, 1, :], start=True, stop=True).then_inc(sem("vm_done"), 1)
            free_slot()
            pe.wait_ge(sem("qrope"), 1)
            pe.wait_ge(sem("kt"), HA)
            pe.wait_ge(sem("vm"), 3)
            for n in range(4):
                for j in range(4):
                    hd, st = 2 * n + j // 2, j % 2
                    ins = tr(bank[n][0:96, j * P:(j + 1) * P], QT[:, st, hd * 96:(hd + 1) * 96], ident)
                ins.then_inc(sem("qtt_done"), 1)
            pe.wait_ge(sem("oa_copied"), 2)

            def scores(u):
                st, hp = u // 4, u % 4
                nk, k0 = (P, 256) if st == 0 else (256, 0)
                if u >= 2:
                    pe.wait_ge(sem("prob"), 2 * (u - 1))
                else:
                    pe.wait_ge(sem("qtt"), 4)
                for a in range(2):
                    hd = 2 * hp + a
                    ins = mm(bank[u % 2][:, a * 256:a * 256 + nk], HT[0:96, hd, st * P:(st + 1) * P],
                             kt(hd)[0:96, k0:k0 + nk], start=True, stop=True)
                ins.then_inc(sem("sc_done"), 1)

            def weigh(u):
                st, hp = u // 4, u % 4
                nt = 1 if st == 0 else 2
                pe.wait_ge(sem("prob"), 2 * (u + 1))
                if u >= 2:
                    pe.wait_ge(sem("pt"), u - 1)
                for a in range(2):
                    for k in range(nt):
                        ins = tr(bank[2 + u % 2][:, (2 * a + k) * P:(2 * a + k + 1) * P],
                                 PR[:, u % 4, a, k * P:(k + 1) * P], ident)
                ins.then_inc(sem("pt_done"), 1)
                pe.wait_ge(sem("pt"), u + 1)
                for a in range(2):
                    hd = 2 * hp + a
                    for k in range(nt):
                        ins = mm(bank[4 + st][:, hd * DH:(hd + 1) * DH], PT[:, u % 4, (2 * a + k) * P:(2 * a + k + 1) * P],
                                 VM[:, 2 if st == 0 else k, hd * DH:(hd + 1) * DH], start=k == 0, stop=k == nt - 1)
                ins.then_inc(sem("pv_att"), 1)

            scores(0)
            for u in range(8):
                if u + 1 < 8:
                    scores(u + 1)
                weigh(u)
            pe.wait_ge(sem("om"), 2)
            turn(token_major(OM), 1)
            gates(0)
            pe.wait_ge(sem("mt"), 1)
            for n in range(4):
                tile_product(MT, False)

            def hidden(first, i=None):
                due = [0]

                def at(k):
                    return first + k if i is None else i * FT + (first + k)

                def gate_up(j):
                    if i is not None or j >= 2:
                        pe.wait_ge(sem("hid"), at((j - 2 if j >= 2 else (-1 if j == 0 else -2)) + 1))
                    for which in range(2):
                        w = arrived(i=i, per=48)[:, :].rearrange("p (k n) -> p k n", k=KC)
                        b = bank[2 * (j % 2) + which]
                        for a in range(2):
                            for k in range(KC):
                                ins = mm(b[:, a * TW:(a + 1) * TW], w[:, k, a * P:(a + 1) * P], HT[:, k, :],
                                         start=k == 0, stop=k == KC - 1)
                        ins.then_inc(sem("tile_used"), 1)

                def down(j):
                    w = arrived(i=i, per=48)[:, :].rearrange("p (k n) -> p k n", k=2)
                    pe.wait_ge(sem("hid"), at(j + 1))
                    if j == 0 and (i is not None):
                        pe.wait_ge(sem("y_taken"), i + 1)
                    for st in range(NST):
                        for h in range(2):
                            for k in range(2):
                                ins = mm(bank[4 + 2 * st + h][:, :], HID[:, j % 2, k * TW + st * P:k * TW + (st + 1) * P],
                                         w[:, k, h * 512:(h + 1) * 512], start=j == 0 and k == 0,
                                         stop=j == FT - 1 and k == 1)
                    ins.then_inc(sem("tile_used"), 1)

                gate_up(0)
                for j in range(1, FT):
                    gate_up(j)
                    down(j - 1)
                down(FT - 1)

            pe.wait_ge(sem("xn"), 4)
            turn(token_major(O), 2)
            pe.wait_ge(sem("ht"), 2)
            gates(1)
            pe.wait_ge(sem("gb_copied"), 8)
            hidden(0)

            pe.wait_ge(sem("y_taken"), 1)
            ada(1)
            pe.wait_ge(sem("xn"), 6)
            turn(token_major(O), 3)
            for n in range(12):
                if n % 4 == 0:
                    pe.wait_ge(sem("xs"), n // 4 + 1)
                tile_product(XS[(n // 4) % 2], n < 8)
            s = arrived(3)
            w1 = s[:, 0:1024].rearrange("p (k n) -> p k n", k=KC)
            a1 = s[:, 1024:1536].rearrange("p (k n) -> p k n", k=KC)
            pe.wait_ge(sem("xs"), 4)
            b = target()
            for k in range(KC):
                ins = mm(b[:, 0:TW], w1[:, k, :], XS[1][:, k, :], start=k == 0, stop=k == KC - 1)
            ins.then_inc(sem("proj_done"), 1)
            pe.wait_ge(sem("xs"), 5)
            b = target()
            for k in range(KC):
                ins = mm(b[0:64, 0:TW], a1[:, k, :], XS[0][:, k, :], start=k == 0, stop=k == KC - 1)
            ins.then_inc(sem("proj_done"), 1)
            free_slot()
            s = arrived()[:, 0:1024].rearrange("p (k n) -> p k n", k=KC)
            pe.wait_ge(sem("xs"), 6)
            b = target()
            for k in range(KC):
                ins = mm(b[:, 0:TW], s[:, k, :], XS[1][:, k, :], start=k == 0, stop=k == KC - 1)
            ins.then_inc(sem("proj_done"), 1)
            free_slot()
            s = arrived()
            pe.wait_ge(sem("proj_copied"), proj[0])
            for d in range(2):
                hp = slice(64 * d, 64 * d + 64)
                for c in range(0, KC, 2):
                    b = target()
                    for a in range(2):
                        ins = mm(b[:, a * TW:(a + 1) * TW], s[hp, (c + a) * P:(c + a + 1) * P], MW[hp, :],
                                 start=True, stop=True)
                    ins.then_inc(sem("proj_done"), 1)
            free_slot()
            s = arrived()
            for c in range(0, KC, 2):
                b = target()
                for a in range(2):
                    ins = mm(b[:, a * TW:(a + 1) * TW], s[0:64, (c + a) * P:(c + a + 1) * P], MA[0:64, :],
                             start=True, stop=True)
                ins.then_inc(sem("proj_done"), 1)
            free_slot()
            pe.wait_ge(sem("kk2"), 1)
            pe.wait_ge(sem("ada_mod"), 2)
            for n in range(4):
                mm(bank[4 + n][:, :], blk, W[8][:, n * 512:(n + 1) * 512], start=True, stop=True).then_inc(sem("nrm_done"), 1)
            pe.wait_ge(sem("rk"), 1)
            pe.wait_ge(sem("nrm"), 4)
            for st in range(NST):
                for c in range(KC):
                    ins = mm(bank[4][:, st * HC + 2 * c:st * HC + 2 * c + 2], XS[0][:, c, st * P:(st + 1) * P],
                             blk[:, 0:P:DH], start=True, stop=True)
            ins.then_inc(sem("bon_done"), 1)
            pe.wait_ge(sem("rw_inputs"), 1)

            with pe.Fori(0, KC) as i:
                pe.wait_ge(sem("s0s"), i * 32 + 32)
                pe.sem_inc(sem("pe_settled"), 1)
                for d in range(2):
                    ins = tr(bank[7][:, 256 + d * DH:256 + (d + 1) * DH], S0S[:, d, :], ident[0:64, 0:64])
                ins.then_inc(sem("s0_t"), 1)
                pe.wait_ge(sem("vs"), i + 1)
                pe.wait_ge(sem("s0p"), i + 1)
                for d in range(2):
                    pe.wait_ge(sem("dec"), i * 2 + (d + 1))
                    for j in range(4):
                        st, h = j // 2, j % 2
                        hp = slice(64 * h, 64 * h + 64)
                        b = bank[4 * d + j]
                        mm(b[:, 0:256], BD[hp, d, st, :], NQ[hp, d, st, :, :], start=True, stop=True)
                        mm(b[:, 256:512], KDC[hp, d, st, :], NQ[hp, d, st, :, :], start=True, stop=True).then_inc(sem("t4"), 1)
                for d in range(2):
                    pe.wait_ge(sem("m4"), i * 8 + (4 * d + 4))
                    pe.sem_inc(sem("pe_settled"), 1)
                    for j in range(4):
                        ins = tr(bank[4 * d][:, j * P:(j + 1) * P], M4[d][:, j, 0, :], ident)
                    ins.then_inc(sem("nt"), 1)
                for lv in range(1, LEVELS):
                    for d in range(2):
                        pe.wait_ge(sem("inv"), i * 26 + (4 * (lv - 1) + 2 * d + 2))
                        for j in range(4):
                            ins = mm(bank[4 * d][:, j * P:(j + 1) * P], M4[d][:, j, 0, :], IX[d][:, j, :],
                                     start=True, stop=True)
                        ins.then_inc(sem("z"), 1)
                    for d in range(2):
                        pe.wait_ge(sem("zc"), i * 12 + (2 * (lv - 1) + d + 1))
                        if lv < LEVELS - 1:
                            for j in range(4):
                                ins = mm(bank[4 * d + 1][:, j * P:(j + 1) * P], IP[d][:, j, :], IZ[d][:, j, :],
                                         start=True, stop=True)
                            ins.then_inc(sem("dx"), 1)
                        for j in range(4):
                            ins = mm(bank[4 * d + 2][:, j * P:(j + 1) * P], IZ[d][:, j, :], IP[d][:, j, :],
                                     start=True, stop=True)
                        ins.then_inc(sem("dp"), 1)
                for d in range(2):
                    for j in range(4):
                        st, h = j // 2, j % 2
                        mm(bank[4 * d + 3][:, j * DH:(j + 1) * DH], M4[d][:, j, 2, :], VS[:, st, 64 * h:64 * h + 64],
                           start=j == 0, stop=True, skip_group_check=True)
                    mm(bank[4 * d + 3][:, 2 * DH:4 * DH], NQ[:, d, 1, 0, :], S0P[:, d, :],
                       start=False, stop=True, skip_group_check=True).then_inc(sem("g"), 1)
                for d in range(2):
                    pe.wait_ge(sem("gs"), i * 2 + (d + 1))
                    pe.wait_ge(sem("inv"), i * 26 + (25 + d))
                    for j in range(4):
                        ins = mm(bank[4 * d][:, j * DH:(j + 1) * DH], IP[d][:, j, :], GS[d][:, j, :], start=True, stop=True)
                    ins.then_inc(sem("u"), 1)
                pe.wait_ge(sem("us"), i * 2 + 2)
                for d in range(2):
                    for j in range(4):
                        st, h = j // 2, j % 2
                        o = bank[3][:, j * DH:(j + 1) * DH]
                        mm(o, M4[d][:, j, 1, :], US[d][:, j, :], start=d == 0 and j == 0, stop=True, skip_group_check=True)
                        mm(o, M4[d][:, j, 3, :], VS[:, st, 64 * h:64 * h + 64], start=False, stop=True,
                           skip_group_check=True)
                    ins = mm(bank[3][:, 2 * DH:4 * DH], NQ[:, d, 1, 1, :], S0P[:, d, :], start=False, stop=True,
                             skip_group_check=True)
                ins.then_inc(sem("y"), 1)
                for d in range(2):
                    tr(bank[4 * d + 1][:, 0:P], BD[:, d, 0, :], ident)
                    tr(bank[4 * d + 1][:, P:2 * P], KDC[:, d, 0, :], ident).then_inc(sem("trk_done"), 1)
                for d in range(2):
                    pe.wait_ge(sem("trk"), i * 2 + (d + 1))
                    for h in range(2):
                        o = bank[4 * d + 2][64 * h:64 * h + 64, 0:DH]
                        mm(o, TRK[:, d, 0, 64 * h:64 * h + 64], US[d][:, h, :], start=True, stop=False)
                        ins = mm(o, TRK[:, d, 1, 64 * h:64 * h + 64], VS[:, 0, 64 * h:64 * h + 64], start=False, stop=True)
                    ins.then_inc(sem("sf_done"), 1)
                for d in range(2):
                    pe.wait_ge(sem("sf"), i * 2 + (d + 1))
                    pe.sem_inc(sem("pe_settled"), 1)
                    tr(bank[4 * d + 1][0:64, 256:256 + P], SF[:, d, :], ident).then_inc(sem("so_done"), 1)
            pe.wait_ge(sem("so"), 2 * KC)
            s = arrived()
            for st in range(NST):
                for h in range(2):
                    b = target()
                    mm(b[:, :], MG[:, st * P:(st + 1) * P], s[:, h * 512:(h + 1) * 512],
                       start=True, stop=True).then_inc(sem("proj_done"), 1)
            free_slot()
            pe.wait_ge(sem("proj_copied"), 16 + 15 + 8 + 4 + 4)
            pe.wait_ge(sem("yg"), 1)
            turn(lambda c, st: Y1[:, c, st, :], 4)
            pe.wait_ge(sem("yt"), 1)
            for n in range(4):
                tile_product(XS[0], False)
            gates(2)
            pe.wait_ge(sem("xn"), 8)
            turn(token_major(O), 5)
            pe.wait_ge(sem("ht"), 3)
            w = arrived()[:, 0:KC * NE].rearrange("p (k n) -> p k n", k=KC)
            pe.wait_ge(sem("gb_copied"), 12)
            for st in range(NST):
                for k in range(KC):
                    ins = mm(bank[4][:, st * NE:(st + 1) * NE], HT[:, k, st * P:(st + 1) * P], w[:, k, :],
                             start=k == 0, stop=k == KC - 1)
            ins.then_inc(sem("logits"), 1)
            free_slot()
            pe.wait_ge(sem("lg"), 1)
            gates(3)
            pe.wait_ge(sem("gb_copied"), 16)
            with pe.Fori(0, NE) as e:
                hidden(FT, i=e)

        @block.scalar
        def _(act):
            counts = Counts()
            made, so_far, in_loop = counts.made, counts.so_far, counts.in_loop
            A = nc.scalar.activation
            sq = [0]

            def load(dst, src, ev):
                act.dma_start(dst, src).then_inc(sem(ev), 16)

            load(CST[:, :], t["cst"], "cst_in")
            r8 = lambda ap: ap.rearrange("(k p) -> k p", p=P)
            load(rows[0][0:96, :], t["ada_b"].rearrange("l (k p) -> (l k) p", p=P), "rows_in")
            load(rows[0][96:104, :], r8(t["c_ctx"]), "rows_in")
            load(rows[0][104:112, :], t["c"].rearrange("a (k p) -> (a k) p", p=P), "rows_in")
            load(rows[1][0:64, :], t["norm_gains"].rearrange("l g (k p) -> (l g k) p", p=P), "rows_in")
            load(rows[1][64:112, :], t["rw_mu"][0].rearrange("g (k p) -> (g k) p", p=P), "rows_in")
            load(rows[2][0:16, :], t["rw_w0"][0].rearrange("g (k p) -> (g k) p", p=P), "rows_in")
            for n, name in enumerate(("rw_a0", "rw_k_k", "rw_k_a", "rw_r_k")):
                load(rows[2][16 + 8 * n:24 + 8 * n, :], r8(t[name][0]), "rows_in")
            load(rows[2][48:50, :], r8(t["mla_q_norm"][0]), "rows_in")
            load(X[:, 0, :], t["x_prompt"][0], "rows_in")
            load(X[:, 1, :], t["x_sample"][0], "rows_in")
            load(W[5][:, 0:(2 * LEVELS + 1) * P], t["msk"], "msk_in")
            act.wait_ge(sem("rows_in"), 16 * 13)
            act.wait_ge(sem("pv"), 1)
            A(CT[:, :, :].rearrange("p s k -> p (s k)"), PV[:, COND:COND + 16], ACT.Silu).then_inc(sem("ct"), 1)

            def rstd(src, junk, n, ready):
                ready()
                for st in range(NST):
                    A(junk(st), src(st), ACT.Square, accum_out=SM[:, st:st + 1]).then_inc(sem("sumsq"), 1)
                sq[0] += 1
                act.wait_ge(sem("meansq"), sq[0])
                A(SM[:, 4:6], SM[:, 2:4], ACT.Sqrt).then_inc(sem("root"), 1)

            def norm_x(ready=lambda: None):
                rstd(lambda st: X[:, st, :], lambda st: O[:, st, :], D, ready)

            def norm_o(ready):
                rstd(lambda st: O[:, st, :], lambda st: W[9][:, st * D:(st + 1) * D], D, ready)

            def copy_gates(n):
                for k in range(4):
                    act.wait_ge(sem("gb_done"), 4 * n + k + 1)
                    A(GB[:, k // 2, (k % 2) * 512:(k % 2 + 1) * 512], bank[4 + k][:, :], ACT.Copy).then_inc(sem("gb_copied"), 1)

            proj = [0]

            low = [0]

            def filled(tile):
                if tile is None:
                    low[0] += 1
                    act.wait_ge(sem("proj_done"), low[0])
                else:
                    act.wait_ge(sem("tile_used"), tile + 1)

            def take(dst, tile, func=ACT.Copy, n=512, src=None, **kw):
                p = proj[0]
                proj[0] += 1
                filled(tile)
                b = bank[p % 4]
                A(dst, b[:, 0:n] if src is None else src(b), func, **kw).then_inc(sem("proj_copied"), 1)

            halves = lambda b: b[:, :].rearrange("p (s n) -> p s n", s=NST)

            norm_x()
            for n in range(12):
                if n < 2:
                    take(W[0][:, n * 512:(n + 1) * 512], 24 + n)
                elif n < 6:
                    take(W[1][:, (n - 2) * 512:(n - 1) * 512], 24 + n)
                elif n < 8:
                    take(V0[:, :, (n - 6) * TW:(n - 5) * TW], 24 + n, src=halves)
                elif n < 10:
                    take(GA[:, :, (n - 8) * TW:(n - 7) * TW], 24 + n, src=halves)
                elif n == 10:
                    take(CQ[:, :, :], 24 + n, src=halves)
                else:
                    take(CKV[:, :, :], 24 + n, src=lambda b: halves(b)[:, :, 0:160])
            act.wait_ge(sem("absf"), 1)
            A(EX[:, :], EX[:, :], ACT.Exp, scale=-1.0).then_inc(made("act_chain"), 1)
            act.wait_ge(sem("act_chain"), so_far("act_chain"))
            A(EX[:, :], EX[:, :], ACT.Ln, bias=1.0).then_inc(sem("ln"), 1)
            act.wait_ge(sem("lfx"), 1)
            A(KG[:, :], EX[:, :], ACT.Exp).then_inc(sem("kg"), 1)
            for lv in range(LEVELS):
                act.wait_ge(sem("diff"), lv + 1)
                A(EX[:, :], EX[:, :], ACT.Exp).then_inc(sem("ex"), 1)
            act.wait_ge(sem("ex_used"), LEVELS)
            A(EX[:, :], BC[:, :], ACT.Exp).then_inc(sem("ex"), 1)
            act.wait_ge(sem("diff"), LEVELS + 1)
            A(EX[:, :], EX[:, :], ACT.Exp).then_inc(sem("ex"), 1)
            act.wait_ge(sem("proj_copied"), 12)
            act.wait_ge(sem("msq_free"), 1)
            for st in range(NST):
                A(W[4][:, 1536:1792], CQ[:, st, :], ACT.Square, accum_out=SM[:, 8 + st:9 + st]).then_inc(made("lat_sq"), 1)
                act.wait_ge(sem("lat_sq"), so_far("lat_sq"))
                A(W[4][:, 1792:1920], CKV[:, st, 0:P], ACT.Square, accum_out=SM[:, 10 + st:11 + st]).then_inc(made("lat_sq"), 1)
                act.wait_ge(sem("lat_sq"), so_far("lat_sq"))
            act.wait_ge(sem("lat_ms"), 1)
            A(SM[:, 8:12], SM[:, 8:12], ACT.Sqrt).then_inc(sem("lat_root"), 1)
            for d in range(2):
                act.wait_ge(sem("kd_done"), d + 1)
                A(KD[:, d, :, :].rearrange("p c n -> p (c n)"), bank[d][:, :], ACT.Copy).then_inc(sem("kd"), 1)
            for d in range(2):
                act.wait_ge(sem("sh_done"), d + 1)
                A(SH[:, d, :, :].rearrange("p c n -> p (c n)"), bank[2 + d][:, :], ACT.Copy).then_inc(sem("sh_copied"), 1)
            for st in range(NST):
                act.wait_ge(sem("oa_done"), st + 1)
                A(OA[:, st, :], bank[4 + st][:, :], ACT.Copy).then_inc(sem("oa_copied"), 1)
            act.wait_ge(sem("lfx"), 1)
            A(SG[:, :, :].rearrange("p s n -> p (s n)"), GA[:, :, :].rearrange("p s n -> p (s n)"), ACT.Silu).then_inc(sem("sg"), 1)
            act.wait_ge(sem("oa_ms"), 1)
            A(SM[:, 32:48], SM[:, 16:32], ACT.Sqrt).then_inc(sem("oa_root"), 1)
            act.wait_ge(sem("ckt_done"), 1)
            A(CKT, bank[7][:, 0:384], ACT.Copy).then_inc(sem("ckt"), 1)
            for n in range(4):
                act.wait_ge(sem("qt_done"), n + 1)
                A(QT[:, n // 2, (n % 2) * 384:(n % 2 + 1) * 384], bank[(1, 2, 3, 6)[n]][:, 0:384], ACT.Copy).then_inc(sem("qt"), 1)
            for hd in range(HA):
                act.wait_ge(sem("kt_done"), hd + 1)
                A(kt(hd)[0:64, :], bank[(7, 0)[hd % 2]][0:64, 0:384], ACT.Copy).then_inc(sem("kt"), 1)
            for n in range(3):
                act.wait_ge(sem("vm_done"), n + 1)
                A(VM[:, n, :], bank[1 + n][:, :], ACT.Copy).then_inc(sem("vm"), 1)
            for n in range(4):
                act.wait_ge(sem("qtt_done"), n + 1)
                A(HTf[0:96, n * 512:(n + 1) * 512], bank[n][0:96, :], ACT.Copy).then_inc(sem("qtt"), 1)
            for u in range(8):
                st = u // 4
                nk = P if st == 0 else 256
                act.wait_ge(sem("nmx"), u + 1)
                for a in range(2):
                    n = 2 * u + a
                    A(PR[:, u % 4, a, 0:nk], bank[u % 2][:, a * 256:a * 256 + nk], ACT.Exp,
                      bias=SM[:, 64 + n:65 + n], scale=SCALE, accum_out=SM[:, 80 + n:81 + n]).then_inc(sem("prob"), 1)
            act.wait_ge(sem("stored_ckv"), 16)
            act.wait_ge(sem("stored_krope"), 16)
            copy_gates(0)
            for n in range(4):
                take(O[:, :, n * TW:(n + 1) * TW], N_EVEN_OUT + n, src=halves)
            norm_o(lambda: act.wait_ge(sem("proj_copied"), proj[0]))
            norm_x(lambda: act.wait_ge(sem("x"), 2))
            copy_gates(1)

            def silus(first, i=None):
                for j in range(FT):
                    used = (N_FFN if i is None else N_MOE) + up_used(j)
                    act.wait_ge(sem("tile_used"), used if i is None else i * 3 * FT + used)
                    A(SIL[:, j % 2, :], bank[2 * (j % 2)][:, :], ACT.Silu).then_inc(sem("silu"), 1)

            silus(0)
            norm_o(lambda: act.wait_ge(sem("o_ready"), 1))
            norm_x(lambda: act.wait_ge(sem("x"), 4))
            for n in range(8):
                take(W[n // 4][:, (n % 4) * 512:(n % 4 + 1) * 512], N_ODD + n)
            for n in range(4):
                take(V1[:, :, n * TW:(n + 1) * TW], N_ODD + 8 + n, src=halves)
            take(MW, None, ACT.Tanh, 256)
            take(MA[0:64, :], None, src=lambda b: b[0:64, 0:TW])
            take(MG, None, ACT.Sigmoid, 256)

            def biased(dst, col):
                p = proj[0]
                proj[0] += 1
                filled(None)
                A(dst[:, 0, :], bank[p % 4][:, 0:TW], ACT.Sigmoid, bias=PV[:, col:col + 1])
                A(dst[:, 1, :], bank[p % 4][:, TW:2 * TW], ACT.Sigmoid, bias=PV[:, col + 1:col + 2]).then_inc(sem("proj_copied"), 1)

            for d in range(2):
                for c in range(0, KC, 2):
                    biased(SGM[d][:, c:c + 2, :], W0 + d * KC + c)
            for c in range(0, KC, 2):
                biased(B[:, c:c + 2, :], A0 + c)
            act.wait_ge(sem("nrm"), 4)
            A(W[8][:, :], W[8][:, :], ACT.Sqrt).then_inc(sem("nrm_root"), 1)
            act.wait_ge(sem("rw_inputs"), 1)
            with act.Fori(0, KC) as i:
                act.wait_ge(sem("km"), i + 1)
                for n in range(4):
                    A(EE[:, n, :], CS[:, n, :], ACT.Exp, bias=SM[:, 100 + n:101 + n], scale=-KAPPA).then_inc(sem("ee"), 1)
                    a = 1 - n // 2
                    A(E2[:, n, :], CS[:, n, a:a + P], ACT.Exp, bias=SM[:, 104 + n:105 + n], scale=KAPPA).then_inc(sem("e2"), 1)
                A(SM[:, 108:112], SM[:, 104:108], ACT.Exp).then_inc(sem("em"), 1)
                for lv in range(1, LEVELS):
                    for d in range(2):
                        act.wait_ge(sem("z"), i * 12 + (2 * (lv - 1) + d + 1))
                        A(IZ[d][:, :, :].rearrange("p j n -> p (j n)"), bank[4 * d][:, :], ACT.Copy).then_inc(sem("zc"), 1)
                for d in range(2):
                    act.wait_ge(sem("g"), i * 2 + (d + 1))
                    A(GS[d][:, :, :].rearrange("p j n -> p (j n)"), bank[4 * d + 3][:, 0:256], ACT.Copy).then_inc(sem("gs"), 1)
                for d in range(2):
                    act.wait_ge(sem("u"), i * 2 + (d + 1))
                    A(US[d][:, :, :].rearrange("p j n -> p (j n)"), bank[4 * d][:, 0:256], ACT.Copy).then_inc(sem("us"), 1)
                act.wait_ge(sem("y"), i + 1)
                A(W[0][:, bass.ds(i * 256, 256)], bank[3][:, 0:256], ACT.Copy).then_inc(sem("y_copy"), 1)
                for d in range(2):
                    act.wait_ge(sem("trk_done"), i * 2 + (d + 1))
                    A(TRK[:, d, :, :].rearrange("p m n -> p (m n)"), bank[4 * d + 1][:, 0:256], ACT.Copy).then_inc(sem("trk"), 1)
                for d in range(2):
                    act.wait_ge(sem("so_done"), i * 2 + (d + 1))
                    A(SO[:, d, :], bank[4 * d + 1][0:64, 256:256 + P], ACT.Copy).then_inc(sem("so"), 1)
            for st in range(NST):
                for h in range(2):
                    take(G1[:, st, h * 512:(h + 1) * 512], None)
            act.wait_ge(sem("gn_ms"), 1)
            A(SM[:, 128:160], SM[:, 128:160], ACT.Sqrt).then_inc(sem("gn_root"), 1)
            for n in range(4):
                take(O[:, :, n * TW:(n + 1) * TW], N_ODD_OUT + n, src=halves)
            norm_o(lambda: act.wait_ge(sem("proj_copied"), proj[0]))
            copy_gates(2)
            norm_x(lambda: act.wait_ge(sem("x"), 6))
            act.wait_ge(sem("lgd"), 1)
            A(SM[:, 60:62], SM[:, 60:62], ACT.Exp).then_inc(sem("lge"), 1)
            act.wait_ge(sem("x"), 6)
            copy_gates(3)
            with act.Fori(0, NE) as e:
                silus(FT, i=e)
            norm_o(lambda: act.wait_ge(sem("o_ready"), 2))

        @block.vector
        def _(dve):
            counts = Counts()
            made, so_far, in_loop = counts.made, counts.so_far, counts.in_loop
            v = nc.vector
            cnt = {"rstd": 0}

            def rstd(n):
                k = cnt["rstd"] = cnt["rstd"] + 1
                dve.wait_ge(sem("sumsq"), 2 * k)
                v.tensor_scalar(SM[:, 2:4], SM[:, 0:2], 1.0 / n, EPS, ALU.mult, ALU.add).then_inc(sem("meansq"), 1)
                dve.wait_ge(sem("root"), k)
                v.reciprocal(SM[:, 6:8], SM[:, 4:6]).then_inc(made("dve_chain"), 1)
                dve.wait_ge(sem("dve_chain"), so_far("dve_chain"))

            def normed_x():
                rstd(D)
                for st in range(NST):
                    v.tensor_scalar(O[:, st, :], X[:, st, :], SM[:, 6 + st:7 + st], None, ALU.mult).then_inc(sem("xn"), 1)

            def modulated(dst, k, scale, shift, ev):
                for st in range(NST):
                    for h in range(2):
                        dve.wait_ge(sem("turned"), 4 * k + 2 * st + h + 1)
                        for c in range(4):
                            n = 4 * h + c
                            ins = v.tensor_scalar(dst[:, n, st * P:(st + 1) * P], bank[2 * st + h][:, c * P:(c + 1) * P],
                                                  AG[:, scale, n, st:st + 1], MOD[:, shift, n, st:st + 1],
                                                  ALU.mult, ALU.add)
                            if (st, n) == (NST - 1, KC - 1):
                                ins.then_inc(made(ev), 1)
                                dve.wait_ge(sem(ev), so_far(ev))
                            else:
                                ins.then_inc(made("dve_chain"), 1)
                                dve.wait_ge(sem("dve_chain"), so_far("dve_chain"))

            def plain(dst, k, ev):
                for st in range(NST):
                    for h in range(2):
                        dve.wait_ge(sem("turned"), 4 * k + 2 * st + h + 1)
                        ins = v.tensor_copy(dst[:, 4 * h:4 * h + 4, st * P:(st + 1) * P],
                                            bank[2 * st + h][:, :].rearrange("p (c n) -> p c n", c=4))
                        done = ev if (st, h) == (1, 1) else "dve_chain"
                        ins.then_inc(made(done), 1)
                        dve.wait_ge(sem(done), so_far(done))

            def residual(n):
                rstd(D)
                dve.wait_ge(sem("gb_copied"), 4 * (n + 1))
                for st in range(NST):
                    v.scalar_tensor_tensor(O[:, st, :], O[:, st, :], SM[:, 6 + st:7 + st], GB[:, st, :],
                                           ALU.mult, ALU.mult).then_inc(made("dve_chain"), 1)
                    dve.wait_ge(sem("dve_chain"), so_far("dve_chain"))
                    done = "x_final" if n == 3 else "x"
                    v.tensor_tensor(X[:, st, :], X[:, st, :], O[:, st, :], ALU.add).then_inc(made(done), 1)
                    dve.wait_ge(sem(done), so_far(done))

            def modulation(l):
                dve.wait_ge(sem("tile_used"), 24 if l == 0 else N_ODD)
                bias = PV[:, ADAB + 48 * l:ADAB + 48 * (l + 1)]
                for st in range(NST):
                    v.tensor_tensor(MOD[:, :, :, st].rearrange("p a k -> p (a k)"),
                                    bank[7][:, 0:96].rearrange("p (n s) -> p n s", s=NST)[:, :, st], bias, ALU.add).then_inc(made("dve_chain"), 1)
                    dve.wait_ge(sem("dve_chain"), so_far("dve_chain"))
                for m, (src, one) in enumerate(((1, 1.0), (2, 0.0), (4, 1.0), (5, 0.0))):
                    gain = PV[:, GAIN + (4 * l + m) * KC:GAIN + (4 * l + m + 1) * KC]
                    for st in range(NST):
                        ins = v.scalar_tensor_tensor(AG[:, m, :, st], MOD[:, src, :, st], one, gain, ALU.add, ALU.mult)
                        done = "ag" if (m, st) == (3, 1) else "dve_chain"
                        ins.then_inc(made(done), 1)
                        dve.wait_ge(sem(done), so_far(done))

            dve.wait_ge(sem("pv_done"), 1)
            v.tensor_copy(PV[:, :], bank[4][:, 0:NPV]).then_inc(made("pv"), 1)
            dve.wait_ge(sem("pv"), so_far("pv"))
            modulation(0)
            dve.wait_ge(sem("rows_in"), 16 * 13)
            normed_x()
            modulated(HT, 0, 0, 0, "ht")

            dve.wait_ge(sem("proj_copied"), 6)
            dve.wait_ge(sem("msk_bytes"), 1)
            f = W[1]
            v.scalar_tensor_tensor(EX[:, :], f[:, :], -1.0, f[:, :], ALU.mult, ALU.max).then_inc(made("absf"), 1)
            dve.wait_ge(sem("absf"), so_far("absf"))
            dve.wait_ge(sem("ln"), 1)
            v.scalar_tensor_tensor(LF[:, :], f[:, :], 0.0, EX[:, :], ALU.min, ALU.subtract).then_inc(made("dve_chain"), 1)
            dve.wait_ge(sem("dve_chain"), so_far("dve_chain"))
            v.tensor_tensor(EX[:, :], LF[:, :], f[:, :], ALU.subtract).then_inc(made("lfx"), 1)
            dve.wait_ge(sem("lfx"), so_far("lfx"))
            for n in range(16):
                a, b = LF[:, n * P:(n + 1) * P], BC[:, n * P:(n + 1) * P]
                if n >= 8:
                    a, b = a[:, ::-1], b[:, ::-1]
                v.tensor_tensor_scan(b, ones, a, 0.0, ALU.mult, ALU.add).then_inc(made("dve_chain"), 1)
                dve.wait_ge(sem("dve_chain"), so_far("dve_chain"))
            v.memset(AT[1][:, :], 0.0).then_inc(made("dve_chain"), 1)
            dve.wait_ge(sem("dve_chain"), so_far("dve_chain"))
            v.memset(AT[0][:, :], 0.0).then_inc(made("dve_chain"), 1)
            dve.wait_ge(sem("dve_chain"), so_far("dve_chain"))

            def take_a(n, m):
                d = n % 8 // 4
                dve.wait_ge(sem("at_done"), n + 1)
                v.copy_predicated(AT[d][:, (n % 4) * 512:(n % 4 + 1) * 512].rearrange("p (j n) -> p j n", j=4),
                                  m[d].unsqueeze(1).to_broadcast([P, 4, P]),
                                  bank[n % 4][:, :].rearrange("p (j n) -> p j n", j=4)).then_inc(made("at"), 1)
                dve.wait_ge(sem("at"), so_far("at"))

            for lv in range(LEVELS + 1):
                if lv < LEVELS:
                    s = 1 << lv
                    if lv == 0:
                        dve.wait_ge(sem("kg"), 1)
                    for d in range(2):
                        half = slice(d * 1024, (d + 1) * 1024)
                        shape = lambda b: b.rearrange("p (n h s) -> p n h s", h=2, s=s)
                        b, e = shape(BC[:, half]), shape(EX[:, half])
                        mid = (b[:, :, 0, s - 1:s] if d == 0 else b[:, :, 1, 0:1]).to_broadcast([P, 512 // s, s])
                        late, early = (1, 0) if d == 0 else (0, 1)
                        v.tensor_tensor(e[:, :, late, :], b[:, :, late, :], mid, ALU.subtract).then_inc(made("dve_chain"), 1)
                        dve.wait_ge(sem("dve_chain"), so_far("dve_chain"))
                        done = "diff" if d else "dve_chain"
                        v.tensor_tensor(e[:, :, early, :], mid, b[:, :, early, :], ALU.subtract).then_inc(made(done), 1)
                        dve.wait_ge(sem(done), so_far(done))
                m = [mask(lv - 1, 0), mask(lv - 1, 1)] if lv else [mask(LEVELS, 0)] * 2
                for g in range(8):
                    take_a(8 * lv + g, m)
                if lv < LEVELS:
                    dve.wait_ge(sem("ex"), lv + 1)
                    for d in range(2):
                        half = slice(d * 1024, (d + 1) * 1024)
                        e, w, k, q = (shape(x) for x in (EX[:, half], WQ[:, half], KG[:, half], W[0][:, 0:1024]))
                        late, early = (1, 0) if d == 0 else (0, 1)
                        v.tensor_tensor(w[:, :, late, :], e[:, :, late, :], q[:, :, late, :], ALU.mult).then_inc(made("dve_chain"), 1)
                        dve.wait_ge(sem("dve_chain"), so_far("dve_chain"))
                        done = "wq" if d else "dve_chain"
                        v.tensor_tensor(w[:, :, early, :], e[:, :, early, :], k[:, :, early, :], ALU.mult).then_inc(made(done), 1)
                        dve.wait_ge(sem(done), so_far(done))
                    v.tensor_copy(SM[:, 198:199], SM[:, 6:7]).then_inc(made("ex_used"), 1)
                    dve.wait_ge(sem("ex_used"), so_far("ex_used"))
            dve.wait_ge(sem("ex"), LEVELS + 1)
            for d in range(2):
                half = slice(d * 1024, (d + 1) * 1024)
                v.tensor_tensor(WQ[:, half], EX[:, half], W[0][:, 0:1024], ALU.mult).then_inc(made("qe"), 1)
                dve.wait_ge(sem("qe"), so_far("qe"))
            for d in range(2):
                half = slice(d * 1024, (d + 1) * 1024)
                b, e = (x[:, half].rearrange("p (n s) -> p n s", s=P) for x in (BC, EX))
                end = (b[:, :, P - 1:P] if d == 0 else b[:, :, 0:1]).to_broadcast([P, 8, P])
                done = "diff" if d else "dve_chain"
                v.tensor_tensor(e, end, b, ALU.subtract).then_inc(made(done), 1)
                dve.wait_ge(sem(done), so_far(done))
            dve.wait_ge(sem("ex"), LEVELS + 2)
            v.tensor_tensor(EX[:, :], EX[:, :], KG[:, :], ALU.mult).then_inc(made("kdf"), 1)
            dve.wait_ge(sem("kdf"), so_far("kdf"))
            v.tensor_copy(SM[:, 198:199], SM[:, 6:7]).then_inc(made("msq_free"), 1)
            dve.wait_ge(sem("msq_free"), so_far("msq_free"))
            dve.wait_ge(sem("lat_sq"), 4)
            v.tensor_scalar(SM[:, 8:10], SM[:, 8:10], 1.0 / 256, EPS, ALU.mult, ALU.add).then_inc(made("dve_chain"), 1)
            dve.wait_ge(sem("dve_chain"), so_far("dve_chain"))
            v.tensor_scalar(SM[:, 10:12], SM[:, 10:12], 1.0 / P, EPS, ALU.mult, ALU.add).then_inc(made("lat_ms"), 1)
            dve.wait_ge(sem("lat_ms"), so_far("lat_ms"))
            dve.wait_ge(sem("lat_root"), 1)
            v.reciprocal(SM[:, 12:16], SM[:, 8:12]).then_inc(made("dve_chain"), 1)
            dve.wait_ge(sem("dve_chain"), so_far("dve_chain"))
            dve.wait_ge(sem("kvg_in"), 16)
            for st in range(NST):
                v.tensor_scalar(CQ[:, st, :], CQ[:, st, :], SM[:, 12 + st:13 + st], None, ALU.mult).then_inc(made("cqn"), 1)
                dve.wait_ge(sem("cqn"), so_far("cqn"))
                v.scalar_tensor_tensor(CKN[:, st, :], CKV[:, st, 0:P], SM[:, 14 + st:15 + st], KVG,
                                       ALU.mult, ALU.mult).then_inc(made("ckn"), 1)
                dve.wait_ge(sem("ckn"), so_far("ckn"))
            cos, sin = CST[:, C_COS:C_COS + 32], CST[:, C_SIN:C_SIN + 32]
            parts = lambda x: x.rearrange("p (a b n) -> p a b n", a=2, b=2)
            v.tensor_copy(KR[:, 2, 64:96], CKV[:, 0, P:P + 32]).then_inc(made("kr"), 1)
            dve.wait_ge(sem("kr"), so_far("kr"))
            kr, ks = CKV[:, 1, P:P + 32], KR[:, 1, 64:96]
            for b in range(2):
                v.tensor_tensor(parts(SM[:, 120:152])[:, :, b, :], parts(kr)[:, :, 1 - b, :], parts(sin)[:, :, b, :],
                                ALU.mult).then_inc(made("dve_chain"), 1)
                dve.wait_ge(sem("dve_chain"), so_far("dve_chain"))
            v.tensor_tensor(ks, kr, cos, ALU.mult).then_inc(made("dve_chain"), 1)
            dve.wait_ge(sem("dve_chain"), so_far("dve_chain"))
            v.tensor_tensor(ks, ks, SM[:, 120:152], ALU.add).then_inc(made("kr"), 1)
            dve.wait_ge(sem("kr"), so_far("kr"))
            dve.wait_ge(sem("cqt_done"), 1)
            for c in range(2):
                done = "cqt" if c else "dve_chain"
                v.tensor_scalar(CQT[:, c, :], bank[6][:, c * TW:(c + 1) * TW], PV[:, QN + c:QN + c + 1], None,
                                ALU.mult).then_inc(made(done), 1)
                dve.wait_ge(sem(done), so_far(done))
            dve.wait_ge(sem("krt_done"), 1)
            for h in range(2):
                done = "krt" if h else "dve_chain"
                v.tensor_copy(KT[h][64:96, 0:1536].rearrange("p (h n) -> p h n", h=4),
                              bank[0][64:96, 0:384].unsqueeze(1).to_broadcast([32, 4, 384])).then_inc(made(done), 1)
                dve.wait_ge(sem(done), so_far(done))
            dve.wait_ge(sem("sh_copied"), 2)
            for d in range(2):
                v.tensor_copy(SM[:, 198:199], SM[:, 6:7]).then_inc(made("sh_ready"), 1)
                dve.wait_ge(sem("sh_ready"), so_far("sh_ready"))
            dve.wait_ge(sem("oa_copied"), 2)
            oa = W[1][:, 0:1024]
            per = lambda x, n=16: x.rearrange("p (h n) -> p h n", n=DH)
            v.tensor_tensor(WQ[:, 0:1024], oa, oa, ALU.mult).then_inc(made("dve_chain"), 1)
            dve.wait_ge(sem("dve_chain"), so_far("dve_chain"))
            v.tensor_reduce(SM[:, 16:32], per(WQ[:, 0:1024]), AX.X, ALU.add).then_inc(made("dve_chain"), 1)
            dve.wait_ge(sem("dve_chain"), so_far("dve_chain"))
            v.tensor_scalar(SM[:, 16:32], SM[:, 16:32], 1.0 / DH, EPS, ALU.mult, ALU.add).then_inc(made("oa_ms"), 1)
            dve.wait_ge(sem("oa_ms"), so_far("oa_ms"))
            dve.wait_ge(sem("oa_root"), 1)
            v.reciprocal(SM[:, 48:64], SM[:, 32:48]).then_inc(made("dve_chain"), 1)
            dve.wait_ge(sem("dve_chain"), so_far("dve_chain"))
            v.tensor_tensor(per(oa), per(oa), SM[:, 48:64].unsqueeze(2).to_broadcast([P, 16, DH]), ALU.mult).then_inc(made("dve_chain"), 1)
            dve.wait_ge(sem("dve_chain"), so_far("dve_chain"))
            dve.wait_ge(sem("hg_in"), 16)
            v.tensor_tensor(per(oa), per(oa), HG.unsqueeze(1).to_broadcast([P, 16, DH]), ALU.mult).then_inc(made("dve_chain"), 1)
            dve.wait_ge(sem("dve_chain"), so_far("dve_chain"))
            dve.wait_ge(sem("sg"), 1)
            v.tensor_tensor(OM[:, :, 0:512], OA[:, :, :], SG[:, :, :], ALU.mult).then_inc(made("om"), 1)
            dve.wait_ge(sem("om"), so_far("om"))
            dve.wait_ge(sem("qt"), 4)
            q = QT[:, 1, :].rearrange("p (h n) -> p h n", h=HA)[:, :, 64:96]
            q4 = q.rearrange("p h (a b n) -> p h a b n", a=2, b=2)
            tq = TQ[:, 0:256].rearrange("p (h n) -> p h n", h=HA)
            t4 = tq.rearrange("p h (a b n) -> p h a b n", a=2, b=2)
            for a in range(2):
                for b in range(2):
                    v.tensor_tensor(t4[:, :, a, b, :], q4[:, :, a, 1 - b, :],
                                    parts(sin)[:, a, b, :].unsqueeze(1).to_broadcast([P, HA, 8]), ALU.mult).then_inc(made("dve_chain"), 1)
                    dve.wait_ge(sem("dve_chain"), so_far("dve_chain"))
            v.tensor_tensor(q, q, cos.unsqueeze(1).to_broadcast([P, HA, 32]), ALU.mult).then_inc(made("dve_chain"), 1)
            dve.wait_ge(sem("dve_chain"), so_far("dve_chain"))
            v.tensor_tensor(q, q, tq, ALU.add).then_inc(made("qrope"), 1)
            dve.wait_ge(sem("qrope"), so_far("qrope"))

            def maxima(u):
                st = u // 4
                nk = P if st == 0 else 256
                dve.wait_ge(sem("sc_done"), u + 1)
                s = bank[u % 2][:, :].rearrange("p (a n) -> p a n", a=2)[:, :, 0:nk]
                v.tensor_reduce(SM[:, 96:98], s, AX.X, ALU.max).then_inc(made("dve_chain"), 1)
                dve.wait_ge(sem("dve_chain"), so_far("dve_chain"))
                v.tensor_scalar(SM[:, 64 + 2 * u:66 + 2 * u], SM[:, 96:98], -SCALE, None, ALU.mult).then_inc(made("nmx"), 1)
                dve.wait_ge(sem("nmx"), so_far("nmx"))

            maxima(0)
            for u in range(8):
                if u < 7:
                    maxima(u + 1)
                dve.wait_ge(sem("pt_done"), u + 1)
                n = 1 if u < 4 else 2
                view = lambda x: x.rearrange("p (a k) -> p a k", a=2)[:, :, 0:n * P]
                v.tensor_copy(view(PT[:, u % 4, :]), view(bank[2 + u % 2][:, :])).then_inc(made("pt"), 1)
                dve.wait_ge(sem("pt"), so_far("pt"))
            dve.wait_ge(sem("prob"), 16)
            v.reciprocal(SM[:, 80:96], SM[:, 80:96]).then_inc(made("dve_chain"), 1)
            dve.wait_ge(sem("dve_chain"), so_far("dve_chain"))
            for st in range(NST):
                dve.wait_ge(sem("pv_att"), 4 * (st + 1))
                done = "om" if st else "dve_chain"
                v.tensor_tensor(per(OM[:, st, 512:1024]), per(bank[4 + st][:, :]),
                                SM[:, 80 + 8 * st:88 + 8 * st].unsqueeze(2).to_broadcast([P, HA, DH]), ALU.mult).then_inc(made(done), 1)
                dve.wait_ge(sem(done), so_far(done))
            dve.wait_ge(sem("stored_hgrn"), 64)
            plain(MT, 1, "mt")
            residual(0)
            normed_x()
            modulated(HT, 2, 2, 3, "ht")

            def hiddens(first, i=None):
                for j in range(FT):
                    dve.wait_ge(sem("silu"), first + j + 1 if i is None else i * FT + (first + j + 1))
                    if i is None and j >= 2:
                        dve.wait_ge(sem("tile_used"), N_FFN + down_used(j - 2))
                    if i is not None:
                        used = down_used(j - 2) if j >= 2 else down_used(FT - 1 - j) - 3 * FT
                        dve.wait_ge(sem("tile_used"), i * 3 * FT + (N_MOE + used))
                    v.tensor_tensor(HID[:, j % 2, :], SIL[:, j % 2, :], bank[2 * (j % 2) + 1][:, :], ALU.mult).then_inc(sem("hid"), 1)

            hiddens(0)
            dve.wait_ge(sem("tile_used"), N_ADA1)
            for n in range(4):
                done = "y_taken" if n == 3 else "dve_chain"
                v.tensor_copy(O[:, n // 2, (n % 2) * 512:(n % 2 + 1) * 512], bank[4 + n][:, :]).then_inc(made(done), 1)
                dve.wait_ge(sem(done), so_far(done))
            v.tensor_copy(SM[:, 198:199], SM[:, 6:7]).then_inc(made("o_ready"), 1)
            dve.wait_ge(sem("o_ready"), so_far("o_ready"))
            residual(1)

            modulation(1)
            v.tensor_copy(SM[:, 198:199], SM[:, 6:7]).then_inc(made("ada_mod"), 1)
            dve.wait_ge(sem("ada_mod"), so_far("ada_mod"))
            v.tensor_copy(SM[:, 198:199], SM[:, 6:7]).then_inc(made("ada_mod"), 1)
            dve.wait_ge(sem("ada_mod"), so_far("ada_mod"))
            normed_x()
            modulated(HT, 3, 0, 0, "dve_chain")
            h16, x16 = (b.rearrange("p (g n) -> p g n", n=P) for b in (HTf, Of))
            v.tensor_tensor(x16[:, :, 1:P - 1], h16[:, :, 0:P - 2], h16[:, :, 2:P], ALU.add).then_inc(made("dve_chain"), 1)
            dve.wait_ge(sem("dve_chain"), so_far("dve_chain"))
            v.tensor_copy(x16[:, :, 0:1], h16[:, :, 1:2]).then_inc(made("dve_chain"), 1)
            dve.wait_ge(sem("dve_chain"), so_far("dve_chain"))
            v.tensor_copy(x16[:, :, P - 1:P], h16[:, :, P - 2:P - 1]).then_inc(made("dve_chain"), 1)
            dve.wait_ge(sem("dve_chain"), so_far("dve_chain"))
            v.scalar_tensor_tensor(Of, Of, 0.5, HTf, ALU.mult, ALU.subtract).then_inc(made("dve_chain"), 1)
            dve.wait_ge(sem("dve_chain"), so_far("dve_chain"))
            for n, m in enumerate((0, 2, 3, 1, 4, 5)):
                if n >= 2:
                    dve.wait_ge(sem("tile_used" if n < 5 else "proj_done"), N_ODD + 4 * (n - 1) if n < 5 else 1)
                for c in range(KC):
                    done = "xs" if c == KC - 1 else "dve_chain"
                    v.scalar_tensor_tensor(XS[n % 2][:, c, :], XX[:, c, :], PV[:, MU + m * KC + c:MU + m * KC + c + 1],
                                           HT[:, c, :], ALU.mult, ALU.add).then_inc(made(done), 1)
                    dve.wait_ge(sem(done), so_far(done))
            dve.wait_ge(sem("proj_copied"), 16 + 15 + 8 + 4)
            col = lambda o, c: PV[:, o + c:o + c + 1]
            for c in range(KC):
                v.tensor_scalar(NK[:, c, :], K[:, c, :], col(KK, c), None, ALU.mult).then_inc(made("dve_chain"), 1)
                dve.wait_ge(sem("dve_chain"), so_far("dve_chain"))
            v.tensor_tensor(W[8][:, :], W[2][:, :], W[2][:, :], ALU.mult).then_inc(made("kk2"), 1)
            dve.wait_ge(sem("kk2"), so_far("kk2"))
            for n in range(4):
                dve.wait_ge(sem("nrm_done"), n + 1)
                v.tensor_scalar(W[8][:, n * 512:(n + 1) * 512], bank[4 + n][:, :], 1e-12, None, ALU.add).then_inc(made("nrm"), 1)
                dve.wait_ge(sem("nrm"), so_far("nrm"))
            dve.wait_ge(sem("nrm_root"), 1)
            v.reciprocal(W[8][:, :], W[8][:, :]).then_inc(made("dve_chain"), 1)
            dve.wait_ge(sem("dve_chain"), so_far("dve_chain"))
            v.scalar_tensor_tensor(W[2][:, :], W[2][:, :], -1.0, W[8][:, :], ALU.mult, ALU.mult).then_inc(made("dve_chain"), 1)
            dve.wait_ge(sem("dve_chain"), so_far("dve_chain"))
            for c in range(KC):
                v.tensor_scalar(XS[1][:, c, :], B[:, c, :], 1.0, col(KA, c), ALU.subtract, ALU.mult).then_inc(made("dve_chain"), 1)
                dve.wait_ge(sem("dve_chain"), so_far("dve_chain"))
            v.scalar_tensor_tensor(W[1][:, :], W[9][:, :], 1.0, W[1][:, :], ALU.add, ALU.mult).then_inc(made("dve_chain"), 1)
            dve.wait_ge(sem("dve_chain"), so_far("dve_chain"))
            v.scalar_tensor_tensor(W[3][:, :], W[2][:, :], -1.0, W[3][:, :], ALU.mult, ALU.mult).then_inc(made("dve_chain"), 1)
            dve.wait_ge(sem("dve_chain"), so_far("dve_chain"))
            for c in range(KC):
                done = "rk" if c == KC - 1 else "dve_chain"
                v.scalar_tensor_tensor(XS[0][:, c, :], R[:, c, :], col(RK, c), K[:, c, :], ALU.mult, ALU.mult).then_inc(made(done), 1)
                dve.wait_ge(sem(done), so_far(done))
            dve.wait_ge(sem("bon_done"), 1)
            v.tensor_copy(SM[:, 160:192], bank[4][:, 0:32]).then_inc(made("dve_chain"), 1)
            dve.wait_ge(sem("dve_chain"), so_far("dve_chain"))
            v.memset(CS[:, :, :], 0.0).then_inc(made("dve_chain"), 1)
            dve.wait_ge(sem("dve_chain"), so_far("dve_chain"))
            v.memset(S0P[:, :, :], 0.0).then_inc(made("dve_chain"), 1)
            dve.wait_ge(sem("dve_chain"), so_far("dve_chain"))
            v.tensor_copy(SM[:, 198:199], SM[:, 6:7]).then_inc(made("rw_free"), 1)
            dve.wait_ge(sem("rw_free"), so_far("rw_free"))
            v.tensor_copy(SM[:, 198:199], SM[:, 6:7]).then_inc(made("rw_inputs"), 1)
            dve.wait_ge(sem("rw_inputs"), so_far("rw_inputs"))
            with dve.Fori(0, KC) as i, in_loop(i, KC, {"dve_chain": 20, "km": 1, "dec": 2, "s0p": 1, "m4": 8, "inv": 26, "sf": 2, "rw_free": 1}):
                for n in range(4):
                    d, st = n // 2, n % 2
                    src = SGM[d][:, :, :].rearrange("p c n -> p (c n)")[:, bass.ds(i * 256 + st * P, P)]
                    if d == 0:
                        v.tensor_tensor_scan(CS[:, n, 1:P + 1], ones, src, 0.0, ALU.mult, ALU.add).then_inc(made("dve_chain"), 1)
                        dve.wait_ge(sem("dve_chain"), so_far("dve_chain"))
                    else:
                        v.tensor_copy(E2[:, n, :], src).then_inc(made("dve_chain"), 1)
                        dve.wait_ge(sem("dve_chain"), so_far("dve_chain"))
                        v.tensor_tensor_scan(CS[:, n, 0:P][:, ::-1], ones, E2[:, n, :][:, ::-1], 0.0,
                                             ALU.mult, ALU.add).then_inc(made("dve_chain"), 1)
                        dve.wait_ge(sem("dve_chain"), so_far("dve_chain"))
                mid = CS[:, :, 64:65].rearrange("p a n -> p (a n)")
                v.tensor_scalar(SM[:, 100:104], mid, KAPPA, None, ALU.mult).then_inc(made("dve_chain"), 1)
                dve.wait_ge(sem("dve_chain"), so_far("dve_chain"))
                v.tensor_scalar(SM[:, 104:108], mid, -KAPPA, None, ALU.mult).then_inc(made("km"), 1)
                dve.wait_ge(sem("km"), so_far("km"))
                at = lambda b: b[:, bass.ds(i * 256, 256)].rearrange("p (s n) -> p s n", s=NST)
                r, k, nk, b = (at(W[n][:, :]) for n in range(4))
                for d in range(2):
                    dve.wait_ge(sem("ee"), i * 4 + (2 * d + 2))
                    dve.wait_ge(sem("e2"), i * 4 + (2 * d + 2))
                    ex, inc = (0, 1) if d == 0 else (1, 0)
                    pair = slice(2 * d, 2 * d + 2)
                    v.tensor_tensor(NQ[:, d, :, 0, :], nk, EE[:, pair, ex:ex + P], ALU.mult).then_inc(made("dve_chain"), 1)
                    dve.wait_ge(sem("dve_chain"), so_far("dve_chain"))
                    v.tensor_tensor(NQ[:, d, :, 1, :], r, EE[:, pair, inc:inc + P], ALU.mult).then_inc(made("dve_chain"), 1)
                    dve.wait_ge(sem("dve_chain"), so_far("dve_chain"))
                    v.tensor_tensor(BD[:, d, :, :], b, E2[:, pair, :], ALU.mult).then_inc(made("dve_chain"), 1)
                    dve.wait_ge(sem("dve_chain"), so_far("dve_chain"))
                    v.tensor_tensor(KDC[:, d, :, :], k, E2[:, pair, :], ALU.mult).then_inc(made("dec"), 1)
                    dve.wait_ge(sem("dec"), so_far("dec"))
                dve.wait_ge(sem("s0_t"), i + 1)
                dve.wait_ge(sem("em"), i + 1)
                for n in range(4):
                    d, hp = n // 2, slice(64 * (n % 2), 64 * (n % 2) + 64)
                    done = "s0p" if n == 3 else "dve_chain"
                    v.tensor_scalar(S0P[hp, d, hp], bank[7][hp, 256 + d * DH:256 + (d + 1) * DH],
                                    SM[hp, 109 + 2 * d:110 + 2 * d], None, ALU.mult).then_inc(made(done), 1)
                    dve.wait_ge(sem(done), so_far(done))
                for d in range(2):
                    tri = CST[:, C_TRI + d * 256:C_TRI + (d + 1) * 256].unsqueeze(1).to_broadcast([P, 2, 256])
                    for j in range(4):
                        dve.wait_ge(sem("t4"), i * 8 + (4 * d + j + 1))
                        v.tensor_tensor(M4[d][:, j, :, :].rearrange("p (a m) n -> p a (m n)", a=2),
                                        bank[4 * d + j][:, :].rearrange("p (a n) -> p a n", a=2), tri, ALU.mult).then_inc(made("m4"), 1)
                        dve.wait_ge(sem("m4"), so_far("m4"))
                for d in range(2):
                    v.tensor_copy(IP[d], ident.unsqueeze(1).to_broadcast([P, 4, P])).then_inc(made("dve_chain"), 1)
                    dve.wait_ge(sem("dve_chain"), so_far("dve_chain"))
                    v.tensor_copy(IX[d], ident.unsqueeze(1).to_broadcast([P, 4, P])).then_inc(made("dve_chain"), 1)
                    dve.wait_ge(sem("dve_chain"), so_far("dve_chain"))
                wide = lambda m: m.unsqueeze(1).to_broadcast([P, 4, P])
                four = lambda b: b[:, :].rearrange("p (j n) -> p j n", j=4)
                for d in range(2):
                    dve.sem_inc(sem("dve_settled"), 1)
                    v.copy_predicated(IP[d], wide(mask(0, d)), M4[d][:, :, 0, :]).then_inc(made("inv"), 1)
                    dve.wait_ge(sem("inv"), so_far("inv"))
                    dve.wait_ge(sem("nt"), i * 2 + (d + 1))
                    dve.sem_inc(sem("dve_settled"), 1)
                    v.copy_predicated(IX[d], wide(mask(0, 1 - d)), four(bank[4 * d])).then_inc(made("inv"), 1)
                    dve.wait_ge(sem("inv"), so_far("inv"))
                for lv in range(1, LEVELS):
                    for d in range(2):
                        if lv < LEVELS - 1:
                            dve.wait_ge(sem("dx"), i * 10 + (2 * (lv - 1) + d + 1))
                            dve.wait_ge(sem("dp"), i * 12 + (2 * (lv - 1) + d + 1))
                            dve.sem_inc(sem("dve_settled"), 1)
                            v.copy_predicated(IX[d], wide(mask(lv, 1 - d)), four(bank[4 * d + 1])).then_inc(made("inv"), 1)
                            dve.wait_ge(sem("inv"), so_far("inv"))
                        dve.wait_ge(sem("dp"), i * 12 + (2 * (lv - 1) + d + 1))
                        dve.sem_inc(sem("dve_settled"), 1)
                        v.copy_predicated(IP[d], wide(mask(lv, d)), four(bank[4 * d + 2])).then_inc(made("inv"), 1)
                        dve.wait_ge(sem("inv"), so_far("inv"))
                for d in range(2):
                    dve.wait_ge(sem("sf_done"), i * 2 + (d + 1))
                    last = EE[:, 2 * d, P:P + 1] if d == 0 else EE[:, 2 * d, 0:1]
                    v.tensor_scalar(SF[:, d, :], bank[4 * d + 2][:, 0:DH], last, None, ALU.mult).then_inc(made("sf"), 1)
                    dve.wait_ge(sem("sf"), so_far("sf"))
                dve.wait_ge(sem("so"), i * 2 + 2)
                v.tensor_copy(SM[:, 199:200], SM[:, 6:7]).then_inc(made("rw_free"), 1)
                dve.wait_ge(sem("rw_free"), so_far("rw_free"))
            y = W[0][:, :]
            h32 = lambda x: x.rearrange("p (g n) -> p g n", n=DH)
            stat = lambda s: s.unsqueeze(2).to_broadcast([P, 32, DH])
            dve.wait_ge(sem("y_copy"), KC)
            v.tensor_reduce(SM[:, 128:160], h32(y), AX.X, ALU.add).then_inc(made("dve_chain"), 1)
            dve.wait_ge(sem("dve_chain"), so_far("dve_chain"))
            v.tensor_scalar(SM[:, 128:160], SM[:, 128:160], 1.0 / DH, None, ALU.mult).then_inc(made("dve_chain"), 1)
            dve.wait_ge(sem("dve_chain"), so_far("dve_chain"))
            v.tensor_tensor(h32(y), h32(y), stat(SM[:, 128:160]), ALU.subtract).then_inc(made("dve_chain"), 1)
            dve.wait_ge(sem("dve_chain"), so_far("dve_chain"))
            v.tensor_tensor(W[2][:, :], y, y, ALU.mult).then_inc(made("dve_chain"), 1)
            dve.wait_ge(sem("dve_chain"), so_far("dve_chain"))
            v.tensor_reduce(SM[:, 128:160], h32(W[2][:, :]), AX.X, ALU.add).then_inc(made("dve_chain"), 1)
            dve.wait_ge(sem("dve_chain"), so_far("dve_chain"))
            v.tensor_scalar(SM[:, 128:160], SM[:, 128:160], 1.0 / DH, GN_EPS, ALU.mult, ALU.add).then_inc(made("gn_ms"), 1)
            dve.wait_ge(sem("gn_ms"), so_far("gn_ms"))
            dve.wait_ge(sem("gn_root"), 1)
            v.reciprocal(SM[:, 128:160], SM[:, 128:160]).then_inc(made("dve_chain"), 1)
            dve.wait_ge(sem("dve_chain"), so_far("dve_chain"))
            v.tensor_tensor(h32(y), h32(y), stat(SM[:, 128:160]), ALU.mult).then_inc(made("dve_chain"), 1)
            dve.wait_ge(sem("dve_chain"), so_far("dve_chain"))
            dve.wait_ge(sem("ln_in"), 32)
            dve.wait_ge(sem("proj_copied"), 16 + 15 + 8 + 4 + 4)
            byc = lambda x: x.rearrange("p (c n) -> p c n", c=KC)
            for st in range(NST):
                yst = Y1[:, :, st, :]
                v.tensor_tensor(yst, yst, byc(W[1][:, 0:1024]), ALU.mult).then_inc(made("dve_chain"), 1)
                dve.wait_ge(sem("dve_chain"), so_far("dve_chain"))
                v.tensor_tensor(yst, yst, byc(W[1][:, 1024:2048]), ALU.add).then_inc(made("dve_chain"), 1)
                dve.wait_ge(sem("dve_chain"), so_far("dve_chain"))
                v.tensor_tensor(h32(V1[:, st, :]), h32(V1[:, st, :]),
                                BON[:, st, :].unsqueeze(2).to_broadcast([P, HC, DH]), ALU.mult).then_inc(made("dve_chain"), 1)
                dve.wait_ge(sem("dve_chain"), so_far("dve_chain"))
                v.tensor_tensor(yst, yst, byc(V1[:, st, :]), ALU.add).then_inc(made("dve_chain"), 1)
                dve.wait_ge(sem("dve_chain"), so_far("dve_chain"))
                done = "yg" if st else "dve_chain"
                v.tensor_tensor(yst, yst, byc(G1[:, st, :]), ALU.mult).then_inc(made(done), 1)
                dve.wait_ge(sem(done), so_far(done))
            plain(XS[0], 4, "yt")
            residual(2)
            normed_x()
            modulated(HT, 5, 2, 3, "ht")

            dve.wait_ge(sem("logits"), 1)
            L = SM[:, 100:116]
            v.tensor_copy(L, bank[4][:, 0:16]).then_inc(made("lg"), 1)
            dve.wait_ge(sem("lg"), so_far("lg"))
            first = [SM[:, 116:132], SM[:, 132:148]]
            per8 = lambda x: x.rearrange("p (s n) -> p s n", s=NST)
            for r in range(2):
                top = SM[:, 56 + 2 * r:58 + 2 * r]
                v.tensor_reduce(top, per8(L), AX.X, ALU.max).then_inc(made("dve_chain"), 1)
                dve.wait_ge(sem("dve_chain"), so_far("dve_chain"))
                v.tensor_tensor(per8(first[r]), per8(L), top.unsqueeze(2).to_broadcast([P, NST, NE]), ALU.is_equal).then_inc(made("dve_chain"), 1)
                dve.wait_ge(sem("dve_chain"), so_far("dve_chain"))
                for st in range(NST):
                    f = first[r][:, st * NE:(st + 1) * NE]
                    v.tensor_tensor_scan(SM[:, 148:156], CST[:, C_ONE:C_ONE + 1].to_broadcast([P, NE]), f, 0.0, ALU.mult, ALU.add).then_inc(made("dve_chain"), 1)
                    dve.wait_ge(sem("dve_chain"), so_far("dve_chain"))
                    v.scalar_tensor_tensor(f, SM[:, 148:156], 1.0, f, ALU.is_equal, ALU.mult).then_inc(made("dve_chain"), 1)
                    dve.wait_ge(sem("dve_chain"), so_far("dve_chain"))
                if r == 0:
                    v.scalar_tensor_tensor(L, first[0], -3.0e38, L, ALU.mult, ALU.add).then_inc(made("dve_chain"), 1)
                    dve.wait_ge(sem("dve_chain"), so_far("dve_chain"))
            v.tensor_tensor(SM[:, 60:62], SM[:, 58:60], SM[:, 56:58], ALU.subtract).then_inc(made("lgd"), 1)
            dve.wait_ge(sem("lgd"), so_far("lgd"))
            dve.wait_ge(sem("lge"), 1)
            v.tensor_scalar(SM[:, 62:64], SM[:, 60:62], 1.0, None, ALU.add).then_inc(made("dve_chain"), 1)
            dve.wait_ge(sem("dve_chain"), so_far("dve_chain"))
            v.reciprocal(SM[:, 62:64], SM[:, 62:64]).then_inc(made("dve_chain"), 1)
            dve.wait_ge(sem("dve_chain"), so_far("dve_chain"))
            v.tensor_tensor(SM[:, 60:62], SM[:, 60:62], SM[:, 62:64], ALU.mult).then_inc(made("dve_chain"), 1)
            dve.wait_ge(sem("dve_chain"), so_far("dve_chain"))
            for st in range(NST):
                cut = slice(st * NE, (st + 1) * NE)
                v.tensor_scalar(GT[:, st, :], first[0][:, cut], SM[:, 62 + st:63 + st], None, ALU.mult).then_inc(made("dve_chain"), 1)
                dve.wait_ge(sem("dve_chain"), so_far("dve_chain"))
                v.scalar_tensor_tensor(GT[:, st, :], first[1][:, cut], SM[:, 60 + st:61 + st], GT[:, st, :],
                                       ALU.mult, ALU.add).then_inc(made("dve_chain"), 1)
                dve.wait_ge(sem("dve_chain"), so_far("dve_chain"))
            v.memset(Of, 0.0).then_inc(made("dve_chain"), 1)
            dve.wait_ge(sem("dve_chain"), so_far("dve_chain"))
            with dve.Fori(0, NE) as e, in_loop(e, NE, {"dve_chain": 4, "y_taken": 1}):
                hiddens(FT, i=e)
                dve.wait_ge(sem("tile_used"), e * 3 * FT + (N_MOE + 3 * FT))
                v.tensor_copy(SM[:, 192:194], GT[:, :, bass.ds(e, 1)].rearrange("p s a -> p (s a)")).then_inc(made("dve_chain"), 1)
                dve.wait_ge(sem("dve_chain"), so_far("dve_chain"))
                for n in range(4):
                    o = O[:, n // 2, (n % 2) * 512:(n % 2 + 1) * 512]
                    done = "y_taken" if n == 3 else "dve_chain"
                    v.scalar_tensor_tensor(o, bank[4 + n][:, :], SM[:, 192 + n // 2:193 + n // 2], o,
                                           ALU.mult, ALU.add).then_inc(made(done), 1)
                    dve.wait_ge(sem(done), so_far(done))
            v.tensor_copy(SM[:, 198:199], SM[:, 6:7]).then_inc(made("o_ready"), 1)
            dve.wait_ge(sem("o_ready"), so_far("o_ready"))
            residual(3)


_INS = ["x_prompt", "x_sample", "cache_ckv", "cache_krope", "state_hgrn", "state_rwkv", "c", "c_ctx", "ada_w", "ada_b",
        "norm_gains", "ev_w_in", "hgrn_norm", "mla_q_norm", "mla_w_q_up", "mla_kv_norm", "mla_w_kv_up", "ev_w_out",
        "rw_mu", "rw_w_r", "rw_w_k", "rw_w_v", "rw_w_o", "rw_w0", "rw_w1", "rw_w2", "rw_a0", "rw_a1", "rw_a2", "rw_g1",
        "rw_g2", "rw_k_k", "rw_k_a", "rw_r_k", "rw_ln_w", "rw_ln_b", "ffn_w_gate", "ffn_w_up", "ffn_w_down",
        "moe_router", "moe_w_gate", "moe_w_up", "moe_w_down"]
_OUTS = [("y_prompt", (1, 128, 1024)), ("y_sample", (1, 128, 1024)), ("new_ckv", (1, 1, 128, 128)),
         ("new_krope", (1, 1, 128, 32)), ("new_hgrn", (1, 1, 2, 8, 64, 64)), ("new_rwkv", (1, 1, 2, 16, 64, 64))]


def kernel(**inputs):
    import concourse.bacc as _bacc
    from concourse.bass_utils import run_bass_kernel_spmd as _run

    nc = _bacc.Bacc("TRN2", target_bir_lowering=False, num_devices=1)
    arrays = {name: np.ascontiguousarray(inputs[name]) for name in _INS}
    arrays["cst"], arrays["msk"] = constants()
    t = {name: nc.dram_tensor(f"in_{name}", a.shape, mybir.dt.from_np(a.dtype), kind="ExternalInput").ap()
         for name, a in arrays.items()}
    out = {name: nc.dram_tensor(f"out_{name}", shape, F32, kind="ExternalOutput").ap() for name, shape in _OUTS}
    program(nc, t, out)
    r = _run(nc, [{f"in_{name}": a for name, a in arrays.items()}], core_ids=[0])
    return tuple(r.results[0][f"out_{name}"] for name, _ in _OUTS)
```

```python
import math
from contextlib import ExitStack, contextmanager

import concourse.bass as bass
import numpy as np
from concourse import mybir

F32 = mybir.dt.float32
I32 = mybir.dt.int32
U8 = mybir.dt.uint8
ALU = mybir.AluOpType
ACT = mybir.ActivationFunctionType
AX = mybir.AxisListType

P = 128
D = 1024
KC = D // P
NST = 2
TW = 256
WARM_LEVEL, WARM_TAIL, WARM_HEAD = 5, 1, 6
RING = 11
FT = 2816 // TW
NE = 8
UNITS = NE + 3
HA, HC = 8, 16
DH = 64
EPS = 1e-6
GN_EPS = 64e-5
KAPPA = math.exp(-0.5)
SCALE = 96 ** -0.5
LEVELS = 7
GRID_W = 64

N_EVEN_OUT = 24 + 12 + 2
N_FFN = N_EVEN_OUT + 4
N_ADA1 = N_FFN + 3 * FT
N_ODD = N_ADA1 + 24
N_ODD_OUT = N_ODD + 12 + 5
N_MOE = N_ODD_OUT + 4 + 1


def up_used(j):
    return 2 if j == 0 else 3 * j + 1


def down_used(j):
    return 3 * j + 5 if j < FT - 1 else 3 * FT


ADAB, COND, GAIN, MU, W0, A0, KK, KA, RK, QN = 0, 96, 112, 176, 224, 240, 248, 256, 264, 272
NPV = 274
C_ID, C_TRI, C_BLK, C_COS, C_SIN, C_ONE = 0, 128, 640, 768, 800, 832
NCST = 833


def constants():
    c = np.zeros((P, NCST), np.float32)
    i = np.arange(P)
    row, col = i[:, None], i[None, :]
    c[:, C_ID:C_ID + P] = row == col
    c[:, C_ONE] = 1
    c[:, C_TRI:C_TRI + P] = row < col
    c[:, C_TRI + P:C_TRI + 2 * P] = row <= col
    c[:, C_TRI + 2 * P:C_TRI + 3 * P] = row > col
    c[:, C_TRI + 3 * P:C_TRI + 4 * P] = row >= col
    c[:, C_BLK:C_BLK + P] = row // DH == col // DH
    inv = (1.0 / (np.float32(10000.0) ** (np.arange(8, dtype=np.float32) / 8))).astype(np.float32)
    ar = (i // GRID_W).astype(np.float32)[:, None] * inv
    ac = (i % GRID_W).astype(np.float32)[:, None] * inv
    ang = np.concatenate([ar, ar, ac, ac], 1)
    sign = np.tile(np.repeat(np.array([-1.0, 1.0], np.float32), 8), 2)
    c[:, C_COS:C_COS + 32] = np.cos(ang)
    c[:, C_SIN:C_SIN + 32] = np.sin(ang) * sign
    m = np.zeros((P, 2 * LEVELS + 1, P), np.float32)
    for l in range(LEVELS):
        same = row >> (l + 1) == col >> (l + 1)
        m[:, 2 * l] = same & ((row >> l) % 2 == 0) & ((col >> l) % 2 == 1)
        m[:, 2 * l + 1] = same & ((row >> l) % 2 == 1) & ((col >> l) % 2 == 0)
    m[:, 2 * LEVELS] = row == col
    return c, m.reshape(P, -1)


def program(nc, t, out):
    ctx = ExitStack()
    with ctx:
        def sb(name, shape, dt=F32):
            return ctx.enter_context(nc.sbuf_tensor(name, shape, dt))

        sems = {}

        def sem(name):
            if name not in sems:
                sems[name] = ctx.enter_context(nc.semaphore(name))
            return sems[name]

        ring = sb("ring", [P, RING, KC * TW])
        X = sb("x", [P, NST, D])
        HT = sb("ht", [P, KC, NST * P])
        O = sb("o", [P, NST, D])
        GB = sb("gb", [P, NST, D])
        W = [sb(f"w{i}", [P, 2048]) for i in range(10)]
        CST = sb("cst", [P, NCST])
        MSK = sb("msk", [P, (2 * LEVELS + 1) * P], U8)
        PV = sb("pv", [P, NPV])
        MOD = sb("mod", [P, 6, KC, NST])
        AG = sb("ag", [P, 4, KC, NST])
        CT = sb("ct", [P, NST, KC])
        SM = sb("sm", [P, 200])
        bank = [ctx.enter_context(nc.psum_tensor(f"bank{i}", [P, 512], F32)) for i in range(8)]

        ident = CST[:, C_ID:C_ID + P]
        ones = CST[:, C_ONE:C_ONE + 1].to_broadcast([P, P])
        blk = CST[:, C_BLK:C_BLK + P]
        before = CST[:, C_TRI:C_TRI + P]

        def sided(x, level, side):
            w = 1 << level
            if len(x.shape) == 3:
                return x.rearrange("p j (n h s) -> p j n h s", h=2, s=w)[:, :, :, side, :]
            return x.rearrange("p (n h s) -> p n h s", h=2, s=w)[:, :, side, :]

        def sided4(b, level, side):
            return sided(b[:, :].rearrange("p (j n) -> p j n", j=4), level, side)

        def mask(level, side):
            n = 2 * level + side
            return MSK[:, n * P:(n + 1) * P]

        Q = W[0][:, 0:1024].rearrange("p (c n) -> p c n", c=4)
        V0 = W[0][:, 1024:2048].rearrange("p (s n) -> p s n", s=NST)
        FL = W[1][:, :].rearrange("p (d c n) -> p d c n", d=2, c=4)
        LF = W[2]
        BC = W[3]
        KG = W[4]
        EX = W[5]
        WQ = W[6]
        AT = [W[7], W[8]]
        GA = W[9][:, 0:1024].rearrange("p (s n) -> p s n", s=NST)
        CQ = W[9][:, 1024:1536].rearrange("p (s n) -> p s n", s=NST)
        CKV = W[9][:, 1536:1856].rearrange("p (s n) -> p s n", s=NST)
        HG = W[9][:, 1856:1920]
        KVG = W[9][:, 1920:2048]
        KR = GB[:, 0, 0:288].rearrange("p (t n) -> p t n", t=3)
        CC = GB[:, 0, 288:416]
        CKN = GB[:, 0, 416:672].rearrange("p (s n) -> p s n", s=NST)
        S0A = GB[:, 1, :].rearrange("p (d c v) -> p d c v", d=2, c=4)
        CQT = W[3][:, 1024:1536].rearrange("p (c n) -> p c n", c=2)
        OA = W[1][:, 0:1024].rearrange("p (s n) -> p s n", s=NST)
        SG = W[1][:, 1024:2048].rearrange("p (s n) -> p s n", s=NST)
        OM = O
        KD = W[2][:, 0:1024].rearrange("p (d c n) -> p d c n", d=2, c=4)
        SH = W[2][:, 1024:2048].rearrange("p (d c n) -> p d c n", d=2, c=4)
        CKT = W[3][:, 0:384]
        TQ = W[3][:, 384:384 + 768]
        QT = W[4][:, 0:1536].rearrange("p (s n) -> p s n", s=NST)
        PR = W[5][:, :].rearrange("p (b h n) -> p b h n", b=4, h=2)
        PT = W[6][:, :].rearrange("p (b n) -> p b n", b=4)
        KT = [W[7], W[8]]
        VM = W[0][:, 0:1536].rearrange("p (t n) -> p t n", t=3)
        MT = W[2][:, :].rearrange("p (c n) -> p c n", c=KC)

        def kt(h):
            return KT[h // 4][:, (h % 4) * 384:(h % 4 + 1) * 384]


        def MROWS(r):
            return W[1 + r // 4][0:NST, (r % 4) * 512:(r % 4 + 1) * 512]

        def fm(b):
            return b[:, :].rearrange("p (c n) -> p c n", c=KC)

        R, K, NK, B = (fm(W[i]) for i in range(4))
        SGM = [fm(W[4]), fm(W[5])]
        V1 = W[6][:, :].rearrange("p (s n) -> p s n", s=NST)
        G1 = W[7][:, :].rearrange("p (s n) -> p s n", s=NST)
        XS = [fm(W[8]), fm(W[9])]
        XX = O[:, :, :].rearrange("p s (c n) -> p (s c) n", n=NST * P)
        Of = O[:, :, :].rearrange("p s n -> p (s n)")
        GBf = GB[:, :, :].rearrange("p s n -> p (s n)")
        HTf = HT[:, :, :].rearrange("p c n -> p (c n)")
        Y1 = W[0][:, :].rearrange("p (c s n) -> p c s n", c=KC, s=NST)
        M4 = [W[9][:, :], Of]
        M4 = [m.rearrange("p (j m n) -> p j m n", j=4, m=4) for m in M4]
        PX = [HTf, GBf]
        IP, IX, IZ = ([b[:, k * 512:(k + 1) * 512].rearrange("p (j n) -> p j n", j=4) for b in PX] for k in range(3))
        GS, US = ([b[:, 512 + k * 256:768 + k * 256].rearrange("p (j n) -> p j n", j=4) for b in PX] for k in range(2))
        NQ = W[8][:, 0:1024].rearrange("p (d s m n) -> p d s m n", d=2, s=2, m=2)
        BD = W[8][:, 1024:1536].rearrange("p (d s n) -> p d s n", d=2, s=2)
        KDC = W[8][:, 1536:2048].rearrange("p (d s n) -> p d s n", d=2, s=2)
        CS = W[7][:, 0:516].rearrange("p (a n) -> p a n", a=4)
        EE = W[7][:, 516:1032].rearrange("p (a n) -> p a n", a=4)
        E2 = W[7][:, 1032:1544].rearrange("p (a n) -> p a n", a=4)
        TRK = W[7][:, 1032:1544].rearrange("p (d m n) -> p d m n", d=2, m=2)
        VS = W[7][:, 1544:1800].rearrange("p (s n) -> p s n", s=NST)
        S0P = HTf[:, 1792:2048].rearrange("p (d v) -> p d v", d=2)
        S0S = HTf[0:DH, 1536:1792].rearrange("p (d n) -> p d n", d=2)
        SO = HTf[DH:P, 1536:1792].rearrange("p (d n) -> p d n", d=2)
        SF = GBf[:, 1536:1664].rearrange("p (d v) -> p d v", d=2)
        BACK = GBf[:, 1920:2048]
        MG = GBf[:, 1664:1920]
        MW, MA = W[7][:, 0:256], W[7][:, 256:512]
        rows = [W[i][:, 1792:1920] for i in (7, 8, 6)]
        BON = SM[:, 160:192].rearrange("p (s h) -> p s h", s=NST)
        SIL = W[0][:, 0:1024].rearrange("p (b n) -> p b n", b=2)
        HID = W[0][:, 1024:2048].rearrange("p (b n) -> p b n", b=2)
        GT = sb("gt", [P, NST, NE])
        TBL = sb("tbl", [P, 16], I32)
        SILU = W[0][:, 0:512].rearrange("p (b n) -> p b n", b=2)
        HIDU = W[0][:, 512:1024].rearrange("p (b n) -> p b n", b=2)
        XG = W[1][:, 0:1024].rearrange("p (c n) -> p c n", c=KC)
        YG = W[1][:, 1024:2048]
        HTM = W[2][:, :].rearrange("p (s n) -> p s n", s=NST)
        ROUTE = W[3]
        CHOSEN, PLACE, TAKEN = ROUTE[:, 0:16], ROUTE[:, 16:32], ROUTE[:, 32:40]
        OVER, ORDER, PICK, TMP8 = (ROUTE[:, 40 + 8 * n:48 + 8 * n] for n in range(4))
        TBLF = ROUTE[:, 80:96]
        UNITV = ROUTE[:, 96:144].rearrange("p (a u) -> p a u", a=2 * NST)
        PLACEU, GTU = UNITV[:, 0:NST, :], UNITV[:, NST:2 * NST, :]
        PG, TMP32 = (ROUTE[:, 160 + 32 * n:192 + 32 * n].rearrange("p (a e) -> p a e", e=NE) for n in range(2))
        PLACE1, GT1 = ROUTE[:, 144:146], ROUTE[:, 146:148]
        IOTA = ROUTE[:, 256:384]
        SEL = ROUTE[:, 512:768].rearrange("p (s n) -> p s n", s=NST)
        SELT = ROUTE[:, 768:1024].rearrange("p (s n) -> p s n", s=NST)

        class Counts:

            def __init__(self):
                self.n, self.i, self.per, self.base = {}, None, {}, {}

            def made(self, name):
                self.n[name] = self.n.get(name, 0) + 1
                return sem(name)

            def so_far(self, name):
                if self.i is None:
                    return self.n.get(name, 0)
                return self.i * self.per[name] + (self.base.get(name, 0) + self.n.get(name, 0))

            @contextmanager
            def in_loop(self, i, n, per):
                self.base, self.n, self.per, self.i = self.n, {}, per, i
                yield
                got, self.n, self.i = self.n, dict(self.base), None
                assert got == per, got
                for name, k in got.items():
                    self.n[name] = self.base.get(name, 0) + n * k

        class Walk:
            def __init__(self):
                self.n, self.due = 0, [0] * RING

            def next(self, loads=1):
                s = self.n % RING
                self.n += 1
                self.due[s] += 16 * loads
                return s, self.due[s]

        kp = lambda ap: ap.rearrange("(k p) n -> p k n", p=P)

        block = ctx.enter_context(nc.Block())

        @block.sync
        def _(sp):
            walk = Walk()

            def tile(parts, i=None, per=0, dues=0):
                n = walk.n
                s, _ = walk.next(len(parts))
                if n >= RING or i is not None:
                    sp.wait_ge(sem("tile_used"), n - RING + 1 if i is None else i * per + (n - RING + 1))
                for dst, src in parts:
                    sp.dma_start(dst(ring[:, s, :]), src).then_inc(sem(f"slot{s}"), 16)

            def cols(w, a, n=TW):
                src = kp(w)[:, :, a if not isinstance(a, int) else slice(a, a + n)]
                return (lambda slot: slot[:, 0:KC * n].rearrange("p (k n) -> p k n", k=KC), src)

            def whole(a, n, src, parts=P):
                return (lambda slot: slot[0:parts, a:a + n], src)

            def ada(l):
                for n in range(24):
                    tile([cols(t["ada_w"][l], n * TW)])

            def down(w, j):
                src = w[j * TW:(j + 1) * TW, :].rearrange("(k p) n -> p k n", p=P)
                return (lambda slot: slot.rearrange("p (k n) -> p k n", k=2), src)

            def hidden(wg, wu, wd):
                for j in range(FT):
                    tile([cols(wg, j * TW)])
                    tile([cols(wu, j * TW)])
                    if j:
                        tile([down(wd, j - 1)])
                tile([down(wd, FT - 1)])

            ada(0)
            w = t["ev_w_in"][0]
            for n in range(11):
                tile([cols(w, n * TW)])
            tile([cols(w, 11 * TW, 160)])
            tile([(lambda s: s[:, 0:1536].rearrange("p (k n) -> p k n", k=2),
                   t["mla_w_q_up"][0].rearrange("(k p) n -> p k n", p=P))])
            tile([whole(0, 1024, t["mla_w_kv_up"][0])])
            for n in range(4):
                tile([cols(t["ev_w_out"][0], n * TW)])
            hidden(t["ffn_w_gate"][0], t["ffn_w_up"][0], t["ffn_w_down"][0])
            ada(1)
            for name in ("rw_w_r", "rw_w_k", "rw_w_v"):
                for n in range(4):
                    tile([cols(t[name][0], n * TW)])
            tile([(lambda s: s[:, 0:1024].rearrange("p (k n) -> p k n", k=KC)[:, :, 0:64], kp(t["rw_w1"][0, 0])),
                  (lambda s: s[:, 0:1024].rearrange("p (k n) -> p k n", k=KC)[:, :, 64:128], kp(t["rw_w1"][0, 1])),
                  (lambda s: s[:, 1024:1536].rearrange("p (k n) -> p k n", k=KC), kp(t["rw_a1"][0]))])
            tile([cols(t["rw_g1"][0], 0, 128)])
            tile([whole(0, 1024, t["rw_w2"][0].rearrange("d k n -> (d k) n"))])
            tile([whole(0, 1024, t["rw_a2"][0], 64)])
            tile([whole(0, 1024, t["rw_g2"][0])])
            for n in range(4):
                tile([cols(t["rw_w_o"][0], n * TW)])
            tile([(lambda s: s[:, 0:KC * NE].rearrange("p (k n) -> p k n", k=KC), kp(t["moe_router"][0]))])
            n0 = walk.n

            def expert_tiles(u, e):
                def expert(name):
                    return t[name][0][bass.ds(e, 1)].rearrange("a k n -> (a k) n")
                wg, wu, wd = expert("moe_w_gate"), expert("moe_w_up"), expert("moe_w_down")

                def etile(part):
                    tile([part], i=u, per=3 * FT)
                for j in range(FT):
                    etile(cols(wg, j * TW))
                    etile(cols(wu, j * TW))
                    if j:
                        etile(down(wd, j - 1))
                etile(down(wd, FT - 1))
                assert walk.n - n0 == 3 * FT

            with sp.Fori(0, NE - 1) as u:
                expert_tiles(u, u)
            walk.n = n0
            sp.wait_ge(sem("table"), 1)
            with sp.Fori(NE - 1, sp.value_load(TBL[0:1, UNITS:UNITS + 1], min_val=NE, max_val=UNITS)) as u:
                expert_tiles(u, sp.value_load(TBL[0:1, bass.ds(u, 1)], min_val=0, max_val=NE - 1))

        @block.gpsimd
        def _(pool):
            counts = Counts()
            made, so_far, in_loop = counts.made, counts.so_far, counts.in_loop
            g = nc.gpsimd

            def load(dst, src, ev):
                pool.dma_start(dst, src).then_inc(sem(ev), 16)

            pool.wait_ge(sem("msk_in"), 16)
            g.tensor_copy(MSK[:, :], W[5][:, 0:(2 * LEVELS + 1) * P]).then_inc(sem("msk_bytes"), 1)
            load(HG, t["hgrn_norm"][0].partition_broadcast(P), "gains_in")
            load(KVG, t["mla_kv_norm"][0].partition_broadcast(P), "gains_in")
            load(KR[:, 0, 64:96], t["cache_krope"][0, 0], "cache_in")
            load(CC, t["cache_ckv"][0, 0], "cache_in")
            g.memset(S0A[:, :, :, :], 0.0).then_inc(made("pool_chain"), 1)
            pool.wait_ge(sem("pool_chain"), so_far("pool_chain"))
            for d in range(2):
                states = t["state_hgrn"][0, 0, d].rearrange("(c h) k v -> h k c v", h=2)
                for h in range(2):
                    load(S0A[64 * h:64 * h + 64, d, :, 64 * h:64 * h + 64], states[h], "s0_in")
            g.memset(KR[:, 0, 0:64], 0.0).then_inc(sem("kr_zero"), 1)
            g.memset(KR[:, 1, 0:64], 0.0).then_inc(sem("kr_zero"), 1)
            g.memset(KR[:, 2, 0:64], 0.0).then_inc(sem("kr_zero"), 1)
            pool.wait_ge(sem("ckn"), 2)
            pool.dma_start(out["new_ckv"][0, 0], CKN[:, 0, :]).then_inc(sem("stored_latents"), 16)
            pool.dma_start(out["new_krope"][0, 0], CKV[:, 0, P:P + 32]).then_inc(sem("stored_latents"), 16)
            for d in range(2):
                pool.wait_ge(sem("sh_copied"), d + 1)
                for h in range(2):
                    dst = out["new_hgrn"][0, 0, d].rearrange("(c h) k v -> h k c v", h=2)[h]
                    pool.dma_start(dst, SH[64 * h:64 * h + 64, d, :, 64 * h:64 * h + 64]).then_inc(sem("stored_hgrn"), 16)
            pool.sem_inc(sem("stored_rwkv"), 32)
            pool.wait_ge(sem("rw_inputs"), 1)
            with pool.Fori(0, KC) as c:
                pool.wait_ge(sem("s0_t"), c + 1)
                pool.sem_inc(sem("pool_settled"), 1)
                for d in range(2):
                    pool.dma_start(S0S[:, d, :].rearrange("v (h k) -> v h k", h=2),
                                   t["state_rwkv"][0, 0, d].rearrange("(c h) v k -> c v h k", h=2)[bass.ds(c, 1)]
                                   .rearrange("a v h k -> (a v) h k")).then_inc(sem("s0s"), 16)
                pool.wait_ge(sem("rw_free"), c + 1)
                pool.sem_inc(sem("pool_settled"), 1)
                g.tensor_copy(VS[:, :, :], V1[:, :, bass.ds(c * P, P)]).then_inc(sem("vs"), 1)
            pool.wait_ge(sem("y_copy"), KC)
            load(W[1][:, 0:1024], t["rw_ln_w"][0].partition_broadcast(P), "ln_in")
            load(W[1][:, 1024:2048], t["rw_ln_b"][0].partition_broadcast(P), "ln_in")
            pool.wait_ge(sem("x_final"), 2)
            pool.dma_start(out["y_prompt"][0], X[:, 0, :]).then_inc(sem("stored_y"), 16)
            pool.dma_start(out["y_sample"][0], X[:, 1, :]).then_inc(sem("stored_y"), 16)
            pool.wait_ge(sem("stored_latents"), 32)
            pool.wait_ge(sem("stored_hgrn"), 64)
            pool.wait_ge(sem("stored_rwkv"), 32 * (KC + 1))
            pool.wait_ge(sem("stored_y"), 32)

        @block.tensor
        def _(pe):
            mm, tr = nc.tensor.matmul, nc.tensor.transpose
            walk = Walk()

            def arrived(loads=1, i=None, per=0):
                s, due = walk.next(loads)
                pe.wait_ge(sem(f"slot{s}"), due if i is None else i * per + due)
                return ring[:, s, :]

            proj = [0]

            def target():
                p = proj[0]
                proj[0] += 1
                if p >= 4:
                    pe.wait_ge(sem("proj_copied"), p - 3)
                return bank[p % 4]

            def products(src, w, feature_major, n=TW):
                b = target()
                for a in range(2):
                    for k in range(KC):
                        if feature_major:
                            ins = mm(b[:, a * TW:(a + 1) * TW], w[:, k, a * P:(a + 1) * P], src[:, k, :],
                                     start=k == 0, stop=k == KC - 1)
                        else:
                            ins = mm(b[:, a * TW:a * TW + n], src[:, k, a * P:(a + 1) * P], w[:, k, 0:n],
                                     start=k == 0, stop=k == KC - 1)
                ins.then_inc(sem("tile_used"), 1)

            def tile_product(src, feature_major, n=TW):
                w = arrived()[:, 0:KC * n].rearrange("p (k n) -> p k n", k=KC)
                products(src, w, feature_major, n)

            def keep_warm(b, n):
                for _ in range(n):
                    mm(b[:, 256:512], ident, CST[:, C_TRI:C_TRI + 256], start=True, stop=True)

            def free_slot():
                pe.drain().then_inc(sem("tile_used"), 1)

            def ada(l):
                def turn_rows(r):
                    pe.wait_ge(sem("ada_rows"), 12 * l + r + 1)
                    for c in range(4):
                        col = (4 * r + c) * 2
                        ins = tr(bank[7][:, col:col + 2], MROWS(r)[:, c * P:(c + 1) * P], ident[0:NST, 0:NST])
                    ins.then_inc(sem("ada_turned"), 1)

                for n in range(24):
                    r = n // 2
                    if n % 2 == 0 and r >= 3:
                        pe.wait_ge(sem("ada_rows"), 12 * l + r - 2)
                    w = arrived()[:, :].rearrange("p (k n) -> p k n", k=KC)
                    for k in range(KC):
                        ins = mm(bank[4 + r % 3][0:NST, (n % 2) * TW:(n % 2 + 1) * TW], CT[:, :, k], w[:, k, :],
                                 start=k == 0, stop=k == KC - 1)
                    ins.then_inc(sem("tile_used"), 1)
                    if n % 2 == 1 and r >= 1:
                        turn_rows(r - 1)
                turn_rows(11)

            def gates(n):
                pe.wait_ge(sem("ag"), n // 2 + 1)
                for st in range(NST):
                    for c in range(KC):
                        b = bank[4 + 2 * st + c // 4]
                        ins = mm(b[:, (c % 4) * P:(c % 4 + 1) * P],
                                 AG[:, n_gate(n), c, st:st + 1].to_broadcast([P, P]), ident, start=True, stop=True)
                        if c % 4 == 3:
                            ins.then_inc(sem("gb_done"), 1)

            def n_gate(n):
                return 1 + 2 * (n % 2)

            def turn(src, k):
                for st in range(NST):
                    for h in range(2):
                        for c in range(4):
                            ins = tr(bank[2 * st + h][:, c * P:(c + 1) * P], src(4 * h + c, st), ident)
                        ins.then_inc(sem("turned"), 1)

            def token_major(buf):
                return lambda c, st: buf[:, st, c * P:(c + 1) * P]

            pe.wait_ge(sem("rows_in"), 16 * 13)
            pe.wait_ge(sem("cst_in"), 16)
            tr(bank[4][:, 0:112], rows[0][0:112, :], ident[0:112, 0:112])
            tr(bank[4][:, 112:224], rows[1][0:112, :], ident[0:112, 0:112])
            tr(bank[4][:, 224:274], rows[2][0:50, :], ident[0:50, 0:50]).then_inc(sem("pv_done"), 1)
            pe.wait_ge(sem("ct"), 1)
            ada(0)

            pe.wait_ge(sem("xn"), 2)
            turn(token_major(O), 0)
            pe.wait_ge(sem("ht"), 1)
            for n in range(12):
                tile_product(HT, n < 6, TW if n < 11 else 160)

            pe.wait_ge(sem("kg"), 1)
            pe.wait_ge(sem("proj_copied"), 12)
            for lv in range(LEVELS + 1):
                keep_warm(bank[7], WARM_LEVEL)
                if lv:
                    pe.wait_ge(sem("wq"), lv)
                for g in range(8):
                    n = 8 * lv + g
                    if n >= 4:
                        pe.wait_ge(sem("at"), n - 3)
                    d, h, pair = g // 4, g // 2 % 2, g % 2
                    hp = slice(64 * h, 64 * h + 64)
                    for j in range(4):
                        seg = ((4 * d + 2 * pair) * 2 + j) * P
                        seg, qs = slice(seg, seg + P), slice(seg - d * 1024, seg - d * 1024 + P)
                        lhs, rhs = (WQ[hp, seg], WQ[hp, seg]) if lv else (KG[hp, seg], W[0][hp, qs])
                        ins = mm(bank[n % 4][:, j * P:(j + 1) * P], lhs, rhs, start=True, stop=True)
                    ins.then_inc(sem("at_done"), 1)
            pe.wait_ge(sem("at"), 8 * (LEVELS + 1))
            pe.wait_ge(sem("qe"), 2)
            pe.wait_ge(sem("s0_in"), 64)
            for st in range(NST):
                for hd in range(HA):
                    c, h = hd // 2, hd % 2
                    o = bank[4 + st][:, hd * DH:(hd + 1) * DH]
                    v = V0[:, st, hd * DH:(hd + 1) * DH]
                    for d in range(2):
                        n = (h * 4 + c) * 2 + st
                        ins = mm(o, AT[d][:, n * P:(n + 1) * P], v, start=hd == 0 and d == 0, stop=True,
                                 skip_group_check=True)
                if st == 1:
                    for c in range(4):
                        for d in range(2):
                            seg = ((d * 4 + c) * 2 + 1) * P
                            ins = mm(bank[5][:, c * P:(c + 1) * P], WQ[:, seg:seg + P], S0A[:, d, c, :],
                                     start=False, stop=True, skip_group_check=True)
                ins.then_inc(sem("oa_done"), 1)
            pe.wait_ge(sem("kdf"), 1)
            for d in range(2):
                for c in range(4):
                    seg = ((d * 4 + c) * 2) * P
                    ins = tr(bank[d][:, c * P:(c + 1) * P], EX[:, seg:seg + P], ident)
                ins.then_inc(sem("kd_done"), 1)
            for d in range(2):
                pe.wait_ge(sem("kd"), d + 1)
                for c in range(4):
                    ins = mm(bank[2 + d][:, c * P:(c + 1) * P], KD[:, d, c, :], V0[:, 0, c * P:(c + 1) * P],
                             start=True, stop=True)
                ins.then_inc(sem("sh_done"), 1)

            pe.wait_ge(sem("cqn"), 2)
            for st in range(NST):
                for c in range(2):
                    ins = tr(bank[6][:, (2 * c + st) * P:(2 * c + st + 1) * P], CQ[:, st, c * P:(c + 1) * P], ident)
            ins.then_inc(sem("latents_turned"), 1)
            pe.wait_ge(sem("ckn"), 2)
            pe.wait_ge(sem("cache_in"), 32)
            for n, src in enumerate((CC, CKN[:, 1, :], CKN[:, 0, :])):
                ins = tr(bank[7][:, n * P:(n + 1) * P], src, ident)
            ins.then_inc(sem("latents_turned"), 1)
            pe.wait_ge(sem("kr_zero"), 3)
            pe.wait_ge(sem("kr"), 2)
            pe.wait_ge(sem("kd"), 2)
            for n in range(3):
                ins = tr(bank[0][0:96, n * P:(n + 1) * P], KR[:, n, :], ident)
            ins.then_inc(sem("latents_turned"), 1)
            w = arrived()[:, 0:1536].rearrange("p (k n) -> p k n", k=2)
            pe.wait_ge(sem("cqt"), 1)
            pe.wait_ge(sem("sh_copied"), 2)
            for st in range(NST):
                for half in range(2):
                    b = bank[(1, 2, 3, 6)[2 * st + half]]
                    for k in range(2):
                        ins = mm(b[:, 0:384], CQT[:, k, st * P:(st + 1) * P], w[:, k, half * 384:(half + 1) * 384],
                                 start=k == 0, stop=k == 1)
                    ins.then_inc(sem("qt_done"), 1)
            free_slot()
            w = arrived()[:, 0:1024].rearrange("p (h m n) -> p h m n", h=HA, m=2)
            pe.wait_ge(sem("ckt"), 1)
            for hd in range(HA):
                b = bank[(7, 0)[hd % 2]]
                if hd == 1:
                    pe.wait_ge(sem("krt"), 1)
                if hd >= 2:
                    pe.wait_ge(sem("kt"), hd - 1)
                mm(b[0:64, 0:384], w[:, hd, 0, :], CKT, start=True, stop=True).then_inc(sem("kt_done"), 1)
            pe.wait_ge(sem("qt"), 4)
            for n in range(3):
                mm(bank[1 + n][:, :], CKT[:, n * P:(n + 1) * P], w[:, :, 1, :], start=True, stop=True).then_inc(sem("vm_done"), 1)
            free_slot()
            pe.wait_ge(sem("qrope"), 1)
            pe.wait_ge(sem("kt"), HA)
            pe.wait_ge(sem("vm"), 3)
            for n in range(4):
                for j in range(4):
                    hd, st = 2 * n + j // 2, j % 2
                    ins = tr(bank[n][0:96, j * P:(j + 1) * P], QT[:, st, hd * 96:(hd + 1) * 96], ident)
                ins.then_inc(sem("qtt_done"), 1)
            pe.wait_ge(sem("oa_copied"), 2)

            def scores(u):
                st, hp = u // 4, u % 4
                nk, k0 = (P, 256) if st == 0 else (256, 0)
                if u >= 2:
                    pe.wait_ge(sem("prob"), 2 * (u - 1))
                else:
                    pe.wait_ge(sem("qtt"), 4)
                for a in range(2):
                    hd = 2 * hp + a
                    ins = mm(bank[u % 2][:, a * 256:a * 256 + nk], HT[0:96, hd, st * P:(st + 1) * P],
                             kt(hd)[0:96, k0:k0 + nk], start=True, stop=True)
                ins.then_inc(sem("sc_done"), 1)
                keep_warm(bank[7], 2)

            def weigh(u):
                st, hp = u // 4, u % 4
                nt = 1 if st == 0 else 2
                pe.wait_ge(sem("prob"), 2 * (u + 1))
                if u >= 2:
                    pe.wait_ge(sem("pt"), u - 1)
                for a in range(2):
                    for k in range(nt):
                        ins = tr(bank[2 + u % 2][:, (2 * a + k) * P:(2 * a + k + 1) * P],
                                 PR[:, u % 4, a, k * P:(k + 1) * P], ident)
                ins.then_inc(sem("pt_done"), 1)
                pe.wait_ge(sem("pt"), u + 1)
                for a in range(2):
                    hd = 2 * hp + a
                    for k in range(nt):
                        ins = mm(bank[4 + st][:, hd * DH:(hd + 1) * DH], PT[:, u % 4, (2 * a + k) * P:(2 * a + k + 1) * P],
                                 VM[:, 2 if st == 0 else k, hd * DH:(hd + 1) * DH], start=k == 0, stop=k == nt - 1)
                ins.then_inc(sem("pv_att"), 1)

            scores(0)
            for u in range(8):
                if u + 1 < 8:
                    scores(u + 1)
                weigh(u)
            pe.wait_ge(sem("om"), 2)
            turn(token_major(OM), 1)
            gates(0)
            pe.wait_ge(sem("mt"), 1)
            for n in range(4):
                tile_product(MT, False)

            def hidden():

                def gate_up(j):
                    if j >= 2:
                        pe.wait_ge(sem("hid"), j - 1)
                    for which in range(2):
                        w = arrived()[:, :].rearrange("p (k n) -> p k n", k=KC)
                        b = bank[2 * (j % 2) + which]
                        for a in range(2):
                            for k in range(KC):
                                ins = mm(b[:, a * TW:(a + 1) * TW], w[:, k, a * P:(a + 1) * P], HT[:, k, :],
                                         start=k == 0, stop=k == KC - 1)
                        ins.then_inc(sem("tile_used"), 1)

                def down(j):
                    w = arrived()[:, :].rearrange("p (k n) -> p k n", k=2)
                    pe.wait_ge(sem("hid"), j + 1)
                    for st in range(NST):
                        for h in range(2):
                            for k in range(2):
                                ins = mm(bank[4 + 2 * st + h][:, :], HID[:, j % 2, k * TW + st * P:k * TW + (st + 1) * P],
                                         w[:, k, h * 512:(h + 1) * 512], start=j == 0 and k == 0,
                                         stop=j == FT - 1 and k == 1)
                    ins.then_inc(sem("tile_used"), 1)

                gate_up(0)
                for j in range(1, FT):
                    gate_up(j)
                    down(j - 1)
                down(FT - 1)

            pe.wait_ge(sem("xn"), 4)
            turn(token_major(O), 2)
            pe.wait_ge(sem("ht"), 2)
            gates(1)
            pe.wait_ge(sem("gb_copied"), 8)
            hidden()

            pe.wait_ge(sem("y_taken"), 1)
            ada(1)
            pe.wait_ge(sem("xn"), 6)
            turn(token_major(O), 3)
            for n in range(12):
                if n % 4 == 0:
                    pe.wait_ge(sem("xs"), n // 4 + 1)
                tile_product(XS[(n // 4) % 2], n < 8)
            s = arrived(3)
            w1 = s[:, 0:1024].rearrange("p (k n) -> p k n", k=KC)
            a1 = s[:, 1024:1536].rearrange("p (k n) -> p k n", k=KC)
            pe.wait_ge(sem("xs"), 4)
            b = target()
            for k in range(KC):
                ins = mm(b[:, 0:TW], w1[:, k, :], XS[1][:, k, :], start=k == 0, stop=k == KC - 1)
            ins.then_inc(sem("proj_done"), 1)
            pe.wait_ge(sem("xs"), 5)
            b = target()
            for k in range(KC):
                ins = mm(b[0:64, 0:TW], a1[:, k, :], XS[0][:, k, :], start=k == 0, stop=k == KC - 1)
            ins.then_inc(sem("proj_done"), 1)
            free_slot()
            s = arrived()[:, 0:1024].rearrange("p (k n) -> p k n", k=KC)
            pe.wait_ge(sem("xs"), 6)
            b = target()
            for k in range(KC):
                ins = mm(b[:, 0:TW], s[:, k, :], XS[1][:, k, :], start=k == 0, stop=k == KC - 1)
            ins.then_inc(sem("proj_done"), 1)
            free_slot()
            pe.wait_ge(sem("kk2"), 1)
            pe.wait_ge(sem("ag"), 2)
            for n in range(4):
                mm(bank[4 + n][:, :], blk, Of[:, n * 512:(n + 1) * 512], start=True, stop=True).then_inc(sem("nrm_done"), 1)
            s = arrived()
            pe.wait_ge(sem("proj_copied"), proj[0])
            for d in range(2):
                hp = slice(64 * d, 64 * d + 64)
                for c in range(0, KC, 2):
                    b = target()
                    for a in range(2):
                        ins = mm(b[:, a * TW:(a + 1) * TW], s[hp, (c + a) * P:(c + a + 1) * P], MW[hp, :],
                                 start=True, stop=True)
                    ins.then_inc(sem("proj_done"), 1)
            free_slot()
            s = arrived()
            for c in range(0, KC, 2):
                b = target()
                for a in range(2):
                    ins = mm(b[:, a * TW:(a + 1) * TW], s[0:64, (c + a) * P:(c + a + 1) * P], MA[0:64, :],
                             start=True, stop=True)
                ins.then_inc(sem("proj_done"), 1)
            free_slot()
            pe.wait_ge(sem("rk"), 1)
            pe.wait_ge(sem("nrm"), 4)
            for st in range(NST):
                for c in range(KC):
                    ins = mm(bank[4][:, st * HC + 2 * c:st * HC + 2 * c + 2], XS[0][:, c, st * P:(st + 1) * P],
                             blk[:, 0:P:DH], start=True, stop=True)
            ins.then_inc(sem("bon_done"), 1)
            pe.wait_ge(sem("rw_inputs"), 1)
            pe.sem_inc(sem("s0_t"), 1)

            with pe.Fori(0, KC) as i:
                pe.wait_ge(sem("s0s"), i * 32 + 32)
                pe.sem_inc(sem("pe_settled"), 1)
                for d in range(2):
                    ins = tr(bank[7][:, 256 + d * DH:256 + (d + 1) * DH], S0S[:, d, :], ident[0:64, 0:64])
                ins.then_inc(sem("s0_t"), 1)
                keep_warm(bank[0], WARM_HEAD)
                for d in range(2):
                    pe.wait_ge(sem("dec"), i * 2 + (d + 1))
                    if d == 0:
                        pe.wait_ge(sem("so"), i * 2 + 2)
                    else:
                        pe.wait_ge(sem("s0p"), i + 1)
                    for j in range(4):
                        st, h = j // 2, j % 2
                        hp = slice(64 * h, 64 * h + 64)
                        b = bank[4 * d + j]
                        mm(b[:, 0:256], BD[hp, d, st, :], NQ[hp, d, st, :, :], start=True, stop=True)
                        mm(b[:, 256:512], KDC[hp, d, st, :], NQ[hp, d, st, :, :], start=True, stop=True).then_inc(sem("t4"), 1)
                for d in range(2):
                    pe.wait_ge(sem("m4"), i * 8 + (4 * d + 4))
                    pe.sem_inc(sem("pe_settled"), 1)
                    for j in range(4):
                        ins = tr(bank[4 * d][:, j * P:(j + 1) * P], M4[d][:, j, 0, :], ident)
                    ins.then_inc(sem("nt"), 1)
                keep_warm(bank[3], WARM_TAIL)
                for lv in range(1, LEVELS):
                    for d in range(2):
                        pe.wait_ge(sem("inv"), i * 26 + (4 * (lv - 1) + 2 * d + 2))
                        for j in range(4):
                            ins = mm(bank[4 * d][:, j * P:(j + 1) * P], M4[d][:, j, 0, :], IX[d][:, j, :],
                                     start=True, stop=True)
                        ins.then_inc(sem("z"), 1)
                    for d in range(2):
                        pe.wait_ge(sem("zc"), i * 12 + (2 * (lv - 1) + d + 1))
                        if lv < LEVELS - 1:
                            for j in range(4):
                                ins = mm(bank[4 * d + 1][:, j * P:(j + 1) * P], IP[d][:, j, :], IZ[d][:, j, :],
                                         start=True, stop=True)
                            ins.then_inc(sem("dx"), 1)
                        for j in range(4):
                            ins = mm(bank[4 * d + 2][:, j * P:(j + 1) * P], IZ[d][:, j, :], IP[d][:, j, :],
                                     start=True, stop=True)
                        ins.then_inc(sem("dp"), 1)
                pe.wait_ge(sem("vs"), i + 1)
                for d in range(2):
                    for j in range(4):
                        st, h = j // 2, j % 2
                        mm(bank[4 * d + 3][:, j * DH:(j + 1) * DH], M4[d][:, j, 2, :], VS[:, st, 64 * h:64 * h + 64],
                           start=j == 0, stop=True, skip_group_check=True)
                    mm(bank[4 * d + 3][:, 2 * DH:4 * DH], NQ[:, d, 1, 0, :], S0P[:, d, :],
                       start=False, stop=True, skip_group_check=True).then_inc(sem("g"), 1)
                keep_warm(bank[5], WARM_TAIL)
                for d in range(2):
                    pe.wait_ge(sem("gs"), i * 2 + (d + 1))
                    pe.wait_ge(sem("inv"), i * 26 + (25 + d))
                    for j in range(4):
                        ins = mm(bank[4 * d][:, j * DH:(j + 1) * DH], IP[d][:, j, :], GS[d][:, j, :], start=True, stop=True)
                    ins.then_inc(sem("u"), 1)
                keep_warm(bank[5], WARM_TAIL)
                pe.wait_ge(sem("us"), i * 2 + 2)
                for d in range(2):
                    for j in range(4):
                        st, h = j // 2, j % 2
                        o = bank[3][:, j * DH:(j + 1) * DH]
                        mm(o, M4[d][:, j, 1, :], US[d][:, j, :], start=d == 0 and j == 0, stop=True, skip_group_check=True)
                        mm(o, M4[d][:, j, 3, :], VS[:, st, 64 * h:64 * h + 64], start=False, stop=True,
                           skip_group_check=True)
                    ins = mm(bank[3][:, 2 * DH:4 * DH], NQ[:, d, 1, 1, :], S0P[:, d, :], start=False, stop=True,
                             skip_group_check=True)
                ins.then_inc(sem("y"), 1)
                for d in range(2):
                    tr(bank[4 * d + 1][:, 0:P], BD[:, d, 0, :], ident)
                    tr(bank[4 * d + 1][:, P:2 * P], KDC[:, d, 0, :], ident).then_inc(sem("trk_done"), 1)
                keep_warm(bank[0], WARM_TAIL)
                for d in range(2):
                    pe.wait_ge(sem("trk"), i * 2 + (d + 1))
                    for h in range(2):
                        o = bank[4 * d + 2][64 * h:64 * h + 64, 0:DH]
                        mm(o, TRK[:, d, 0, 64 * h:64 * h + 64], US[d][:, h, :], start=True, stop=False)
                        ins = mm(o, TRK[:, d, 1, 64 * h:64 * h + 64], VS[:, 0, 64 * h:64 * h + 64], start=False, stop=True)
                    ins.then_inc(sem("sf_done"), 1)
                keep_warm(bank[0], WARM_TAIL)
                for d in range(2):
                    pe.wait_ge(sem("sf"), i * 2 + (d + 1))
                    pe.sem_inc(sem("pe_settled"), 1)
                    tr(bank[4 * d + 1][0:64, 256:256 + P], SF[:, d, :], ident).then_inc(sem("so_done"), 1)
            pe.wait_ge(sem("so"), 2 * KC + 2)
            s = arrived()
            for st in range(NST):
                for h in range(2):
                    b = target()
                    mm(b[:, :], MG[:, st * P:(st + 1) * P], s[:, h * 512:(h + 1) * 512],
                       start=True, stop=True).then_inc(sem("proj_done"), 1)
            free_slot()
            pe.wait_ge(sem("proj_copied"), 16 + 15 + 8 + 4 + 4)
            pe.wait_ge(sem("yg"), 1)
            turn(lambda c, st: Y1[:, c, st, :], 4)
            pe.wait_ge(sem("yt"), 1)
            for n in range(4):
                tile_product(XS[0], False)
            gates(2)
            pe.wait_ge(sem("xn"), 8)
            turn(token_major(O), 5)
            pe.wait_ge(sem("ht"), 3)
            w = arrived()[:, 0:KC * NE].rearrange("p (k n) -> p k n", k=KC)
            pe.wait_ge(sem("gb_copied"), 12)
            for st in range(NST):
                for k in range(KC):
                    ins = mm(bank[4][:, st * NE:(st + 1) * NE], HT[:, k, st * P:(st + 1) * P], w[:, k, :],
                             start=k == 0, stop=k == KC - 1)
            ins.then_inc(sem("logits"), 1)
            free_slot()
            for st in range(NST):
                for h in range(2):
                    for c in range(4):
                        ins = tr(bank[2 * st + h][:, c * P:(c + 1) * P], HT[:, 4 * h + c, st * P:(st + 1) * P], ident)
                    ins.then_inc(sem("htm_done"), 1)
            pe.wait_ge(sem("lg"), 1)
            gates(3)
            pe.wait_ge(sem("chosen"), 1)
            pe.wait_ge(sem("htm"), 4)
            mm(bank[0][:, 0:NE], before, CHOSEN[:, 0:NE], start=True, stop=True)
            mm(bank[0][:, NE:2 * NE], before, CHOSEN[:, NE:2 * NE], start=True, stop=False)
            mm(bank[0][:, NE:2 * NE], ones, CHOSEN[:, 0:NE], start=False, stop=True)
            for st in range(NST):
                mm(bank[0][:, 2 * NE:3 * NE], ones, CHOSEN[:, st * NE:(st + 1) * NE], start=st == 0, stop=st == 1)
            mm(bank[1][:, 0:P], ones, before, start=True, stop=True).then_inc(sem("placed"), 1)
            pe.wait_ge(sem("gb_copied"), 16)

            def gather():
                for c in range(KC):
                    for st in range(NST):
                        ins = mm(bank[2 + c // 4][:, (c % 4) * P:(c % 4 + 1) * P], HTM[:, st, c * P:(c + 1) * P],
                                 SEL[:, st, :], start=st == 0, stop=st == 1)
                    if c % 4 == 3:
                        ins.then_inc(sem("gathered"), 1)

            pe.wait_ge(sem("sel"), 1)
            gather()
            pe.wait_ge(sem("table"), 1)
            with pe.Fori(0, pe.value_load(TBL[0:1, UNITS:UNITS + 1], min_val=NE, max_val=UNITS)) as u:
                def gate_up(j):
                    pe.wait_ge(sem("hid"), u * FT + (FT + j - 1 if j else FT))
                    for which in range(2):
                        w = arrived(i=u, per=48)[:, :].rearrange("p (k n) -> p k n", k=KC)
                        for a in range(2):
                            n = 2 * which + a
                            for k in range(KC):
                                ins = mm(bank[j % 2][:, n * P:(n + 1) * P], w[:, k, a * P:(a + 1) * P], XG[:, k, :],
                                         start=k == 0, stop=k == KC - 1)
                        ins.then_inc(sem("tile_used"), 1)

                def down(j):
                    w = arrived(i=u, per=48)[:, :].rearrange("p (k n) -> p k n", k=2)
                    pe.wait_ge(sem("hid"), u * FT + (FT + j + 1))
                    if j == 0:
                        pe.wait_ge(sem("y_taken"), u + 1)
                    for h in range(2):
                        for k in range(2):
                            ins = mm(bank[4 + h][:, :], HIDU[:, j % 2, k * P:(k + 1) * P], w[:, k, h * 512:(h + 1) * 512],
                                     start=j == 0 and k == 0, stop=j == FT - 1 and k == 1)
                    ins.then_inc(sem("tile_used"), 1)

                pe.wait_ge(sem("xg"), u * 2 + 2)
                gate_up(0)
                for j in range(1, FT):
                    gate_up(j)
                    down(j - 1)
                    if j == 2:
                        for st in range(NST):
                            ins = tr(bank[6][:, st * P:(st + 1) * P], SEL[:, st, :], ident)
                        ins.then_inc(sem("selt_done"), 1)
                down(FT - 1)
                pe.wait_ge(sem("sel"), u + 2)
                gather()
                pe.wait_ge(sem("selt"), u + 1)
                pe.wait_ge(sem("unit_out"), u * 2 + 2)
                for st in range(NST):
                    for h in range(2):
                        mm(bank[(6, 4)[st] + h][:, :], SELT[:, st, :], YG[:, h * 512:(h + 1) * 512],
                           start=True, stop=True).then_inc(sem("scattered"), 1)

        @block.scalar
        def _(act):
            counts = Counts()
            made, so_far, in_loop = counts.made, counts.so_far, counts.in_loop
            A = nc.scalar.activation
            sq = [0]

            def load(dst, src, ev):
                act.dma_start(dst, src).then_inc(sem(ev), 16)

            load(CST[:, :], t["cst"], "cst_in")
            r8 = lambda ap: ap.rearrange("(k p) -> k p", p=P)
            load(rows[0][0:96, :], t["ada_b"].rearrange("l (k p) -> (l k) p", p=P), "rows_in")
            load(rows[0][96:104, :], r8(t["c_ctx"]), "rows_in")
            load(rows[0][104:112, :], t["c"].rearrange("a (k p) -> (a k) p", p=P), "rows_in")
            load(rows[1][0:64, :], t["norm_gains"].rearrange("l g (k p) -> (l g k) p", p=P), "rows_in")
            load(rows[1][64:112, :], t["rw_mu"][0].rearrange("g (k p) -> (g k) p", p=P), "rows_in")
            load(rows[2][0:16, :], t["rw_w0"][0].rearrange("g (k p) -> (g k) p", p=P), "rows_in")
            for n, name in enumerate(("rw_a0", "rw_k_k", "rw_k_a", "rw_r_k")):
                load(rows[2][16 + 8 * n:24 + 8 * n, :], r8(t[name][0]), "rows_in")
            load(rows[2][48:50, :], r8(t["mla_q_norm"][0]), "rows_in")
            load(X[:, 0, :], t["x_prompt"][0], "rows_in")
            load(X[:, 1, :], t["x_sample"][0], "rows_in")
            load(W[5][:, 0:(2 * LEVELS + 1) * P], t["msk"], "msk_in")
            act.wait_ge(sem("rows_in"), 16 * 13)
            act.wait_ge(sem("pv"), 1)
            A(CT[:, :, :].rearrange("p s k -> p (s k)"), PV[:, COND:COND + 16], ACT.Silu).then_inc(sem("ct"), 1)

            def rstd(src, junk, n, ready):
                ready()
                for st in range(NST):
                    A(junk(st), src(st), ACT.Square, accum_out=SM[:, st:st + 1]).then_inc(sem("sumsq"), 1)
                sq[0] += 1
                act.wait_ge(sem("meansq"), sq[0])
                A(SM[:, 4:6], SM[:, 2:4], ACT.Sqrt).then_inc(sem("root"), 1)

            def norm_x(ready=lambda: None):
                rstd(lambda st: X[:, st, :], lambda st: O[:, st, :], D, ready)

            def norm_o(ready):
                rstd(lambda st: O[:, st, :], lambda st: W[9][:, st * D:(st + 1) * D], D, ready)

            def copy_gates(n):
                for k in range(4):
                    act.wait_ge(sem("gb_done"), 4 * n + k + 1)
                    A(GB[:, k // 2, (k % 2) * 512:(k % 2 + 1) * 512], bank[4 + k][:, :], ACT.Copy).then_inc(sem("gb_copied"), 1)

            proj = [0]

            low = [0]

            def filled(tile):
                if tile is None:
                    low[0] += 1
                    act.wait_ge(sem("proj_done"), low[0])
                else:
                    act.wait_ge(sem("tile_used"), tile + 1)

            def take(dst, tile, func=ACT.Copy, n=512, src=None, **kw):
                p = proj[0]
                proj[0] += 1
                filled(tile)
                b = bank[p % 4]
                A(dst, b[:, 0:n] if src is None else src(b), func, **kw).then_inc(sem("proj_copied"), 1)

            halves = lambda b: b[:, :].rearrange("p (s n) -> p s n", s=NST)

            def ada_rows(l):
                for r in range(12):
                    act.wait_ge(sem("tile_used"), (N_ADA1 if l else 0) + 2 * r + 2)
                    A(MROWS(r), bank[4 + r % 3][0:NST, :], ACT.Copy).then_inc(sem("ada_rows"), 1)

            norm_x()
            ada_rows(0)
            for n in range(12):
                if n < 2:
                    take(W[0][:, n * 512:(n + 1) * 512], 24 + n)
                elif n < 6:
                    take(W[1][:, (n - 2) * 512:(n - 1) * 512], 24 + n)
                elif n < 8:
                    take(V0[:, :, (n - 6) * TW:(n - 5) * TW], 24 + n, src=halves)
                elif n < 10:
                    take(GA[:, :, (n - 8) * TW:(n - 7) * TW], 24 + n, src=halves)
                elif n == 10:
                    take(CQ[:, :, :], 24 + n, src=halves)
                else:
                    take(CKV[:, :, :], 24 + n, src=lambda b: halves(b)[:, :, 0:160])
            act.wait_ge(sem("absf"), 1)
            A(EX[:, :], EX[:, :], ACT.Exp, scale=-1.0).then_inc(made("act_chain"), 1)
            act.wait_ge(sem("act_chain"), so_far("act_chain"))
            A(EX[:, :], EX[:, :], ACT.Ln, bias=1.0).then_inc(sem("ln"), 1)
            act.wait_ge(sem("lfx"), 1)
            A(KG[:, :], EX[:, :], ACT.Exp).then_inc(sem("kg"), 1)
            for lv in range(LEVELS):
                act.wait_ge(sem("diff"), lv + 1)
                A(EX[:, :], EX[:, :], ACT.Exp).then_inc(sem("ex"), 1)
            act.wait_ge(sem("wq"), LEVELS)
            A(EX[:, :], BC[:, :], ACT.Exp).then_inc(sem("ex"), 1)
            act.wait_ge(sem("diff"), LEVELS + 1)
            A(EX[:, :], EX[:, :], ACT.Exp).then_inc(sem("ex"), 1)
            act.wait_ge(sem("proj_copied"), 12)
            act.wait_ge(sem("kdf"), 1)
            for st in range(NST):
                A(W[4][:, 1536:1792], CQ[:, st, :], ACT.Square, accum_out=SM[:, 8 + st:9 + st]).then_inc(made("lat_sq"), 1)
                act.wait_ge(sem("lat_sq"), so_far("lat_sq"))
                A(W[4][:, 1792:1920], CKV[:, st, 0:P], ACT.Square, accum_out=SM[:, 10 + st:11 + st]).then_inc(made("lat_sq"), 1)
                act.wait_ge(sem("lat_sq"), so_far("lat_sq"))
            act.wait_ge(sem("var"), 1)
            A(SM[:, 8:12], SM[:, 8:12], ACT.Sqrt).then_inc(sem("var_root"), 1)
            for d in range(2):
                act.wait_ge(sem("kd_done"), d + 1)
                A(KD[:, d, :, :].rearrange("p c n -> p (c n)"), bank[d][:, :], ACT.Copy).then_inc(sem("kd"), 1)
            for d in range(2):
                act.wait_ge(sem("sh_done"), d + 1)
                A(SH[:, d, :, :].rearrange("p c n -> p (c n)"), bank[2 + d][:, :], ACT.Copy).then_inc(sem("sh_copied"), 1)
            for st in range(NST):
                act.wait_ge(sem("oa_done"), st + 1)
                A(OA[:, st, :], bank[4 + st][:, :], ACT.Copy).then_inc(sem("oa_copied"), 1)
            act.wait_ge(sem("lfx"), 1)
            A(SG[:, :, :].rearrange("p s n -> p (s n)"), GA[:, :, :].rearrange("p s n -> p (s n)"), ACT.Silu).then_inc(sem("sg"), 1)
            act.wait_ge(sem("var"), 2)
            A(SM[:, 32:48], SM[:, 16:32], ACT.Sqrt).then_inc(sem("var_root"), 1)
            act.wait_ge(sem("latents_turned"), 2)
            A(CKT, bank[7][:, 0:384], ACT.Copy).then_inc(sem("ckt"), 1)
            for n in range(4):
                act.wait_ge(sem("qt_done"), n + 1)
                A(QT[:, n // 2, (n % 2) * 384:(n % 2 + 1) * 384], bank[(1, 2, 3, 6)[n]][:, 0:384], ACT.Copy).then_inc(sem("qt"), 1)
            for hd in range(HA):
                act.wait_ge(sem("kt_done"), hd + 1)
                A(kt(hd)[0:64, :], bank[(7, 0)[hd % 2]][0:64, 0:384], ACT.Copy).then_inc(sem("kt"), 1)
            for n in range(3):
                act.wait_ge(sem("vm_done"), n + 1)
                A(VM[:, n, :], bank[1 + n][:, :], ACT.Copy).then_inc(sem("vm"), 1)
            for n in range(4):
                act.wait_ge(sem("qtt_done"), n + 1)
                A(HTf[0:96, n * 512:(n + 1) * 512], bank[n][0:96, :], ACT.Copy).then_inc(sem("qtt"), 1)
            for u in range(8):
                st = u // 4
                nk = P if st == 0 else 256
                act.wait_ge(sem("nmx"), u + 1)
                for a in range(2):
                    n = 2 * u + a
                    A(PR[:, u % 4, a, 0:nk], bank[u % 2][:, a * 256:a * 256 + nk], ACT.Exp,
                      bias=SM[:, 64 + n:65 + n], scale=SCALE, accum_out=SM[:, 80 + n:81 + n]).then_inc(sem("prob"), 1)
            act.wait_ge(sem("stored_latents"), 32)
            copy_gates(0)
            for n in range(4):
                take(O[:, :, n * TW:(n + 1) * TW], N_EVEN_OUT + n, src=halves)
            norm_o(lambda: act.wait_ge(sem("proj_copied"), proj[0]))
            norm_x(lambda: act.wait_ge(sem("x"), 2))
            copy_gates(1)

            for j in range(FT):
                act.wait_ge(sem("tile_used"), N_FFN + up_used(j))
                A(SIL[:, j % 2, :], bank[2 * (j % 2)][:, :], ACT.Silu).then_inc(sem("silu"), 1)
            norm_o(lambda: act.wait_ge(sem("o_ready"), 1))
            norm_x(lambda: act.wait_ge(sem("x"), 4))
            ada_rows(1)
            for n in range(8):
                take(W[n // 4][:, (n % 4) * 512:(n % 4 + 1) * 512], N_ODD + n)
            for n in range(4):
                take(V1[:, :, n * TW:(n + 1) * TW], N_ODD + 8 + n, src=halves)
            take(MW, None, ACT.Tanh, 256)
            take(MA[0:64, :], None, src=lambda b: b[0:64, 0:TW])
            take(MG, None, ACT.Sigmoid, 256)

            def biased(dst, col):
                p = proj[0]
                proj[0] += 1
                filled(None)
                A(dst[:, 0, :], bank[p % 4][:, 0:TW], ACT.Sigmoid, bias=PV[:, col:col + 1])
                A(dst[:, 1, :], bank[p % 4][:, TW:2 * TW], ACT.Sigmoid, bias=PV[:, col + 1:col + 2]).then_inc(sem("proj_copied"), 1)

            act.wait_ge(sem("nrm"), 4)
            A(Of, Of, ACT.Sqrt).then_inc(sem("nrm_root"), 1)
            for d in range(2):
                for c in range(0, KC, 2):
                    biased(SGM[d][:, c:c + 2, :], W0 + d * KC + c)
            for c in range(0, KC, 2):
                biased(B[:, c:c + 2, :], A0 + c)
            act.wait_ge(sem("rw_inputs"), 1)
            act.sem_inc(sem("so"), 2)

            def decays():
                for n in range(4):
                    A(EE[:, n, :], CS[:, n, :], ACT.Exp, bias=SM[:, 100 + n:101 + n], scale=-KAPPA).then_inc(sem("ee"), 1)
                    a = 1 - n // 2
                    A(E2[:, n, :], CS[:, n, a:a + P], ACT.Exp, bias=SM[:, 104 + n:105 + n], scale=KAPPA).then_inc(sem("e2"), 1)
                A(SM[:, 108:112], SM[:, 104:108], ACT.Exp).then_inc(sem("em"), 1)

            act.wait_ge(sem("km"), 1)
            decays()
            with act.Fori(0, KC) as i:
                for d in range(2):
                    A(IP[d], ident.unsqueeze(1).to_broadcast([P, 4, P]), ACT.Copy).then_inc(sem("inv_start"), 1)
                    A(IX[d], ident.unsqueeze(1).to_broadcast([P, 4, P]), ACT.Copy).then_inc(sem("inv_start"), 1)
                for lv in range(1, LEVELS):
                    for d in range(2):
                        act.wait_ge(sem("z"), i * 12 + (2 * (lv - 1) + d + 1))
                        A(sided(IZ[d], lv, d), sided4(bank[4 * d], lv, d), ACT.Copy).then_inc(sem("zc"), 1)
                for d in range(2):
                    act.wait_ge(sem("g"), i * 2 + (d + 1))
                    A(GS[d][:, :, :].rearrange("p j n -> p (j n)"), bank[4 * d + 3][:, 0:256], ACT.Copy).then_inc(sem("gs"), 1)
                for d in range(2):
                    act.wait_ge(sem("u"), i * 2 + (d + 1))
                    A(US[d][:, :, :].rearrange("p j n -> p (j n)"), bank[4 * d][:, 0:256], ACT.Copy).then_inc(sem("us"), 1)
                act.wait_ge(sem("y"), i + 1)
                A(W[0][:, bass.ds(i * 256, 256)], bank[3][:, 0:256], ACT.Copy).then_inc(sem("y_copy"), 1)
                for d in range(2):
                    act.wait_ge(sem("trk_done"), i * 2 + (d + 1))
                    A(TRK[:, d, :, :].rearrange("p m n -> p (m n)"), bank[4 * d + 1][:, 0:256], ACT.Copy).then_inc(sem("trk"), 1)
                act.wait_ge(sem("km"), i + 2)
                act.wait_ge(sem("sf"), i * 2 + 2)
                decays()
                act.wait_ge(sem("stored_rwkv"), i * 32 + 32)
                for d in range(2):
                    act.wait_ge(sem("so_done"), i * 2 + (d + 1))
                    A(SO[:, d, :], bank[4 * d + 1][0:64, 256:256 + P], ACT.Copy).then_inc(sem("so"), 1)
                act.wait_ge(sem("so"), i * 2 + 4)
                for d in range(2):
                    dst = out["new_rwkv"][0, 0, d].rearrange("(c h) v k -> c v h k", h=2)[bass.ds(i, 1)]
                    act.dma_start(dst.rearrange("a v h k -> (a v) h k"),
                                  SO[:, d, :].rearrange("v (h k) -> v h k", h=2)).then_inc(sem("stored_rwkv"), 16)
            for st in range(NST):
                for h in range(2):
                    take(G1[:, st, h * 512:(h + 1) * 512], None)
            act.wait_ge(sem("var"), 3)
            A(SM[:, 128:160], SM[:, 128:160], ACT.Sqrt).then_inc(sem("var_root"), 1)
            for n in range(4):
                take(O[:, :, n * TW:(n + 1) * TW], N_ODD_OUT + n, src=halves)
            norm_o(lambda: act.wait_ge(sem("proj_copied"), proj[0]))
            copy_gates(2)
            norm_x(lambda: act.wait_ge(sem("x"), 6))
            act.wait_ge(sem("lgd"), 1)
            A(SM[:, 60:62], SM[:, 60:62], ACT.Exp).then_inc(sem("lge"), 1)
            for n in range(4):
                act.wait_ge(sem("htm_done"), n + 1)
                A(HTM[:, n // 2, (n % 2) * 512:(n % 2 + 1) * 512], bank[n][:, :], ACT.Copy).then_inc(sem("htm"), 1)
            act.wait_ge(sem("x"), 6)
            copy_gates(3)
            for n in range(2):
                act.wait_ge(sem("gathered"), n + 1)
                A(XG[:, 4 * n:4 * n + 4, :].rearrange("p c n -> p (c n)"), bank[2 + n][:, :], ACT.Copy).then_inc(sem("xg"), 1)
            act.wait_ge(sem("table"), 1)
            with act.Fori(0, act.value_load(TBL[0:1, UNITS:UNITS + 1], min_val=NE, max_val=UNITS)) as u:
                for j in range(FT):
                    act.wait_ge(sem("tile_used"), u * 3 * FT + (N_MOE + up_used(j)))
                    A(SILU[:, j % 2, :], bank[j % 2][:, 0:TW], ACT.Silu).then_inc(sem("silu"), 1)
                    if j == 3:
                        act.wait_ge(sem("selt_done"), u + 1)
                        A(SELT[:, :, :].rearrange("p s n -> p (s n)"), bank[6][:, 0:TW], ACT.Copy).then_inc(sem("selt"), 1)
                act.wait_ge(sem("tile_used"), u * 3 * FT + (N_MOE + 3 * FT))
                for n in range(2):
                    A(YG[:, n * 512:(n + 1) * 512], bank[4 + n][:, :], ACT.Copy).then_inc(sem("unit_out"), 1)
                for n in range(2):
                    act.wait_ge(sem("gathered"), u * 2 + (n + 3))
                    A(XG[:, 4 * n:4 * n + 4, :].rearrange("p c n -> p (c n)"), bank[2 + n][:, :],
                      ACT.Copy).then_inc(sem("xg"), 1)
            norm_o(lambda: act.wait_ge(sem("o_ready"), 2))

        @block.vector
        def _(dve):
            counts = Counts()
            made, so_far, in_loop = counts.made, counts.so_far, counts.in_loop
            v = nc.vector
            cnt = {"rstd": 0}

            def rstd(n):
                k = cnt["rstd"] = cnt["rstd"] + 1
                dve.wait_ge(sem("sumsq"), 2 * k)
                v.tensor_scalar(SM[:, 2:4], SM[:, 0:2], 1.0 / n, EPS, ALU.mult, ALU.add).then_inc(sem("meansq"), 1)
                dve.wait_ge(sem("root"), k)
                v.reciprocal(SM[:, 6:8], SM[:, 4:6]).then_inc(made("dve_chain"), 1)
                dve.wait_ge(sem("dve_chain"), so_far("dve_chain"))

            def normed_x():
                rstd(D)
                for st in range(NST):
                    v.tensor_scalar(O[:, st, :], X[:, st, :], SM[:, 6 + st:7 + st], None, ALU.mult).then_inc(sem("xn"), 1)

            def modulated(dst, k, scale, shift, ev):
                for st in range(NST):
                    for h in range(2):
                        dve.wait_ge(sem("turned"), 4 * k + 2 * st + h + 1)
                        for c in range(4):
                            n = 4 * h + c
                            ins = v.tensor_scalar(dst[:, n, st * P:(st + 1) * P], bank[2 * st + h][:, c * P:(c + 1) * P],
                                                  AG[:, scale, n, st:st + 1], MOD[:, shift, n, st:st + 1],
                                                  ALU.mult, ALU.add)
                            if (st, n) == (NST - 1, KC - 1):
                                ins.then_inc(made(ev), 1)
                                dve.wait_ge(sem(ev), so_far(ev))
                            else:
                                ins.then_inc(made("dve_chain"), 1)
                                dve.wait_ge(sem("dve_chain"), so_far("dve_chain"))

            def plain(dst, k, ev):
                for st in range(NST):
                    for h in range(2):
                        dve.wait_ge(sem("turned"), 4 * k + 2 * st + h + 1)
                        ins = v.tensor_copy(dst[:, 4 * h:4 * h + 4, st * P:(st + 1) * P],
                                            bank[2 * st + h][:, :].rearrange("p (c n) -> p c n", c=4))
                        done = ev if (st, h) == (1, 1) else "dve_chain"
                        ins.then_inc(made(done), 1)
                        dve.wait_ge(sem(done), so_far(done))

            def residual(n):
                rstd(D)
                dve.wait_ge(sem("gb_copied"), 4 * (n + 1))
                for st in range(NST):
                    v.scalar_tensor_tensor(O[:, st, :], O[:, st, :], SM[:, 6 + st:7 + st], GB[:, st, :],
                                           ALU.mult, ALU.mult).then_inc(made("dve_chain"), 1)
                    dve.wait_ge(sem("dve_chain"), so_far("dve_chain"))
                    done = "x_final" if n == 3 else "x"
                    v.tensor_tensor(X[:, st, :], X[:, st, :], O[:, st, :], ALU.add).then_inc(made(done), 1)
                    dve.wait_ge(sem(done), so_far(done))

            def modulation(l):
                dve.wait_ge(sem("ada_turned"), 12 * (l + 1))
                bias = PV[:, ADAB + 48 * l:ADAB + 48 * (l + 1)]
                for st in range(NST):
                    v.tensor_tensor(MOD[:, :, :, st].rearrange("p a k -> p (a k)"),
                                    bank[7][:, 0:96].rearrange("p (n s) -> p n s", s=NST)[:, :, st], bias, ALU.add).then_inc(made("dve_chain"), 1)
                    dve.wait_ge(sem("dve_chain"), so_far("dve_chain"))
                for m, (src, one) in enumerate(((1, 1.0), (2, 0.0), (4, 1.0), (5, 0.0))):
                    gain = PV[:, GAIN + (4 * l + m) * KC:GAIN + (4 * l + m + 1) * KC]
                    for st in range(NST):
                        ins = v.scalar_tensor_tensor(AG[:, m, :, st], MOD[:, src, :, st], one, gain, ALU.add, ALU.mult)
                        done = "ag" if (m, st) == (3, 1) else "dve_chain"
                        ins.then_inc(made(done), 1)
                        dve.wait_ge(sem(done), so_far(done))

            dve.wait_ge(sem("pv_done"), 1)
            v.tensor_copy(PV[:, :], bank[4][:, 0:NPV]).then_inc(made("pv"), 1)
            dve.wait_ge(sem("pv"), so_far("pv"))
            dve.wait_ge(sem("rows_in"), 16 * 13)
            normed_x()
            modulation(0)
            modulated(HT, 0, 0, 0, "ht")

            dve.wait_ge(sem("proj_copied"), 6)
            dve.wait_ge(sem("msk_bytes"), 1)
            f = W[1]
            v.scalar_tensor_tensor(EX[:, :], f[:, :], -1.0, f[:, :], ALU.mult, ALU.max).then_inc(made("absf"), 1)
            dve.wait_ge(sem("absf"), so_far("absf"))
            dve.wait_ge(sem("ln"), 1)
            v.scalar_tensor_tensor(LF[:, :], f[:, :], 0.0, EX[:, :], ALU.min, ALU.subtract).then_inc(made("dve_chain"), 1)
            dve.wait_ge(sem("dve_chain"), so_far("dve_chain"))
            v.tensor_tensor(EX[:, :], LF[:, :], f[:, :], ALU.subtract).then_inc(made("lfx"), 1)
            dve.wait_ge(sem("lfx"), so_far("lfx"))
            for n in range(16):
                a, b = LF[:, n * P:(n + 1) * P], BC[:, n * P:(n + 1) * P]
                if n >= 8:
                    a, b = a[:, ::-1], b[:, ::-1]
                v.tensor_tensor_scan(b, ones, a, 0.0, ALU.mult, ALU.add).then_inc(made("dve_chain"), 1)
                dve.wait_ge(sem("dve_chain"), so_far("dve_chain"))
            v.memset(AT[1][:, :], 0.0).then_inc(made("dve_chain"), 1)
            dve.wait_ge(sem("dve_chain"), so_far("dve_chain"))
            v.memset(AT[0][:, :], 0.0).then_inc(made("dve_chain"), 1)
            dve.wait_ge(sem("dve_chain"), so_far("dve_chain"))

            def take_a(lv, g):
                n, d = 8 * lv + g, g // 4
                dst = AT[d][:, (n % 4) * 512:(n % 4 + 1) * 512].rearrange("p (j n) -> p j n", j=4)
                dve.wait_ge(sem("at_done"), n + 1)
                if lv:
                    m = sided(mask(lv - 1, d), lv - 1, 1 - d).unsqueeze(1).to_broadcast([P, 4, P >> lv, 1 << (lv - 1)])
                    v.copy_predicated(sided(dst, lv - 1, 1 - d), m, sided4(bank[n % 4], lv - 1, 1 - d)).then_inc(made("at"), 1)
                else:
                    v.copy_predicated(dst, mask(LEVELS, 0).unsqueeze(1).to_broadcast([P, 4, P]),
                                      bank[n % 4][:, :].rearrange("p (j n) -> p j n", j=4)).then_inc(made("at"), 1)
                dve.wait_ge(sem("at"), so_far("at"))

            for lv in range(LEVELS + 1):
                if lv < LEVELS:
                    s = 1 << lv
                    if lv == 0:
                        dve.wait_ge(sem("kg"), 1)
                    for d in range(2):
                        half = slice(d * 1024, (d + 1) * 1024)
                        shape = lambda b: b.rearrange("p (n h s) -> p n h s", h=2, s=s)
                        b, e = shape(BC[:, half]), shape(EX[:, half])
                        mid = (b[:, :, 0, s - 1:s] if d == 0 else b[:, :, 1, 0:1]).to_broadcast([P, 512 // s, s])
                        late, early = (1, 0) if d == 0 else (0, 1)
                        v.tensor_tensor(e[:, :, late, :], b[:, :, late, :], mid, ALU.subtract).then_inc(made("dve_chain"), 1)
                        dve.wait_ge(sem("dve_chain"), so_far("dve_chain"))
                        done = "diff" if d else "dve_chain"
                        v.tensor_tensor(e[:, :, early, :], mid, b[:, :, early, :], ALU.subtract).then_inc(made(done), 1)
                        dve.wait_ge(sem(done), so_far(done))
                for g in range(8):
                    take_a(lv, g)
                if lv < LEVELS:
                    dve.wait_ge(sem("ex"), lv + 1)
                    for d in range(2):
                        half = slice(d * 1024, (d + 1) * 1024)
                        e, w, k, q = (shape(x) for x in (EX[:, half], WQ[:, half], KG[:, half], W[0][:, 0:1024]))
                        late, early = (1, 0) if d == 0 else (0, 1)
                        v.tensor_tensor(w[:, :, late, :], e[:, :, late, :], q[:, :, late, :], ALU.mult).then_inc(made("dve_chain"), 1)
                        dve.wait_ge(sem("dve_chain"), so_far("dve_chain"))
                        done = "wq" if d else "dve_chain"
                        v.tensor_tensor(w[:, :, early, :], e[:, :, early, :], k[:, :, early, :], ALU.mult).then_inc(made(done), 1)
                        dve.wait_ge(sem(done), so_far(done))
            dve.wait_ge(sem("ex"), LEVELS + 1)
            for d in range(2):
                half = slice(d * 1024, (d + 1) * 1024)
                v.tensor_tensor(WQ[:, half], EX[:, half], W[0][:, 0:1024], ALU.mult).then_inc(made("qe"), 1)
                dve.wait_ge(sem("qe"), so_far("qe"))
            for d in range(2):
                half = slice(d * 1024, (d + 1) * 1024)
                b, e = (x[:, half].rearrange("p (n s) -> p n s", s=P) for x in (BC, EX))
                end = (b[:, :, P - 1:P] if d == 0 else b[:, :, 0:1]).to_broadcast([P, 8, P])
                done = "diff" if d else "dve_chain"
                v.tensor_tensor(e, end, b, ALU.subtract).then_inc(made(done), 1)
                dve.wait_ge(sem(done), so_far(done))
            dve.wait_ge(sem("ex"), LEVELS + 2)
            v.tensor_tensor(EX[:, :], EX[:, :], KG[:, :], ALU.mult).then_inc(made("kdf"), 1)
            dve.wait_ge(sem("kdf"), so_far("kdf"))
            dve.wait_ge(sem("lat_sq"), 4)
            v.tensor_scalar(SM[:, 8:10], SM[:, 8:10], 1.0 / 256, EPS, ALU.mult, ALU.add).then_inc(made("dve_chain"), 1)
            dve.wait_ge(sem("dve_chain"), so_far("dve_chain"))
            v.tensor_scalar(SM[:, 10:12], SM[:, 10:12], 1.0 / P, EPS, ALU.mult, ALU.add).then_inc(made("var"), 1)
            dve.wait_ge(sem("var"), so_far("var"))
            dve.wait_ge(sem("var_root"), 1)
            v.reciprocal(SM[:, 12:16], SM[:, 8:12]).then_inc(made("dve_chain"), 1)
            dve.wait_ge(sem("dve_chain"), so_far("dve_chain"))
            dve.wait_ge(sem("gains_in"), 32)
            for st in range(NST):
                v.tensor_scalar(CQ[:, st, :], CQ[:, st, :], SM[:, 12 + st:13 + st], None, ALU.mult).then_inc(made("cqn"), 1)
                dve.wait_ge(sem("cqn"), so_far("cqn"))
                v.scalar_tensor_tensor(CKN[:, st, :], CKV[:, st, 0:P], SM[:, 14 + st:15 + st], KVG,
                                       ALU.mult, ALU.mult).then_inc(made("ckn"), 1)
                dve.wait_ge(sem("ckn"), so_far("ckn"))
            cos, sin = CST[:, C_COS:C_COS + 32], CST[:, C_SIN:C_SIN + 32]
            parts = lambda x: x.rearrange("p (a b n) -> p a b n", a=2, b=2)
            v.tensor_copy(KR[:, 2, 64:96], CKV[:, 0, P:P + 32]).then_inc(made("kr"), 1)
            dve.wait_ge(sem("kr"), so_far("kr"))
            kr, ks = CKV[:, 1, P:P + 32], KR[:, 1, 64:96]
            for b in range(2):
                v.tensor_tensor(parts(SM[:, 120:152])[:, :, b, :], parts(kr)[:, :, 1 - b, :], parts(sin)[:, :, b, :],
                                ALU.mult).then_inc(made("dve_chain"), 1)
                dve.wait_ge(sem("dve_chain"), so_far("dve_chain"))
            v.tensor_tensor(ks, kr, cos, ALU.mult).then_inc(made("dve_chain"), 1)
            dve.wait_ge(sem("dve_chain"), so_far("dve_chain"))
            v.tensor_tensor(ks, ks, SM[:, 120:152], ALU.add).then_inc(made("kr"), 1)
            dve.wait_ge(sem("kr"), so_far("kr"))
            dve.wait_ge(sem("latents_turned"), 1)
            for c in range(2):
                done = "cqt" if c else "dve_chain"
                v.tensor_scalar(CQT[:, c, :], bank[6][:, c * TW:(c + 1) * TW], PV[:, QN + c:QN + c + 1], None,
                                ALU.mult).then_inc(made(done), 1)
                dve.wait_ge(sem(done), so_far(done))
            dve.wait_ge(sem("latents_turned"), 3)
            for h in range(2):
                done = "krt" if h else "dve_chain"
                v.tensor_copy(KT[h][64:96, 0:1536].rearrange("p (h n) -> p h n", h=4),
                              bank[0][64:96, 0:384].unsqueeze(1).to_broadcast([32, 4, 384])).then_inc(made(done), 1)
                dve.wait_ge(sem(done), so_far(done))
            dve.wait_ge(sem("oa_copied"), 2)
            oa = W[1][:, 0:1024]
            per = lambda x, n=16: x.rearrange("p (h n) -> p h n", n=DH)
            v.tensor_tensor(WQ[:, 0:1024], oa, oa, ALU.mult).then_inc(made("dve_chain"), 1)
            dve.wait_ge(sem("dve_chain"), so_far("dve_chain"))
            v.tensor_reduce(SM[:, 16:32], per(WQ[:, 0:1024]), AX.X, ALU.add).then_inc(made("dve_chain"), 1)
            dve.wait_ge(sem("dve_chain"), so_far("dve_chain"))
            v.tensor_scalar(SM[:, 16:32], SM[:, 16:32], 1.0 / DH, EPS, ALU.mult, ALU.add).then_inc(made("var"), 1)
            dve.wait_ge(sem("var"), so_far("var"))
            dve.wait_ge(sem("var_root"), 2)
            v.reciprocal(SM[:, 48:64], SM[:, 32:48]).then_inc(made("dve_chain"), 1)
            dve.wait_ge(sem("dve_chain"), so_far("dve_chain"))
            v.tensor_tensor(per(oa), per(oa), SM[:, 48:64].unsqueeze(2).to_broadcast([P, 16, DH]), ALU.mult).then_inc(made("dve_chain"), 1)
            dve.wait_ge(sem("dve_chain"), so_far("dve_chain"))
            dve.wait_ge(sem("gains_in"), 32)
            v.tensor_tensor(per(oa), per(oa), HG.unsqueeze(1).to_broadcast([P, 16, DH]), ALU.mult).then_inc(made("dve_chain"), 1)
            dve.wait_ge(sem("dve_chain"), so_far("dve_chain"))
            dve.wait_ge(sem("sg"), 1)
            v.tensor_tensor(OM[:, :, 0:512], OA[:, :, :], SG[:, :, :], ALU.mult).then_inc(made("om"), 1)
            dve.wait_ge(sem("om"), so_far("om"))
            dve.wait_ge(sem("qt"), 4)
            q = QT[:, 1, :].rearrange("p (h n) -> p h n", h=HA)[:, :, 64:96]
            q4 = q.rearrange("p h (a b n) -> p h a b n", a=2, b=2)
            tq = TQ[:, 0:256].rearrange("p (h n) -> p h n", h=HA)
            t4 = tq.rearrange("p h (a b n) -> p h a b n", a=2, b=2)
            for a in range(2):
                for b in range(2):
                    v.tensor_tensor(t4[:, :, a, b, :], q4[:, :, a, 1 - b, :],
                                    parts(sin)[:, a, b, :].unsqueeze(1).to_broadcast([P, HA, 8]), ALU.mult).then_inc(made("dve_chain"), 1)
                    dve.wait_ge(sem("dve_chain"), so_far("dve_chain"))
            v.tensor_tensor(q, q, cos.unsqueeze(1).to_broadcast([P, HA, 32]), ALU.mult).then_inc(made("dve_chain"), 1)
            dve.wait_ge(sem("dve_chain"), so_far("dve_chain"))
            v.tensor_tensor(q, q, tq, ALU.add).then_inc(made("qrope"), 1)
            dve.wait_ge(sem("qrope"), so_far("qrope"))

            def maxima(u):
                st = u // 4
                nk = P if st == 0 else 256
                dve.wait_ge(sem("sc_done"), u + 1)
                s = bank[u % 2][:, :].rearrange("p (a n) -> p a n", a=2)[:, :, 0:nk]
                v.tensor_reduce(SM[:, 96:98], s, AX.X, ALU.max).then_inc(made("dve_chain"), 1)
                dve.wait_ge(sem("dve_chain"), so_far("dve_chain"))
                v.tensor_scalar(SM[:, 64 + 2 * u:66 + 2 * u], SM[:, 96:98], -SCALE, None, ALU.mult).then_inc(made("nmx"), 1)
                dve.wait_ge(sem("nmx"), so_far("nmx"))

            maxima(0)
            for u in range(8):
                if u < 7:
                    maxima(u + 1)
                dve.wait_ge(sem("pt_done"), u + 1)
                n = 1 if u < 4 else 2
                view = lambda x: x.rearrange("p (a k) -> p a k", a=2)[:, :, 0:n * P]
                v.tensor_copy(view(PT[:, u % 4, :]), view(bank[2 + u % 2][:, :])).then_inc(made("pt"), 1)
                dve.wait_ge(sem("pt"), so_far("pt"))
            dve.wait_ge(sem("prob"), 16)
            v.reciprocal(SM[:, 80:96], SM[:, 80:96]).then_inc(made("dve_chain"), 1)
            dve.wait_ge(sem("dve_chain"), so_far("dve_chain"))
            for st in range(NST):
                dve.wait_ge(sem("pv_att"), 4 * (st + 1))
                done = "om" if st else "dve_chain"
                v.tensor_tensor(per(OM[:, st, 512:1024]), per(bank[4 + st][:, :]),
                                SM[:, 80 + 8 * st:88 + 8 * st].unsqueeze(2).to_broadcast([P, HA, DH]), ALU.mult).then_inc(made(done), 1)
                dve.wait_ge(sem(done), so_far(done))
            dve.wait_ge(sem("stored_hgrn"), 64)
            plain(MT, 1, "mt")
            residual(0)
            normed_x()
            modulated(HT, 2, 2, 3, "ht")

            for j in range(FT):
                dve.wait_ge(sem("silu"), j + 1)
                if j >= 2:
                    dve.wait_ge(sem("tile_used"), N_FFN + down_used(j - 2))
                v.tensor_tensor(HID[:, j % 2, :], SIL[:, j % 2, :], bank[2 * (j % 2) + 1][:, :], ALU.mult).then_inc(sem("hid"), 1)
            dve.wait_ge(sem("tile_used"), N_ADA1)
            for n in range(4):
                done = "y_taken" if n == 3 else "dve_chain"
                v.tensor_copy(O[:, n // 2, (n % 2) * 512:(n % 2 + 1) * 512], bank[4 + n][:, :]).then_inc(made(done), 1)
                dve.wait_ge(sem(done), so_far(done))
            v.tensor_copy(SM[:, 198:199], SM[:, 6:7]).then_inc(made("o_ready"), 1)
            dve.wait_ge(sem("o_ready"), so_far("o_ready"))
            residual(1)

            normed_x()
            modulation(1)
            modulated(HT, 3, 0, 0, "dve_chain")
            h16, x16 = (b.rearrange("p (g n) -> p g n", n=P) for b in (HTf, Of))
            v.tensor_tensor(x16[:, :, 1:P - 1], h16[:, :, 0:P - 2], h16[:, :, 2:P], ALU.add).then_inc(made("dve_chain"), 1)
            dve.wait_ge(sem("dve_chain"), so_far("dve_chain"))
            v.tensor_copy(x16[:, :, 0:1], h16[:, :, 1:2]).then_inc(made("dve_chain"), 1)
            dve.wait_ge(sem("dve_chain"), so_far("dve_chain"))
            v.tensor_copy(x16[:, :, P - 1:P], h16[:, :, P - 2:P - 1]).then_inc(made("dve_chain"), 1)
            dve.wait_ge(sem("dve_chain"), so_far("dve_chain"))
            v.scalar_tensor_tensor(Of, Of, 0.5, HTf, ALU.mult, ALU.subtract).then_inc(made("dve_chain"), 1)
            dve.wait_ge(sem("dve_chain"), so_far("dve_chain"))
            for n, m in enumerate((0, 2, 3, 1, 4, 5)):
                if n >= 2:
                    dve.wait_ge(sem("tile_used" if n < 5 else "proj_done"), N_ODD + 4 * (n - 1) if n < 5 else 1)
                for c in range(KC):
                    done = "xs" if c == KC - 1 else "dve_chain"
                    v.scalar_tensor_tensor(XS[n % 2][:, c, :], XX[:, c, :], PV[:, MU + m * KC + c:MU + m * KC + c + 1],
                                           HT[:, c, :], ALU.mult, ALU.add).then_inc(made(done), 1)
                    dve.wait_ge(sem(done), so_far(done))
            dve.wait_ge(sem("proj_copied"), 16 + 8)
            col = lambda o, c: PV[:, o + c:o + c + 1]
            for c in range(KC):
                v.tensor_scalar(NK[:, c, :], K[:, c, :], col(KK, c), None, ALU.mult).then_inc(made("dve_chain"), 1)
                dve.wait_ge(sem("dve_chain"), so_far("dve_chain"))
            v.tensor_tensor(Of, W[2][:, :], W[2][:, :], ALU.mult).then_inc(made("kk2"), 1)
            dve.wait_ge(sem("kk2"), so_far("kk2"))
            for n in range(4):
                dve.wait_ge(sem("nrm_done"), n + 1)
                v.tensor_scalar(Of[:, n * 512:(n + 1) * 512], bank[4 + n][:, :], 1e-12, None, ALU.add).then_inc(made("nrm"), 1)
                dve.wait_ge(sem("nrm"), so_far("nrm"))
            dve.wait_ge(sem("nrm_root"), 1)
            v.reciprocal(Of, Of).then_inc(made("dve_chain"), 1)
            dve.wait_ge(sem("dve_chain"), so_far("dve_chain"))
            v.scalar_tensor_tensor(W[2][:, :], W[2][:, :], -1.0, Of, ALU.mult, ALU.mult).then_inc(made("dve_chain"), 1)
            dve.wait_ge(sem("dve_chain"), so_far("dve_chain"))
            dve.wait_ge(sem("proj_copied"), 16 + 15 + 8 + 4)
            for c in range(KC):
                v.tensor_scalar(XS[1][:, c, :], B[:, c, :], 1.0, col(KA, c), ALU.subtract, ALU.mult).then_inc(made("dve_chain"), 1)
                dve.wait_ge(sem("dve_chain"), so_far("dve_chain"))
            v.scalar_tensor_tensor(W[1][:, :], W[9][:, :], 1.0, W[1][:, :], ALU.add, ALU.mult).then_inc(made("dve_chain"), 1)
            dve.wait_ge(sem("dve_chain"), so_far("dve_chain"))
            v.scalar_tensor_tensor(W[3][:, :], W[2][:, :], -1.0, W[3][:, :], ALU.mult, ALU.mult).then_inc(made("dve_chain"), 1)
            dve.wait_ge(sem("dve_chain"), so_far("dve_chain"))
            for c in range(KC):
                done = "rk" if c == KC - 1 else "dve_chain"
                v.scalar_tensor_tensor(XS[0][:, c, :], R[:, c, :], col(RK, c), K[:, c, :], ALU.mult, ALU.mult).then_inc(made(done), 1)
                dve.wait_ge(sem(done), so_far(done))
            v.memset(CS[:, :, :], 0.0).then_inc(made("dve_chain"), 1)
            dve.wait_ge(sem("dve_chain"), so_far("dve_chain"))
            for d in range(2):
                v.memset(IZ[d], 0.0).then_inc(made("dve_chain"), 1)
                dve.wait_ge(sem("dve_chain"), so_far("dve_chain"))
            v.memset(S0P[:, :, :], 0.0).then_inc(made("dve_chain"), 1)
            dve.wait_ge(sem("dve_chain"), so_far("dve_chain"))
            v.tensor_copy(SM[:, 198:199], SM[:, 6:7]).then_inc(made("rw_free"), 1)
            dve.wait_ge(sem("rw_free"), so_far("rw_free"))
            v.tensor_copy(SM[:, 198:199], SM[:, 6:7]).then_inc(made("rw_inputs"), 1)
            dve.wait_ge(sem("rw_inputs"), so_far("rw_inputs"))

            def sums(c):
                for n in range(4):
                    d, st = n // 2, n % 2
                    src = SGM[d][:, :, :].rearrange("p c n -> p (c n)")[:, bass.ds(c * 256 + st * P, P)]
                    if d == 0:
                        v.tensor_tensor_scan(CS[:, n, 1:P + 1], ones, src, 0.0, ALU.mult, ALU.add).then_inc(made("dve_chain"), 1)
                        dve.wait_ge(sem("dve_chain"), so_far("dve_chain"))
                    else:
                        v.tensor_copy(BACK, src).then_inc(made("dve_chain"), 1)
                        dve.wait_ge(sem("dve_chain"), so_far("dve_chain"))
                        v.tensor_tensor_scan(CS[:, n, 0:P][:, ::-1], ones, BACK[:, ::-1], 0.0,
                                             ALU.mult, ALU.add).then_inc(made("dve_chain"), 1)
                        dve.wait_ge(sem("dve_chain"), so_far("dve_chain"))
                mid = CS[:, :, 64:65].rearrange("p a n -> p (a n)")
                v.tensor_scalar(SM[:, 100:104], mid, KAPPA, None, ALU.mult).then_inc(made("dve_chain"), 1)
                dve.wait_ge(sem("dve_chain"), so_far("dve_chain"))
                v.tensor_scalar(SM[:, 104:108], mid, -KAPPA, None, ALU.mult).then_inc(made("km"), 1)
                dve.wait_ge(sem("km"), so_far("km"))

            sums(0)
            dve.wait_ge(sem("bon_done"), 1)
            v.tensor_copy(SM[:, 160:192], bank[4][:, 0:32]).then_inc(made("dve_chain"), 1)
            dve.wait_ge(sem("dve_chain"), so_far("dve_chain"))
            with dve.Fori(0, KC) as i, in_loop(i, KC, {"dve_chain": 16, "km": 1, "dec": 2, "s0p": 1, "m4": 8, "inv": 26, "sf": 2, "rw_free": 1}):
                at = lambda b: b[:, bass.ds(i * 256, 256)].rearrange("p (s n) -> p s n", s=NST)
                r, k, nk, b = (at(W[n][:, :]) for n in range(4))
                for d in range(2):
                    dve.wait_ge(sem("ee"), i * 4 + (2 * d + 2))
                    dve.wait_ge(sem("e2"), i * 4 + (2 * d + 2))
                    ex, inc = (0, 1) if d == 0 else (1, 0)
                    pair = slice(2 * d, 2 * d + 2)
                    v.tensor_tensor(NQ[:, d, :, 0, :], nk, EE[:, pair, ex:ex + P], ALU.mult).then_inc(made("dve_chain"), 1)
                    dve.wait_ge(sem("dve_chain"), so_far("dve_chain"))
                    v.tensor_tensor(NQ[:, d, :, 1, :], r, EE[:, pair, inc:inc + P], ALU.mult).then_inc(made("dve_chain"), 1)
                    dve.wait_ge(sem("dve_chain"), so_far("dve_chain"))
                    v.tensor_tensor(BD[:, d, :, :], b, E2[:, pair, :], ALU.mult).then_inc(made("dve_chain"), 1)
                    dve.wait_ge(sem("dve_chain"), so_far("dve_chain"))
                    v.tensor_tensor(KDC[:, d, :, :], k, E2[:, pair, :], ALU.mult).then_inc(made("dec"), 1)
                    dve.wait_ge(sem("dec"), so_far("dec"))
                dve.wait_ge(sem("s0_t"), i + 2)
                dve.wait_ge(sem("em"), i + 1)
                for n in range(4):
                    d, hp = n // 2, slice(64 * (n % 2), 64 * (n % 2) + 64)
                    done = "s0p" if n == 3 else "dve_chain"
                    v.tensor_scalar(S0P[hp, d, hp], bank[7][hp, 256 + d * DH:256 + (d + 1) * DH],
                                    SM[hp, 109 + 2 * d:110 + 2 * d], None, ALU.mult).then_inc(made(done), 1)
                    dve.wait_ge(sem(done), so_far(done))
                for d in range(2):
                    tri = CST[:, C_TRI + d * 256:C_TRI + (d + 1) * 256].unsqueeze(1).to_broadcast([P, 2, 256])
                    for j in range(4):
                        dve.wait_ge(sem("t4"), i * 8 + (4 * d + j + 1))
                        v.tensor_tensor(M4[d][:, j, :, :].rearrange("p (a m) n -> p a (m n)", a=2),
                                        bank[4 * d + j][:, :].rearrange("p (a n) -> p a n", a=2), tri, ALU.mult).then_inc(made("m4"), 1)
                        dve.wait_ge(sem("m4"), so_far("m4"))
                dve.wait_ge(sem("inv_start"), i * 4 + 4)
                wide = lambda m: m.unsqueeze(1).to_broadcast([P, 4, P])
                halves4 = lambda m, level, side: sided(m, level, side).unsqueeze(1).to_broadcast([P, 4, DH >> level, 1 << level])
                four = lambda b: b[:, :].rearrange("p (j n) -> p j n", j=4)
                for d in range(2):
                    dve.sem_inc(sem("dve_settled"), 1)
                    v.copy_predicated(IP[d], wide(mask(0, d)), M4[d][:, :, 0, :]).then_inc(made("inv"), 1)
                    dve.wait_ge(sem("inv"), so_far("inv"))
                    dve.wait_ge(sem("nt"), i * 2 + (d + 1))
                    dve.sem_inc(sem("dve_settled"), 1)
                    v.copy_predicated(IX[d], wide(mask(0, 1 - d)), four(bank[4 * d])).then_inc(made("inv"), 1)
                    dve.wait_ge(sem("inv"), so_far("inv"))
                for lv in range(1, LEVELS):
                    for d in range(2):
                        if lv < LEVELS - 1:
                            dve.wait_ge(sem("dx"), i * 10 + (2 * (lv - 1) + d + 1))
                            dve.wait_ge(sem("dp"), i * 12 + (2 * (lv - 1) + d + 1))
                            dve.sem_inc(sem("dve_settled"), 1)
                            v.copy_predicated(sided(IX[d], lv, d), halves4(mask(lv, 1 - d), lv, d), sided4(bank[4 * d + 1], lv, d)).then_inc(made("inv"), 1)
                            dve.wait_ge(sem("inv"), so_far("inv"))
                        dve.wait_ge(sem("dp"), i * 12 + (2 * (lv - 1) + d + 1))
                        dve.sem_inc(sem("dve_settled"), 1)
                        v.copy_predicated(sided(IP[d], lv, 1 - d), halves4(mask(lv, d), lv, 1 - d), sided4(bank[4 * d + 2], lv, 1 - d)).then_inc(made("inv"), 1)
                        dve.wait_ge(sem("inv"), so_far("inv"))
                sums((i + 1) % KC)
                for d in range(2):
                    dve.wait_ge(sem("sf_done"), i * 2 + (d + 1))
                    last = EE[:, 2 * d, P:P + 1] if d == 0 else EE[:, 2 * d, 0:1]
                    v.tensor_scalar(SF[:, d, :], bank[4 * d + 2][:, 0:DH], last, None, ALU.mult).then_inc(made("sf"), 1)
                    dve.wait_ge(sem("sf"), so_far("sf"))
                v.tensor_copy(SM[:, 199:200], SM[:, 6:7]).then_inc(made("rw_free"), 1)
                dve.wait_ge(sem("rw_free"), so_far("rw_free"))
            y = W[0][:, :]
            h32 = lambda x: x.rearrange("p (g n) -> p g n", n=DH)
            stat = lambda s: s.unsqueeze(2).to_broadcast([P, 32, DH])
            dve.wait_ge(sem("y_copy"), KC)
            v.tensor_reduce(SM[:, 128:160], h32(y), AX.X, ALU.add).then_inc(made("dve_chain"), 1)
            dve.wait_ge(sem("dve_chain"), so_far("dve_chain"))
            v.tensor_scalar(SM[:, 128:160], SM[:, 128:160], 1.0 / DH, None, ALU.mult).then_inc(made("dve_chain"), 1)
            dve.wait_ge(sem("dve_chain"), so_far("dve_chain"))
            v.tensor_tensor(h32(y), h32(y), stat(SM[:, 128:160]), ALU.subtract).then_inc(made("dve_chain"), 1)
            dve.wait_ge(sem("dve_chain"), so_far("dve_chain"))
            v.tensor_tensor(W[2][:, :], y, y, ALU.mult).then_inc(made("dve_chain"), 1)
            dve.wait_ge(sem("dve_chain"), so_far("dve_chain"))
            v.tensor_reduce(SM[:, 128:160], h32(W[2][:, :]), AX.X, ALU.add).then_inc(made("dve_chain"), 1)
            dve.wait_ge(sem("dve_chain"), so_far("dve_chain"))
            v.tensor_scalar(SM[:, 128:160], SM[:, 128:160], 1.0 / DH, GN_EPS, ALU.mult, ALU.add).then_inc(made("var"), 1)
            dve.wait_ge(sem("var"), so_far("var"))
            dve.wait_ge(sem("var_root"), 3)
            v.reciprocal(SM[:, 128:160], SM[:, 128:160]).then_inc(made("dve_chain"), 1)
            dve.wait_ge(sem("dve_chain"), so_far("dve_chain"))
            v.tensor_tensor(h32(y), h32(y), stat(SM[:, 128:160]), ALU.mult).then_inc(made("dve_chain"), 1)
            dve.wait_ge(sem("dve_chain"), so_far("dve_chain"))
            dve.wait_ge(sem("ln_in"), 32)
            dve.wait_ge(sem("proj_copied"), 16 + 15 + 8 + 4 + 4)
            byc = lambda x: x.rearrange("p (c n) -> p c n", c=KC)
            for st in range(NST):
                yst = Y1[:, :, st, :]
                v.tensor_tensor(yst, yst, byc(W[1][:, 0:1024]), ALU.mult).then_inc(made("dve_chain"), 1)
                dve.wait_ge(sem("dve_chain"), so_far("dve_chain"))
                v.tensor_tensor(yst, yst, byc(W[1][:, 1024:2048]), ALU.add).then_inc(made("dve_chain"), 1)
                dve.wait_ge(sem("dve_chain"), so_far("dve_chain"))
                v.tensor_tensor(h32(V1[:, st, :]), h32(V1[:, st, :]),
                                BON[:, st, :].unsqueeze(2).to_broadcast([P, HC, DH]), ALU.mult).then_inc(made("dve_chain"), 1)
                dve.wait_ge(sem("dve_chain"), so_far("dve_chain"))
                v.tensor_tensor(yst, yst, byc(V1[:, st, :]), ALU.add).then_inc(made("dve_chain"), 1)
                dve.wait_ge(sem("dve_chain"), so_far("dve_chain"))
                done = "yg" if st else "dve_chain"
                v.tensor_tensor(yst, yst, byc(G1[:, st, :]), ALU.mult).then_inc(made(done), 1)
                dve.wait_ge(sem(done), so_far(done))
            plain(XS[0], 4, "yt")
            residual(2)
            normed_x()
            dve.wait_ge(sem("stored_rwkv"), 32 * (KC + 1))
            modulated(HT, 5, 2, 3, "ht")

            dve.wait_ge(sem("logits"), 1)
            L = SM[:, 100:116]
            v.tensor_copy(L, bank[4][:, 0:16]).then_inc(made("lg"), 1)
            dve.wait_ge(sem("lg"), so_far("lg"))
            first = [SM[:, 116:132], SM[:, 132:148]]
            per8 = lambda x: x.rearrange("p (s n) -> p s n", s=NST)
            for r in range(2):
                top = SM[:, 56 + 2 * r:58 + 2 * r]
                v.tensor_reduce(top, per8(L), AX.X, ALU.max).then_inc(made("dve_chain"), 1)
                dve.wait_ge(sem("dve_chain"), so_far("dve_chain"))
                v.tensor_tensor(per8(first[r]), per8(L), top.unsqueeze(2).to_broadcast([P, NST, NE]), ALU.is_equal).then_inc(made("dve_chain"), 1)
                dve.wait_ge(sem("dve_chain"), so_far("dve_chain"))
                for st in range(NST):
                    f = first[r][:, st * NE:(st + 1) * NE]
                    v.tensor_tensor_scan(SM[:, 148:156], CST[:, C_ONE:C_ONE + 1].to_broadcast([P, NE]), f, 0.0, ALU.mult, ALU.add).then_inc(made("dve_chain"), 1)
                    dve.wait_ge(sem("dve_chain"), so_far("dve_chain"))
                    v.scalar_tensor_tensor(f, SM[:, 148:156], 1.0, f, ALU.is_equal, ALU.mult).then_inc(made("dve_chain"), 1)
                    dve.wait_ge(sem("dve_chain"), so_far("dve_chain"))
                if r == 0:
                    v.scalar_tensor_tensor(L, first[0], -3.0e38, L, ALU.mult, ALU.add).then_inc(made("dve_chain"), 1)
                    dve.wait_ge(sem("dve_chain"), so_far("dve_chain"))
            v.tensor_tensor(CHOSEN, first[0], first[1], ALU.add).then_inc(made("chosen"), 1)
            dve.wait_ge(sem("chosen"), so_far("chosen"))
            v.tensor_tensor(SM[:, 60:62], SM[:, 58:60], SM[:, 56:58], ALU.subtract).then_inc(made("lgd"), 1)
            dve.wait_ge(sem("lgd"), so_far("lgd"))
            dve.wait_ge(sem("lge"), 1)
            v.tensor_scalar(SM[:, 62:64], SM[:, 60:62], 1.0, None, ALU.add).then_inc(made("dve_chain"), 1)
            dve.wait_ge(sem("dve_chain"), so_far("dve_chain"))
            v.reciprocal(SM[:, 62:64], SM[:, 62:64]).then_inc(made("dve_chain"), 1)
            dve.wait_ge(sem("dve_chain"), so_far("dve_chain"))
            v.tensor_tensor(SM[:, 60:62], SM[:, 60:62], SM[:, 62:64], ALU.mult).then_inc(made("dve_chain"), 1)
            dve.wait_ge(sem("dve_chain"), so_far("dve_chain"))
            for st in range(NST):
                cut = slice(st * NE, (st + 1) * NE)
                v.tensor_scalar(GT[:, st, :], first[0][:, cut], SM[:, 62 + st:63 + st], None, ALU.mult).then_inc(made("dve_chain"), 1)
                dve.wait_ge(sem("dve_chain"), so_far("dve_chain"))
                v.scalar_tensor_tensor(GT[:, st, :], first[1][:, cut], SM[:, 60 + st:61 + st], GT[:, st, :],
                                       ALU.mult, ALU.add).then_inc(made("dve_chain"), 1)
                dve.wait_ge(sem("dve_chain"), so_far("dve_chain"))
            v.memset(Of, 0.0).then_inc(made("dve_chain"), 1)
            dve.wait_ge(sem("dve_chain"), so_far("dve_chain"))
            dve.wait_ge(sem("placed"), 1)
            v.scalar_tensor_tensor(PLACE, bank[0][:, 0:16], 1.0, CHOSEN, ALU.add, ALU.mult).then_inc(made("dve_chain"), 1)
            dve.wait_ge(sem("dve_chain"), so_far("dve_chain"))
            v.tensor_scalar(PLACE, PLACE, 1.0, None, ALU.subtract).then_inc(made("dve_chain"), 1)
            dve.wait_ge(sem("dve_chain"), so_far("dve_chain"))
            v.tensor_copy(TAKEN, bank[0][:, 16:24]).then_inc(made("dve_chain"), 1)
            dve.wait_ge(sem("dve_chain"), so_far("dve_chain"))
            v.tensor_copy(IOTA, bank[1][:, 0:P]).then_inc(made("dve_chain"), 1)
            dve.wait_ge(sem("dve_chain"), so_far("dve_chain"))
            v.tensor_scalar(OVER, TAKEN, float(P), None, ALU.is_gt).then_inc(made("dve_chain"), 1)
            dve.wait_ge(sem("dve_chain"), so_far("dve_chain"))
            v.tensor_tensor_scan(ORDER, CST[:, C_ONE:C_ONE + 1].to_broadcast([P, NE]), OVER, 0.0, ALU.mult, ALU.add).then_inc(made("dve_chain"), 1)
            dve.wait_ge(sem("dve_chain"), so_far("dve_chain"))
            v.memset(UNITV[:, :, :], -1.0).then_inc(made("dve_chain"), 1)
            dve.wait_ge(sem("dve_chain"), so_far("dve_chain"))
            v.tensor_copy(UNITV[:, 0:2, 0:NE], per8(PLACE)).then_inc(made("dve_chain"), 1)
            dve.wait_ge(sem("dve_chain"), so_far("dve_chain"))

            def select(u, chain):
                v.tensor_copy(PLACE1, PLACEU[:, :, bass.ds(u, 1)].rearrange("p s a -> p (s a)")).then_inc(made(chain), 1)
                dve.wait_ge(sem(chain), so_far(chain))
                for st in range(NST):
                    done = "sel" if st else chain
                    v.tensor_scalar(SEL[:, st, :], IOTA, PLACE1[:, st:st + 1], None, ALU.is_equal).then_inc(made(done), 1)
                    dve.wait_ge(sem(done), so_far(done))

            select(0, "dve_chain")
            v.tensor_copy(PG[:, 0:2, :], per8(PLACE)).then_inc(made("dve_chain"), 1)
            dve.wait_ge(sem("dve_chain"), so_far("dve_chain"))
            v.tensor_copy(PG[:, 2:4, :], GT[:, :, :]).then_inc(made("dve_chain"), 1)
            dve.wait_ge(sem("dve_chain"), so_far("dve_chain"))
            v.tensor_copy(UNITV[:, 2:4, 0:NE], GT[:, :, :]).then_inc(made("dve_chain"), 1)
            dve.wait_ge(sem("dve_chain"), so_far("dve_chain"))
            v.memset(TBLF, 0.0).then_inc(made("dve_chain"), 1)
            dve.wait_ge(sem("dve_chain"), so_far("dve_chain"))
            v.tensor_copy(TBLF[:, 0:NE], IOTA[:, 0:NE]).then_inc(made("dve_chain"), 1)
            dve.wait_ge(sem("dve_chain"), so_far("dve_chain"))
            for k in range(UNITS - NE):
                u = NE + k
                v.scalar_tensor_tensor(PICK, ORDER, float(k + 1), OVER, ALU.is_equal, ALU.mult).then_inc(made("dve_chain"), 1)
                dve.wait_ge(sem("dve_chain"), so_far("dve_chain"))
                v.tensor_tensor(TMP8, PICK, IOTA[:, 0:NE], ALU.mult).then_inc(made("dve_chain"), 1)
                dve.wait_ge(sem("dve_chain"), so_far("dve_chain"))
                v.tensor_reduce(TBLF[:, u:u + 1], TMP8, AX.X, ALU.add).then_inc(made("dve_chain"), 1)
                dve.wait_ge(sem("dve_chain"), so_far("dve_chain"))
                v.tensor_tensor(TMP32, PG, PICK.unsqueeze(1).to_broadcast([P, 4, NE]), ALU.mult).then_inc(made("dve_chain"), 1)
                dve.wait_ge(sem("dve_chain"), so_far("dve_chain"))
                v.tensor_reduce(UNITV[:, :, u:u + 1], TMP32, AX.X, ALU.add).then_inc(made("dve_chain"), 1)
                dve.wait_ge(sem("dve_chain"), so_far("dve_chain"))
            v.tensor_scalar(PLACEU[:, :, NE:UNITS], PLACEU[:, :, NE:UNITS], float(P), None, ALU.subtract).then_inc(made("dve_chain"), 1)
            dve.wait_ge(sem("dve_chain"), so_far("dve_chain"))
            v.tensor_scalar(TBLF[:, UNITS:UNITS + 1], ORDER[:, NE - 1:NE], float(NE), None, ALU.add).then_inc(made("dve_chain"), 1)
            dve.wait_ge(sem("dve_chain"), so_far("dve_chain"))
            v.tensor_copy(TBL[:, :], TBLF).then_inc(made("table"), 1)
            dve.wait_ge(sem("table"), so_far("table"))
            units = dve.value_load(TBL[0:1, UNITS:UNITS + 1], min_val=NE, max_val=UNITS)
            with dve.Fori(0, units) as u, in_loop(u, NE, {"unit_chain": 6, "sel": 1, "y_taken": 1}):
                for j in range(FT):
                    dve.wait_ge(sem("silu"), u * FT + (FT + j + 1))
                    used = down_used(j - 2) if j >= 2 else down_used(FT - 1 - j) - 3 * FT
                    dve.wait_ge(sem("tile_used"), u * 3 * FT + (N_MOE + used))
                    v.tensor_tensor(HIDU[:, j % 2, :], SILU[:, j % 2, :], bank[j % 2][:, TW:2 * TW],
                                    ALU.mult).then_inc(sem("hid"), 1)
                    if j == 4:
                        dve.wait_ge(sem("selt_done"), u + 1)
                        select(u + 1, "unit_chain")
                v.tensor_copy(GT1, GTU[:, :, bass.ds(u, 1)].rearrange("p s a -> p (s a)")).then_inc(made("unit_chain"), 1)
                dve.wait_ge(sem("unit_chain"), so_far("unit_chain"))
                for n in range(4):
                    st, h = n // 2, n % 2
                    dve.wait_ge(sem("scattered"), u * 4 + (n + 1))
                    o = O[:, st, h * 512:(h + 1) * 512]
                    done = "y_taken" if n == 3 else "unit_chain"
                    v.scalar_tensor_tensor(o, bank[(6, 4)[st] + h][:, :], GT1[:, st:st + 1], o,
                                           ALU.mult, ALU.add).then_inc(made(done), 1)
                    dve.wait_ge(sem(done), so_far(done))
            v.tensor_copy(SM[:, 198:199], SM[:, 6:7]).then_inc(made("o_ready"), 1)
            dve.wait_ge(sem("o_ready"), so_far("o_ready"))
            residual(3)


_INS = ["x_prompt", "x_sample", "cache_ckv", "cache_krope", "state_hgrn", "state_rwkv", "c", "c_ctx", "ada_w", "ada_b",
        "norm_gains", "ev_w_in", "hgrn_norm", "mla_q_norm", "mla_w_q_up", "mla_kv_norm", "mla_w_kv_up", "ev_w_out",
        "rw_mu", "rw_w_r", "rw_w_k", "rw_w_v", "rw_w_o", "rw_w0", "rw_w1", "rw_w2", "rw_a0", "rw_a1", "rw_a2", "rw_g1",
        "rw_g2", "rw_k_k", "rw_k_a", "rw_r_k", "rw_ln_w", "rw_ln_b", "ffn_w_gate", "ffn_w_up", "ffn_w_down",
        "moe_router", "moe_w_gate", "moe_w_up", "moe_w_down"]
_OUTS = [("y_prompt", (1, 128, 1024)), ("y_sample", (1, 128, 1024)), ("new_ckv", (1, 1, 128, 128)),
         ("new_krope", (1, 1, 128, 32)), ("new_hgrn", (1, 1, 2, 8, 64, 64)), ("new_rwkv", (1, 1, 2, 16, 64, 64))]


def kernel(**inputs):
    import concourse.bacc as _bacc
    from concourse.bass_utils import run_bass_kernel_spmd as _run

    nc = _bacc.Bacc("TRN2", target_bir_lowering=False, num_devices=1)
    arrays = {name: np.ascontiguousarray(inputs[name]) for name in _INS}
    arrays["cst"], arrays["msk"] = constants()
    t = {name: nc.dram_tensor(f"in_{name}", a.shape, mybir.dt.from_np(a.dtype), kind="ExternalInput").ap()
         for name, a in arrays.items()}
    out = {name: nc.dram_tensor(f"out_{name}", shape, F32, kind="ExternalOutput").ap() for name, shape in _OUTS}
    program(nc, t, out)
    r = _run(nc, [{f"in_{name}": a for name, a in arrays.items()}], core_ids=[0])
    return tuple(r.results[0][f"out_{name}"] for name, _ in _OUTS)
```
